# Optimizing a Trainium2 kernel written in Bass

```python
import math
import jax, jax.numpy as jnp
from jax import lax
import numpy as np

D_MODEL = 1024
BATCH = 1
SEQ = 512
DEPTH = 2

BLOCK = 128
A_WIDTH = D_MODEL // 2
A_HEAD_DIM = 64
A_HEADS = A_WIDTH // A_HEAD_DIM
A_KV_HEADS = A_HEADS // 4
WINDOW = 128
B_WIDTH = D_MODEL - A_WIDTH
SSM_GROUP = 16
SSM_GROUPS = B_WIDTH // SSM_GROUP
SSM_STATE = 64
DT_MIN = 0.001
DT_MAX = 0.1
C_WIDTH = D_MODEL
C_HEADS = A_HEADS
C_HEAD_DIM = C_WIDTH // C_HEADS
C_KV_HEADS = C_HEADS // 4
IDX_HEADS = 8
IDX_DIM = 64
TOPK_MAX = 256
NUM_BUCKETS = 32
REL_MAX_DIST = 1024
EPS = 1e-6
NEG_INF = -1e30

EVEN_SPLITS = (A_WIDTH, A_KV_HEADS * A_HEAD_DIM, A_KV_HEADS * A_HEAD_DIM, A_WIDTH, B_WIDTH, B_WIDTH)
ODD_SPLITS = (C_WIDTH, C_KV_HEADS * C_HEAD_DIM, C_KV_HEADS * C_HEAD_DIM, C_WIDTH,
              IDX_HEADS * IDX_DIM, IDX_DIM, IDX_HEADS)
N_EVEN = (DEPTH + 1) // 2
N_ODD = DEPTH // 2


def rms_norm(x, g):
    xf = x.astype(jnp.float32)
    y = xf * lax.rsqrt(jnp.mean(xf * xf, axis=-1, keepdims=True) + EPS)
    return (y * g.astype(jnp.float32)).astype(x.dtype)

def split_cols(z, sizes):
    idx = np.cumsum(sizes)[:-1].tolist()
    return jnp.split(z, idx, axis=-1)

def t5_bucket(dist):
    n = jnp.maximum(dist, 0)
    max_exact = NUM_BUCKETS // 2
    nf = jnp.maximum(n, 1).astype(jnp.float32)
    large = max_exact + (jnp.log(nf / max_exact) / math.log(REL_MAX_DIST / max_exact)
                         * (NUM_BUCKETS - max_exact)).astype(jnp.int32)
    large = jnp.minimum(large, NUM_BUCKETS - 1)
    return jnp.where(n < max_exact, n, large)

def swa_sink_attention(q, k, v, sinks, rel_bias):
    bsz, L, H, Dh = q.shape
    hkv = k.shape[2]
    G = H // hkv
    nb = L // BLOCK
    qb = q.reshape(bsz, nb, BLOCK, hkv, G, Dh)
    kb = k.reshape(bsz, nb, BLOCK, hkv, Dh)
    vb = v.reshape(bsz, nb, BLOCK, hkv, Dh)
    k_band = jnp.concatenate([jnp.concatenate([jnp.zeros_like(kb[:, :1]), kb[:, :-1]], axis=1), kb], axis=2)
    v_band = jnp.concatenate([jnp.concatenate([jnp.zeros_like(vb[:, :1]), vb[:, :-1]], axis=1), vb], axis=2)
    logits = jnp.einsum('bnqhgd,bnkhd->bnhgqk', qb, k_band).astype(jnp.float32) * (Dh ** -0.5)
    i = jnp.arange(BLOCK, dtype=jnp.int32)[:, None]
    j = jnp.arange(2 * BLOCK, dtype=jnp.int32)[None, :]
    d = i + BLOCK - j
    in_window = (d >= 0) & (d < WINDOW)
    first = (jnp.arange(nb) == 0)[:, None, None] & (j < BLOCK)[None]
    mask = in_window[None] & ~first
    bias = rel_bias[t5_bucket(d)].astype(jnp.float32)
    bias = bias.transpose(2, 0, 1).reshape(hkv, G, BLOCK, 2 * BLOCK)
    logits = jnp.where(mask[None, :, None, None], logits + bias, NEG_INF)
    sink = jnp.broadcast_to(sinks.astype(jnp.float32).reshape(1, 1, hkv, G, 1, 1), logits.shape[:-1] + (1,))
    p = jax.nn.softmax(jnp.concatenate([logits, sink], axis=-1), axis=-1)[..., :-1]
    out = jnp.einsum('bnhgqk,bnkhd->bnqhgd', p.astype(v.dtype), v_band)
    return out.reshape(bsz, L, H * Dh)

def ssm_combine(e1, e2):
    a1r, a1i, b1r, b1i = e1
    a2r, a2i, b2r, b2i = e2
    ar = a1r * a2r - a1i * a2i
    ai = a1r * a2i + a1i * a2r
    br = a2r * b1r - a2i * b1i + b2r
    bi = a2r * b1i + a2i * b1r + b2i
    return (ar, ai, br, bi)

def s5_mixer(u, log_dt, a_re, a_im, b_re, b_im, c_re, c_im, d_skip, glu_w, glu_b):
    bsz, L, W = u.shape
    G, P = a_re.shape
    ug = u.reshape(bsz, L, G, W // G)
    dt = jnp.exp(log_dt)[:, None]
    mag = jnp.exp(a_re * dt)
    ang = a_im * dt
    ab_re = mag * jnp.cos(ang)
    ab_im = mag * jnp.sin(ang)
    den = a_re * a_re + a_im * a_im
    n_re = ab_re - 1.0
    n_im = ab_im
    f_re = (n_re * a_re + n_im * a_im) / den
    f_im = (n_im * a_re - n_re * a_im) / den
    bb_re = f_re[..., None] * b_re - f_im[..., None] * b_im
    bb_im = f_re[..., None] * b_im + f_im[..., None] * b_re
    bu_re = jnp.einsum('blgh,gph->blgp', ug, bb_re)
    bu_im = jnp.einsum('blgh,gph->blgp', ug, bb_im)
    at_re = jnp.broadcast_to(ab_re[None, None], (1, L, G, P))
    at_im = jnp.broadcast_to(ab_im[None, None], (1, L, G, P))
    _, _, x_re, x_im = lax.associative_scan(ssm_combine, (at_re, at_im, bu_re, bu_im), axis=1)
    y = (jnp.einsum('blgp,ghp->blgh', x_re, c_re) - jnp.einsum('blgp,ghp->blgh', x_im, c_im)
         + d_skip * ug)
    y = jax.nn.gelu(y.reshape(bsz, L, W))
    h = y @ glu_w + glu_b
    return h[..., :W] * jax.nn.sigmoid(h[..., W:])

def dsa_attention(q, k, v, qi, ki, wi, rel_bias):
    bsz, L, H, Dh = q.shape
    hkv = k.shape[2]
    G = H // hkv
    nb = L // BLOCK
    topk = min(TOPK_MAX, L // 4)
    qb = q.reshape(bsz, nb, BLOCK, hkv, G, Dh).transpose(1, 0, 2, 3, 4, 5)
    qib = qi.reshape(bsz, nb, BLOCK, IDX_HEADS, IDX_DIM).transpose(1, 0, 2, 3, 4)
    wib = wi.reshape(bsz, nb, BLOCK, IDX_HEADS).transpose(1, 0, 2, 3)
    starts = jnp.arange(nb, dtype=jnp.int32) * BLOCK
    key_pos = jnp.arange(L, dtype=jnp.int32)

    def one_block(args):
        q_blk, qi_blk, w_blk, start = args
        t = start + jnp.arange(BLOCK, dtype=jnp.int32)
        rel = jax.nn.relu(jnp.einsum('bqhd,bsd->bqhs', qi_blk, ki).astype(jnp.float32) * (IDX_DIM ** -0.5))
        score = jnp.einsum('bqhs,bqh->bqs', rel, w_blk.astype(jnp.float32))
        score = jnp.where(key_pos[None, None, :] <= t[None, :, None], score, NEG_INF)
        _, idx = lax.top_k(score, topk)
        valid = idx <= t[None, :, None]
        k_sel = jax.vmap(lambda kk, ii: kk[ii])(k, idx)
        v_sel = jax.vmap(lambda vv, ii: vv[ii])(v, idx)
        logits = jnp.einsum('bqhgd,bqkhd->bqhgk', q_blk, k_sel).astype(jnp.float32) * (Dh ** -0.5)
        bias = rel_bias[t5_bucket(t[None, :, None] - idx)].astype(jnp.float32)
        bias = bias.reshape(bsz, BLOCK, topk, hkv, G).transpose(0, 1, 3, 4, 2)
        logits = jnp.where(valid[:, :, None, None, :], logits + bias, NEG_INF)
        p = jax.nn.softmax(logits, axis=-1).astype(v.dtype)
        return jnp.einsum('bqhgk,bqkhd->bqhgd', p, v_sel)

    out = lax.map(one_block, (qb, qib, wib, starts))
    return out.transpose(1, 0, 2, 3, 4, 5).reshape(bsz, L, H * Dh)

def even_layer(hn, rel_bias, w_in, w_out, q_g, k_g, sinks, log_dt, a_re, a_im, b_re, b_im,
               c_re, c_im, d_skip, glu_w, glu_b):
    bsz, L, _ = hn.shape
    q, k, v, gate_a, u, gate_b = split_cols(hn @ w_in, EVEN_SPLITS)
    q = rms_norm(q.reshape(bsz, L, A_HEADS, A_HEAD_DIM), q_g)
    k = rms_norm(k.reshape(bsz, L, A_KV_HEADS, A_HEAD_DIM), k_g)
    v = v.reshape(bsz, L, A_KV_HEADS, A_HEAD_DIM)
    att = swa_sink_attention(q, k, v, sinks, rel_bias) * jax.nn.silu(gate_a)
    ssm = s5_mixer(u, log_dt, a_re, a_im, b_re, b_im, c_re, c_im, d_skip, glu_w, glu_b) * jax.nn.silu(gate_b)
    return jnp.concatenate([att, ssm], axis=-1) @ w_out

def odd_layer(hn, rel_bias, w_in, w_out, q_g, k_g):
    bsz, L, _ = hn.shape
    q, k, v, gate, qi, ki, wi = split_cols(hn @ w_in, ODD_SPLITS)
    q = rms_norm(q.reshape(bsz, L, C_HEADS, C_HEAD_DIM), q_g)
    k = rms_norm(k.reshape(bsz, L, C_KV_HEADS, C_HEAD_DIM), k_g)
    v = v.reshape(bsz, L, C_KV_HEADS, C_HEAD_DIM)
    qi = qi.reshape(bsz, L, IDX_HEADS, IDX_DIM)
    wi = wi * (IDX_HEADS ** -0.5)
    att = dsa_attention(q, k, v, qi, ki, wi, rel_bias)
    return (att * jax.nn.silu(gate)) @ w_out

def first_inputs(seed: int = 0) -> dict:
    key = jax.random.key(seed)
    ks = jax.random.split(key, 24)
    f32 = jnp.float32

    def nrm(k, shape, s):
        return jax.random.normal(k, shape, f32) * s

    ev_in = sum(EVEN_SPLITS)
    od_in = sum(ODD_SPLITS)
    ssm_n = jnp.arange(SSM_STATE, dtype=f32)
    return {
        'x': nrm(ks[0], (BATCH, SEQ, D_MODEL), 1.0),
        'rel_bias': nrm(ks[1], (NUM_BUCKETS, A_HEADS), 0.5),
        'norm_g': 1.0 + nrm(ks[2], (DEPTH, D_MODEL), 0.02),
        'ev_w_in': nrm(ks[3], (N_EVEN, D_MODEL, ev_in), D_MODEL ** -0.5),
        'ev_w_out': nrm(ks[4], (N_EVEN, A_WIDTH + B_WIDTH, D_MODEL), (A_WIDTH + B_WIDTH) ** -0.5),
        'ev_q_norm_g': 1.0 + nrm(ks[5], (N_EVEN, A_HEAD_DIM), 0.02),
        'ev_k_norm_g': 1.0 + nrm(ks[6], (N_EVEN, A_HEAD_DIM), 0.02),
        'ev_sinks': nrm(ks[7], (N_EVEN, A_HEADS), 1.0),
        'ev_ssm_log_dt': jax.random.uniform(ks[8], (N_EVEN, SSM_GROUPS), f32, math.log(DT_MIN), math.log(DT_MAX)),
        'ev_ssm_a_re': -0.5 + nrm(ks[9], (N_EVEN, SSM_GROUPS, SSM_STATE), 0.01),
        'ev_ssm_a_im': jnp.pi * ssm_n + nrm(ks[10], (N_EVEN, SSM_GROUPS, SSM_STATE), 0.01),
        'ev_ssm_b_re': nrm(ks[11], (N_EVEN, SSM_GROUPS, SSM_STATE, SSM_GROUP), (2 * SSM_GROUP) ** -0.5),
        'ev_ssm_b_im': nrm(ks[12], (N_EVEN, SSM_GROUPS, SSM_STATE, SSM_GROUP), (2 * SSM_GROUP) ** -0.5),
        'ev_ssm_c_re': nrm(ks[13], (N_EVEN, SSM_GROUPS, SSM_GROUP, SSM_STATE), (2 * SSM_STATE) ** -0.5),
        'ev_ssm_c_im': nrm(ks[14], (N_EVEN, SSM_GROUPS, SSM_GROUP, SSM_STATE), (2 * SSM_STATE) ** -0.5),
        'ev_ssm_d': nrm(ks[15], (N_EVEN, SSM_GROUPS, SSM_GROUP), 1.0),
        'ev_glu_w': nrm(ks[16], (N_EVEN, B_WIDTH, 2 * B_WIDTH), B_WIDTH ** -0.5),
        'ev_glu_b': nrm(ks[17], (N_EVEN, 2 * B_WIDTH), 0.01),
        'od_w_in': nrm(ks[18], (N_ODD, D_MODEL, od_in), D_MODEL ** -0.5),
        'od_w_out': nrm(ks[19], (N_ODD, C_WIDTH, D_MODEL), C_WIDTH ** -0.5),
        'od_q_norm_g': 1.0 + nrm(ks[20], (N_ODD, C_HEAD_DIM), 0.02),
        'od_k_norm_g': 1.0 + nrm(ks[21], (N_ODD, C_HEAD_DIM), 0.02),
    }

def first_block(x, rel_bias, norm_g, ev_w_in, ev_w_out, ev_q_norm_g, ev_k_norm_g, ev_sinks,
              ev_ssm_log_dt, ev_ssm_a_re, ev_ssm_a_im, ev_ssm_b_re, ev_ssm_b_im, ev_ssm_c_re,
              ev_ssm_c_im, ev_ssm_d, ev_glu_w, ev_glu_b, od_w_in, od_w_out, od_q_norm_g, od_k_norm_g):
    h = x
    for layer in range(DEPTH):
        hn = rms_norm(h, norm_g[layer])
        j = layer // 2
        if layer % 2 == 0:
            out = even_layer(hn, rel_bias, ev_w_in[j], ev_w_out[j], ev_q_norm_g[j], ev_k_norm_g[j],
                             ev_sinks[j], ev_ssm_log_dt[j], ev_ssm_a_re[j], ev_ssm_a_im[j],
                             ev_ssm_b_re[j], ev_ssm_b_im[j], ev_ssm_c_re[j], ev_ssm_c_im[j],
                             ev_ssm_d[j], ev_glu_w[j], ev_glu_b[j])
        else:
            out = odd_layer(hn, rel_bias, od_w_in[j], od_w_out[j], od_q_norm_g[j], od_k_norm_g[j])
        h = h + out
    return h


HEAD_DIM = 64
N_HEADS_TOTAL = D_MODEL // HEAD_DIM
N_MEM_HEADS = 4
N_MIX_HEADS = N_HEADS_TOTAL - N_MEM_HEADS
D_MIX = N_MIX_HEADS * HEAD_DIM
D_MEMQ = N_MEM_HEADS * HEAD_DIM
MEM_TOKENS = 256
D_FF = 2816
CONV_WIDTH = 3
ROPE_THETA = 10000.0
Q_BLOCK = 128
DILATED_BRANCHES = ((128, 1), (512, 4), (2048, 16))
N_MIXERS = 2
N_A_LAYERS = (DEPTH + 1) // 2
N_B_LAYERS = DEPTH // 2
FOX_IN = 3 * D_MIX + N_MIX_HEADS + D_MEMQ
DIL_IN = 3 * D_MIX + D_MEMQ
NORM_EPS = 1e-6
NEG = -1e30


def rmsnorm(x, g):
    xf = x.astype(jnp.float32)
    y = xf * lax.rsqrt(jnp.mean(xf * xf, axis=-1, keepdims=True) + NORM_EPS)
    return (y * g.astype(jnp.float32)).astype(x.dtype)

def split_heads(t, n_heads):
    b, s, _ = t.shape
    return t.reshape(b, s, n_heads, HEAD_DIM).transpose(0, 2, 1, 3)

def merge_heads(t):
    b, h, s, d = t.shape
    return t.transpose(0, 2, 1, 3).reshape(b, s, h * d)

def rope_tables(seq):
    inv = 1.0 / (ROPE_THETA ** (jnp.arange(0, HEAD_DIM, 2, dtype=jnp.float32) / HEAD_DIM))
    ang = jnp.arange(seq, dtype=jnp.float32)[:, None] * inv[None, :]
    return jnp.cos(ang), jnp.sin(ang)

def apply_rope(x, cos, sin):
    x1, x2 = jnp.split(x.astype(jnp.float32), 2, axis=-1)
    y = jnp.concatenate([x1 * cos - x2 * sin, x2 * cos + x1 * sin], axis=-1)
    return y.astype(x.dtype)

def fox_attention(q, k, v, log_f):
    b, h, s, dh = q.shape
    c = lax.cumsum(log_f, axis=2)
    nb = s // Q_BLOCK
    scale = dh ** -0.5
    qb = q.reshape(b, h, nb, Q_BLOCK, dh).transpose(2, 0, 1, 3, 4)
    cb = c.reshape(b, h, nb, Q_BLOCK).transpose(2, 0, 1, 3)
    starts = jnp.arange(nb, dtype=jnp.int32) * Q_BLOCK
    kpos = jnp.arange(s, dtype=jnp.int32)

    def one_block(args):
        qi, ci, st = args
        sc = jnp.einsum('bhqd,bhkd->bhqk', qi, k, preferred_element_type=jnp.float32) * scale
        sc = sc + ci[..., :, None] - c[..., None, :]
        qpos = st + jnp.arange(Q_BLOCK, dtype=jnp.int32)
        sc = jnp.where(kpos[None, :] <= qpos[:, None], sc, NEG)
        p = jax.nn.softmax(sc, axis=-1)
        return jnp.einsum('bhqk,bhkd->bhqd', p.astype(v.dtype), v)

    out = lax.map(one_block, (qb, cb, starts))
    return out.transpose(1, 2, 0, 3, 4).reshape(b, h, s, dh)

def dilated_branch(q, k, v, window, dilation):
    b, h, s, dh = q.shape
    L = window // dilation
    chunk = dilation * L
    sp = -(-s // chunk) * chunk
    n = sp // dilation
    nb = n // L
    scale = dh ** -0.5

    def strided(t):
        t = jnp.pad(t, ((0, 0), (0, 0), (0, sp - s), (0, 0)))
        t = t.reshape(b, h, n, dilation, dh).transpose(0, 1, 3, 2, 4)
        return t.reshape(b, h, dilation, nb, L, dh)

    def with_prev(t):
        prev = jnp.pad(t, ((0, 0), (0, 0), (0, 0), (1, 0), (0, 0), (0, 0)))[:, :, :, :-1]
        return jnp.concatenate([prev, t], axis=4)

    qs = strided(q)
    kb = with_prev(strided(k))
    vb = with_prev(strided(v))
    sc = jnp.einsum('bhrnqd,bhrnkd->bhrnqk', qs, kb, preferred_element_type=jnp.float32) * scale
    a = jnp.arange(L, dtype=jnp.int32)
    cidx = jnp.arange(2 * L, dtype=jnp.int32)
    blk = jnp.arange(nb, dtype=jnp.int32)
    dist = a[:, None] + L - cidx[None, :]
    valid = (dist >= 0) & (dist <= L)
    valid = valid[None] & ((blk[:, None, None] > 0) | (cidx[None, None, :] >= L))
    sc = jnp.where(valid, sc, NEG)
    m = jnp.max(sc, axis=-1, keepdims=True)
    e = jnp.exp(sc - m)
    den = jnp.sum(e, axis=-1, keepdims=True)
    o = jnp.einsum('bhrnqk,bhrnkd->bhrnqd', (e / den).astype(v.dtype), vb)
    lse = (m + jnp.log(den))[..., 0]
    o = o.reshape(b, h, dilation, n, dh).transpose(0, 1, 3, 2, 4).reshape(b, h, sp, dh)[:, :, :s]
    lse = lse.reshape(b, h, dilation, n).transpose(0, 1, 3, 2).reshape(b, h, sp)[:, :, :s]
    return o, lse

def dilated_attention(q, k, v):
    outs, lses = [], []
    for window, dilation in DILATED_BRANCHES:
        o, lse = dilated_branch(q, k, v, window, dilation)
        outs.append(o)
        lses.append(lse)
    wts = jax.nn.softmax(jnp.stack(lses, axis=0), axis=0)
    return jnp.einsum('gbhs,gbhsd->bhsd', wts.astype(v.dtype), jnp.stack(outs, axis=0))

def memory_attention(qm, mem_n, w_mem_kv):
    km, vm = jnp.split(mem_n @ w_mem_kv, 2, axis=-1)
    km = split_heads(km, N_MEM_HEADS)
    vm = split_heads(vm, N_MEM_HEADS)
    sc = jnp.einsum('bhqd,bhkd->bhqk', qm, km, preferred_element_type=jnp.float32) * (HEAD_DIM ** -0.5)
    p = jax.nn.softmax(sc, axis=-1)
    return jnp.einsum('bhqk,bhkd->bhqd', p.astype(vm.dtype), vm)

def conv_ffn(xn, w_up, conv_w, conv_b, w_down):
    u = xn @ w_up
    s = u.shape[1]
    up = jnp.pad(u, ((0, 0), (CONV_WIDTH - 1, 0), (0, 0)))
    c = conv_b
    for j in range(CONV_WIDTH):
        c = c + conv_w[j] * up[:, j:j + s]
    val, gate = jnp.split(c, 2, axis=-1)
    return (jax.nn.silu(gate) * val) @ w_down

def second_inputs(seed: int = 0) -> dict:
    key = jax.random.key(seed)
    ks = jax.random.split(key, 16)
    f32 = jnp.float32
    nrm = lambda k, shape, scale: jax.random.normal(k, shape, f32) * scale
    forget_bias_init = 3.0
    return {
        'x': nrm(ks[0], (BATCH, SEQ, D_MODEL), 1.0),
        'mem': nrm(ks[1], (BATCH, MEM_TOKENS, D_MODEL), 1.0),
        'norm_mix': 1.0 + nrm(ks[2], (DEPTH, D_MODEL), 0.1),
        'norm_mem': 1.0 + nrm(ks[3], (DEPTH, D_MODEL), 0.1),
        'norm_ffn': 1.0 + nrm(ks[4], (DEPTH, D_MODEL), 0.1),
        'w_in_fox': nrm(ks[5], (N_A_LAYERS, D_MODEL, FOX_IN), D_MODEL ** -0.5),
        'b_forget': forget_bias_init + nrm(ks[6], (N_A_LAYERS, N_MIX_HEADS), 0.5),
        'w_in_dil': nrm(ks[7], (N_B_LAYERS, D_MODEL, DIL_IN), D_MODEL ** -0.5),
        'w_mem_kv': nrm(ks[8], (DEPTH, D_MODEL, 2 * D_MEMQ), D_MODEL ** -0.5),
        'w_out': nrm(ks[9], (DEPTH, D_MODEL, D_MODEL), D_MODEL ** -0.5),
        'w_up': nrm(ks[10], (DEPTH, D_MODEL, 2 * D_FF), D_MODEL ** -0.5),
        'conv_w': nrm(ks[11], (DEPTH, CONV_WIDTH, 2 * D_FF), CONV_WIDTH ** -0.5),
        'conv_b': nrm(ks[12], (DEPTH, 2 * D_FF), 0.02),
        'w_down': nrm(ks[13], (DEPTH, D_FF, D_MODEL), D_FF ** -0.5),
        'norm_final': 1.0 + nrm(ks[14], (D_MODEL,), 0.1),
    }

def second_block(x, mem, norm_mix, norm_mem, norm_ffn, w_in_fox, b_forget, w_in_dil,
              w_mem_kv, w_out, w_up, conv_w, conv_b, w_down, norm_final):
    s = x.shape[1]
    cos, sin = rope_tables(s)
    h = x
    for layer in range(DEPTH):
        kind = layer % N_MIXERS
        slot = layer // N_MIXERS
        xn = rmsnorm(h, norm_mix[layer])
        mn = rmsnorm(mem, norm_mem[layer])
        if kind == 0:
            proj = xn @ w_in_fox[slot]
            q, k, v, f_logit, qm = jnp.split(
                proj, [D_MIX, 2 * D_MIX, 3 * D_MIX, 3 * D_MIX + N_MIX_HEADS], axis=-1)
            log_f = jax.nn.log_sigmoid(
                (f_logit + b_forget[slot]).astype(jnp.float32)).transpose(0, 2, 1)
            mix = fox_attention(split_heads(q, N_MIX_HEADS), split_heads(k, N_MIX_HEADS),
                                split_heads(v, N_MIX_HEADS), log_f)
        else:
            proj = xn @ w_in_dil[slot]
            q, k, v, qm = jnp.split(proj, [D_MIX, 2 * D_MIX, 3 * D_MIX], axis=-1)
            qh = apply_rope(split_heads(q, N_MIX_HEADS), cos, sin)
            kh = apply_rope(split_heads(k, N_MIX_HEADS), cos, sin)
            mix = dilated_attention(qh, kh, split_heads(v, N_MIX_HEADS))
        mem_out = memory_attention(split_heads(qm, N_MEM_HEADS), mn, w_mem_kv[layer])
        heads = jnp.concatenate([mix, mem_out], axis=1)
        h = h + merge_heads(heads) @ w_out[layer]
        h = h + conv_ffn(rmsnorm(h, norm_ffn[layer]), w_up[layer], conv_w[layer],
                         conv_b[layer], w_down[layer])
    return rmsnorm(h, norm_final)


def setup_inputs(seed=0):
    out = dict(first_inputs(seed))
    for name, value in second_inputs(seed + 1).items():
        if name != "x":
            out[name + "_2"] = value
    return out


def reference(
    x, rel_bias, norm_g, ev_w_in, ev_w_out, ev_q_norm_g, ev_k_norm_g, ev_sinks, ev_ssm_log_dt,
    ev_ssm_a_re, ev_ssm_a_im, ev_ssm_b_re, ev_ssm_b_im, ev_ssm_c_re, ev_ssm_c_im, ev_ssm_d,
    ev_glu_w, ev_glu_b, od_w_in, od_w_out, od_q_norm_g, od_k_norm_g, mem_2, norm_mix_2,
    norm_mem_2, norm_ffn_2, w_in_fox_2, b_forget_2, w_in_dil_2, w_mem_kv_2, w_out_2, w_up_2,
    conv_w_2, conv_b_2, w_down_2, norm_final_2,
):
    x = first_block(
        x, rel_bias, norm_g, ev_w_in, ev_w_out, ev_q_norm_g, ev_k_norm_g, ev_sinks,
        ev_ssm_log_dt, ev_ssm_a_re, ev_ssm_a_im, ev_ssm_b_re, ev_ssm_b_im, ev_ssm_c_re,
        ev_ssm_c_im, ev_ssm_d, ev_glu_w, ev_glu_b, od_w_in, od_w_out, od_q_norm_g, od_k_norm_g,
    )
    return second_block(
        x, mem_2, norm_mix_2, norm_mem_2, norm_ffn_2, w_in_fox_2, b_forget_2, w_in_dil_2,
        w_mem_kv_2, w_out_2, w_up_2, conv_w_2, conv_b_2, w_down_2, norm_final_2,
    )


_drawn_inputs = setup_inputs


def setup_inputs(seed=0):
    import zlib

    import numpy as np

    out = dict(_drawn_inputs(seed))
    spreads = {}
    factors = {'norm_g': 3.103,
     'ev_q_norm_g': 8.0,
     'ev_k_norm_g': 8.0,
     'ev_sinks': 4.864,
     'ev_ssm_log_dt': 3.827,
     'ev_ssm_a_re': 200.0,
     'ev_ssm_a_im': 3.757,
     'ev_ssm_b_re': 4.757,
     'ev_ssm_b_im': 4.728,
     'ev_ssm_c_re': 4.676,
     'ev_ssm_c_im': 4.864,
     'ev_glu_b': 8.0,
     'od_q_norm_g': 8.0,
     'od_k_norm_g': 8.0,
     'norm_mem_2': 4.65,
     'conv_b_2': 18.815,
     'norm_ffn_2': 3.645,
     'b_forget_2': 54.024}
    for name, (base, spread) in spreads.items():
        noise = np.random.default_rng([zlib.crc32(name.encode()), seed]).standard_normal(out[name].shape)
        drawn = base * np.exp(spread * noise) if base else spread * noise
        out[name] = __import__('jax').numpy.asarray(drawn.astype(out[name].dtype))
    for name, factor in factors.items():
        out[name] = (out[name] * factor).astype(out[name].dtype)
    return out
```

```python
import math
from contextlib import ExitStack

import numpy as np

import concourse.bass as bass
from concourse import mybir

F32 = mybir.dt.float32
F32R = mybir.dt.float32r
BF16 = mybir.dt.bfloat16
I32 = mybir.dt.int32
ALU = mybir.AluOpType
ACT = mybir.ActivationFunctionType

P = 128
S = 512
T = S // P
D = 1024
KD = D // P
EPS = 1e-6
NEG = -1e30
BIG = 3e38
MAGIC = 12582912.0

AH, AD, AKV = 8, 64, 2
CH, CD, CKV = 8, 128, 2
IH, ID = 8, 64
TOPK = 128
G, GH, GP = 32, 16, 64
ST = G * GP // P
FH, FD = 12, 64
MH, MT = 4, 256
DFF = 2816
FC = DFF // P
NB = 32
BX = 640

C_NORM_G, C_MIX, C_MEM, C_FFN, C_GLU, C_SKIP, C_EQ, C_EK, C_OQ, C_OK = 0, 16, 32, 48, 64, 72, 76, 77, 78, 79
C_ROWS = 80
C_CONV = C_ROWS
C_MAG = C_CONV + 2 * 176
C_TURN, C_FRE, C_FIM = C_MAG + ST, C_MAG + 2 * ST, C_MAG + 3 * ST
C_COLS = C_MAG + 4 * ST

RAW, SPLIT, SLOT = 2, 3, 2048


class Signal:

    def __init__(self, ctx, nc, name):
        self.s = ctx.enter_context(nc.semaphore(name))
        self.base = 0

    def at(self, n):
        return self.base + n

    def passed(self, n):
        self.base += n


class Weights:

    def __init__(self, ctx, nc):
        self.slots = []
        self.raw = ctx.enter_context(nc.sbuf_tensor("w_raw", [P, RAW, SLOT], F32))
        self.hi = ctx.enter_context(nc.sbuf_tensor("w_hi", [P, SPLIT, SLOT], F32R))
        self.lo = ctx.enter_context(nc.sbuf_tensor("w_lo", [P, SPLIT, SLOT], F32R))
        self.loaded = [ctx.enter_context(nc.semaphore(f"w_loaded{i}")) for i in range(RAW)]
        self.hi_done = ctx.enter_context(nc.semaphore("w_hi_done"))
        self.split_done = ctx.enter_context(nc.semaphore("w_split_done"))
        self.used = ctx.enter_context(nc.semaphore("w_used"))
        self.sent = 0
        self.cut = 0
        self.arrived = [0] * RAW
        self.need = []

    def add(self, kk, nn, pieces):
        self.slots.append((kk, nn, pieces))
        r = (len(self.slots) - 1) % RAW
        self.arrived[r] += 16 * len(pieces)
        self.need.append(self.arrived[r])

    def load(self, sp, until):
        for n in range(self.sent, min(len(self.slots), until + RAW + SPLIT)):
            kk, nn, pieces = self.slots[n]
            if n >= RAW:
                sp.wait_ge(self.split_done, n - RAW + 1)
            dst = self.raw[:, n % RAW, 0:kk * nn].rearrange("p (k n) -> p k n", k=kk)
            for c, src in pieces:
                sp.dma_start(dst[:, :, c:c + src.shape[2]], src).then_inc(self.loaded[n % RAW], 16)
            self.sent = n + 1

    def split(self, pool, until):
        for n in range(self.cut, min(len(self.slots), until + SPLIT)):
            kk, nn, _ = self.slots[n]
            size = kk * nn
            raw, hi, lo = self.raw[:, n % RAW, 0:size], self.hi[:, n % SPLIT, 0:size], self.lo[:, n % SPLIT, 0:size]
            pool.wait_ge(self.loaded[n % RAW], self.need[n])
            if n >= SPLIT:
                pool.wait_ge(self.used, n - SPLIT + 1)
            pool.tensor_scalar(hi, raw, 1.0, 1.0, ALU.mult, ALU.mult).then_inc(self.hi_done, 1)
            pool.wait_ge(self.hi_done, n + 1)
            pool.tensor_tensor(lo, raw, hi.bitcast(F32), ALU.subtract).then_inc(self.split_done, 1)
            self.cut = n + 1

    def parts(self, n):
        kk, nn, _ = self.slots[n]
        view = lambda t: t[:, n % SPLIT, 0:kk * nn].rearrange("p (k n) -> p k n", k=kk)
        return view(self.hi), view(self.lo)


def block_kernel(nc, t, out):
    ctx = ExitStack()
    with ctx:
        sb = lambda name, shape, dt=F32: ctx.enter_context(nc.sbuf_tensor(name, shape, dt))
        sig = lambda name: Signal(ctx, nc, name)
        W = Weights(ctx, nc)

        def tiles(w, k0, kk):
            return w[k0 * P:(k0 + kk) * P, :].rearrange("(k p) n -> p k n", p=P)

        def wide(w, c0, width, kd=KD):
            first = len(W.slots)
            for c in range(c0, c0 + width, 256):
                n = min(256, c0 + width - c)
                W.add(kd, n, [(0, tiles(w, 0, kd)[:, :, c:c + n])])
            return first

        def deep(w, k_first, k_tiles):
            first = len(W.slots)
            for half in range(2):
                for k in range(k_first, k_first + k_tiles, 4):
                    kk = min(4, k_first + k_tiles - k)
                    W.add(kk, 512, [(0, tiles(w, k, kk)[:, :, half * 512:half * 512 + 512])])
            return first

        ev, od, fox, dil = t["ev_w_in"][0], t["od_w_in"][0], t["w_in_fox_2"][0], t["w_in_dil_2"][0]
        AW, CW, FW = AH * AD, CH * CD, FH * FD
        w_ev_q = wide(ev, 0, AW)
        w_ev_k = len(W.slots)
        W.add(KD, 4 * AD, [(64 * i, tiles(ev, 0, KD)[:, :, AW + 64 * (i // 2):AW + 64 * (i // 2) + 64]) for i in range(4)])
        w_ev_v = wide(ev, AW + 128, 128)
        w_ev_rest = wide(ev, AW + 256, 3 * 512)
        w_glu = len(W.slots)
        for half in range(2):
            W.add(4, 512, [(0, tiles(t["ev_glu_w"][0], 0, 4)[:, :, half * 512:half * 512 + 512])])
        w_ev_out = deep(t["ev_w_out"][0], 0, KD)
        w_od_q = wide(od, 0, CW)
        w_od_k = wide(od, CW, 256)
        w_od_v = wide(od, CW + 256, 256)
        w_od_gate = wide(od, CW + 512, CW)
        w_od_qi = wide(od, 2 * CW + 512, IH * ID)
        w_od_ki = len(W.slots)
        ki0 = 2 * CW + 512 + IH * ID
        W.add(KD, 2 * ID, [(64 * i, tiles(od, 0, KD)[:, :, ki0:ki0 + 64]) for i in range(2)])
        w_od_wi = wide(od, ki0 + 64, IH)
        w_od_out = deep(t["od_w_out"][0], 0, KD)
        w_mem_k, w_mem_v, w_q, w_k, w_v, w_qm, w_out = ([0, 0] for _ in range(7))
        HALF = FC // 2
        w_up, w_down = {}, {}
        for layer in range(2):
            w_mem_k[layer] = wide(t["w_mem_kv_2"][layer], 0, 256)
            w_mem_v[layer] = wide(t["w_mem_kv_2"][layer], 256, 256)
            w_in = (fox, dil)[layer]
            w_q[layer] = wide(w_in, 0, FW)
            w_k[layer] = wide(w_in, FW, FW)
            w_v[layer] = wide(w_in, 2 * FW, FW)
            if layer == 0:
                w_forget = wide(w_in, 3 * FW, FH)
            w_qm[layer] = wide(w_in, 3 * FW + (FH if layer == 0 else 0), 256)
            w_out[layer] = deep(t["w_out_2"][layer], 0, KD)
            for part in range(2):
                first = len(W.slots)
                for i in range(part * HALF, (part + 1) * HALF):
                    up = tiles(t["w_up_2"][layer], 0, KD)
                    W.add(KD, 256, [(0, up[:, :, i * P:(i + 1) * P]), (P, up[:, :, DFF + i * P:DFF + (i + 1) * P])])
                w_up[layer, part] = first
                w_down[layer, part] = deep(t["w_down_2"][layer], part * HALF, HALF)

        h = sb("h", [P, T, D])
        x_hi = sb("x_hi", [P, KD, S], F32R)
        x_lo = sb("x_lo", [P, KD, S], F32R)
        col = sb("col", [P, C_COLS])
        ident = sb("ident", [P, P])
        ident_b = sb("ident_b", [P, P], BF16)
        causal = sb("causal", [P, S])
        head_sum = sb("head_sum", [P, 2, 40])
        sel64 = sb("sel64", [12, 6 * P])
        sel128 = sb("sel128", [12, 12 * P])
        eps_col = sb("eps_col", [P, 1])
        pih_col = sb("pih_col", [P, 1])
        neg_sink = sb("neg_sink", [P, AH])
        ssm_bt = sb("ssm_bt", [P, 2, 4, P])
        ssm_ct = sb("ssm_ct", [P, 3, 4, P])
        ps = ctx.enter_context(nc.psum_tensor("ps", [P, 8, 512], F32))
        bias_rows = nc.dram_tensor("bias_rows", [2, AH, P, BX], F32, kind="Internal")

        dve_link, act_link = sig("dve_link"), sig("act_link")
        names = ("mm_done", "bank_free", "loads_in", "a_ready", "b_ready", "c_ready", "d_ready", "e_ready",
                 "scores_done", "logits_ready", "probs_ready", "probs_scaled", "turned", "turned_copied",
                 "pv_done", "out_free", "bias_in", "bias_in2", "dt_in", "stored")
        sg = {n: sig(n) for n in names}
        mm_done, bank_free, loads_in = sg["mm_done"], sg["bank_free"], sg["loads_in"]
        bias_in = (sg["bias_in"], sg["bias_in2"])

        def linker(eng, link):
            def run(ins):
                link.passed(1)
                ins.then_inc(link.s, 1)
                eng.wait_ge(link.s, link.base)
            return run

        def stage():
            return nc.Block()

        def product(pe, o, w, x, start, stop, token_major):
            for i, (a, b) in enumerate(((w[0], x[0]), (w[0], x[1]), (w[1], x[0]))):
                l, r = (b, a) if token_major else (a, b)
                mm = pe.matmul(o, l, r, start=start and i == 0, stop=stop and i == 2)
            return mm

        with ExitStack() as c:
            st = lambda name, shape, dt=F32: c.enter_context(nc.sbuf_tensor(name, shape, dt))
            rows = st("rows", [C_ROWS, P])
            conv_rows = st("conv_rows", [88, 4, P])
            bucket = st("bucket", [NB, BX])
            rel = st("rel", [NB, AH])
            neg_rows = st("neg_rows", [AH, 2, BX])
            brow = st("brow", [AH, 2, BX])
            a_rows = st("a_rows", [16, 2, P])
            dtl = st("dtl", [16, 2])
            R = st("R", [16, 26, P])
            RI = st("RI", [16, P], I32)
            par = st("par", [16, 4, P])
            b_in = st("b_in", [P, 2, ST, GH])
            bb = st("bb", [P, 2, ST, GH])
            b_tmp = st("b_tmp", [P, ST, GH])
            b_pre = st("b_pre", [P, 2, 4, P])
            c_pre = st("c_pre", [P, 2, 4, P])
            sink_b = st("sink_b", [P, AH])
            b = c.enter_context(stage())
            zeroed, par_in, brow_ready, rows_stored = sg["a_ready"], sg["b_ready"], sg["c_ready"], sg["d_ready"]
            turned_in, par_done, dt_in, bb_ready = sg["turned"], sg["probs_ready"], sg["dt_in"], sg["e_ready"]
            n_loads = []

            @b.sync
            def _(sp):
                sp.dma_start(h[:, :, :], t["x"][0].rearrange("(t p) d -> p t d", p=P)).then_inc(loads_in.s, 16)
                W.load(sp, -SPLIT)
                sp.wait_ge(brow_ready.s, brow_ready.at(1))
                for a in range(2):
                    sp.dma_start(bias_rows[a, :, :, :], brow[:, a, :].unsqueeze(1).to_broadcast([AH, P, BX])).then_inc(rows_stored.s, 16)
                sp.wait_ge(rows_stored.s, rows_stored.at(32))
                sp.wait_ge(loads_in.s, loads_in.at(16))

            @b.gpsimd
            def _(pool):
                pool.memset(c_pre[:, :, :, :], 0.0).then_inc(zeroed.s, 1)

            @b.scalar
            def _(act):
                def load(dst, src):
                    act.dma_start(dst, src).then_inc(par_in.s, 16)
                    n_loads.append(1)
                for l in range(2):
                    for name, c0 in (("norm_g", C_NORM_G), ("norm_mix_2", C_MIX), ("norm_mem_2", C_MEM), ("norm_ffn_2", C_FFN)):
                        load(rows[c0 + 8 * l:c0 + 8 * l + 8, :], t[name][l].rearrange("(k p) -> k p", p=P))
                    for j in range(2):
                        load(conv_rows[44 * j:44 * j + 44, 2 * l, :], t["conv_w_2"][l, j].rearrange("(k p) -> k p", p=P))
                    load(conv_rows[0:44, 2 * l + 1, :], t["conv_w_2"][l, 2].rearrange("(k p) -> k p", p=P))
                    load(conv_rows[44:88, 2 * l + 1, :], t["conv_b_2"][l].rearrange("(k p) -> k p", p=P))
                load(rows[C_GLU:C_GLU + 8, :], t["ev_glu_b"][0].rearrange("(k p) -> k p", p=P))
                load(rows[C_SKIP:C_SKIP + 4, :], t["ev_ssm_d"][0].rearrange("(k g) h -> k (g h)", k=4))
                for c0, name in ((C_EQ, "ev_q_norm_g"), (C_EK, "ev_k_norm_g")):
                    for i in range(2):
                        load(rows[c0:c0 + 1, 64 * i:64 * i + 64], t[name])
                load(rows[C_OQ:C_OQ + 1, :], t["od_q_norm_g"])
                load(rows[C_OK:C_OK + 1, :], t["od_k_norm_g"])
                load(dtl[:, :], t["ev_ssm_log_dt"][0].rearrange("(j g) -> j g", g=2))
                load(a_rows[:, 0, :], t["ev_ssm_a_re"][0].rearrange("(j g) p -> j (g p)", g=2))
                load(a_rows[:, 1, :], t["ev_ssm_a_im"][0].rearrange("(j g) p -> j (g p)", g=2))
                load(b_in[:, 0, :, :], t["ev_ssm_b_re"][0].rearrange("(j g) p h -> (g p) j h", g=2))
                load(b_in[:, 1, :, :], t["ev_ssm_b_im"][0].rearrange("(j g) p h -> (g p) j h", g=2))
                load(rel[:, :], t["rel_bias"])
                load(bucket[:, :], t["c_bucket"])
                load(neg_rows[:, :, :], t["c_neg_rows"])
                load(ident[:, :], t["c_ident"])
                load(causal[:, :], t["c_causal"])
                load(head_sum[:, :, :], t["c_head_sum"])
                load(sel64[:, :], t["c_sel64"])
                load(sel128[:, :], t["c_sel128"])
                load(sink_b[:, :], t["ev_sinks"].to_broadcast([P, AH]))
                act.wait_ge(zeroed.s, zeroed.at(1))
                for part, name in enumerate(("ev_ssm_c_re", "ev_ssm_c_im")):
                    for g in range(8):
                        src = t[name][0].rearrange("(c g) h p -> g h c p", g=8)[g]
                        load(c_pre[16 * g:16 * g + 16, part, :, 64 * (g % 2):64 * (g % 2) + 64], src)
                act.wait_ge(dt_in.s, dt_in.at(1))
                act.activation(R[:, 12, :], R[:, 11, :], ACT.Sin, scale=6.283185).then_inc(dt_in.s, 1)
                act.activation(R[:, 13, :], R[:, 11, :], ACT.Sin, scale=3.1415925).then_inc(dt_in.s, 1)
                act.wait_ge(turned_in.s, turned_in.at(1))
                act.activation(col[:, 0:C_ROWS], ps[:, 0, 0:C_ROWS], ACT.Copy).then_inc(par_done.s, 1)
                act.activation(col[:, C_CONV:C_CONV + 352], ps[:, 1, 0:352], ACT.Copy).then_inc(par_done.s, 1)
                act.wait_ge(turned_in.s, turned_in.at(4))
                for i, (part, sign) in enumerate(((0, 1.0), (0, -1.0), (1, -1.0))):
                    act.activation(ssm_ct[:, i, :, :], ps[:, 4 + part, :].rearrange("p (c n) -> p c n", c=4),
                                   ACT.Copy, scale=sign).then_inc(par_done.s, 1)
                act.wait_ge(turned_in.s, turned_in.at(5))
                for part in range(2):
                    act.activation(ssm_bt[:, part, :, :], ps[:, 6 + part, :].rearrange("p (c n) -> p c n", c=4),
                                   ACT.Copy).then_inc(par_done.s, 1)

            @b.tensor
            def _(pe):
                pe.wait_ge(par_in.s, par_in.at(16 * len(n_loads)))
                pe.transpose(ps[:, 0, 0:C_ROWS], rows[:, :], ident[0:C_ROWS, 0:C_ROWS])
                for i in range(4):
                    mm = pe.transpose(ps[:, 1, 88 * i:88 * i + 88], conv_rows[:, i, :], ident[0:88, 0:88])
                mm.then_inc(turned_in.s, 1)
                pe.matmul(ps[0:AH, 2, :], rel[:, :], bucket[:, 0:512], start=True, stop=True)
                pe.matmul(ps[0:AH, 3, 0:BX - 512], rel[:, :], bucket[:, 512:BX], start=True, stop=True).then_inc(turned_in.s, 1)
                pe.wait_ge(par_done.s, par_done.at(2))
                pe.wait_ge(brow_ready.s, brow_ready.at(2))
                for i in range(4):
                    mm = pe.transpose(ps[:, 1, 16 * i:16 * i + 16], par[:, i, :], ident[0:16, 0:16])
                mm.then_inc(turned_in.s, 1)
                for part in range(2):
                    for k in range(4):
                        mm = pe.transpose(ps[:, 4 + part, k * P:(k + 1) * P], c_pre[:, part, k, :], ident[:, :])
                mm.then_inc(turned_in.s, 1)
                pe.wait_ge(bb_ready.s, bb_ready.at(1))
                for part in range(2):
                    for k in range(4):
                        mm = pe.transpose(ps[:, 6 + part, k * P:(k + 1) * P], b_pre[:, part, k, :], ident[:, :])
                mm.then_inc(turned_in.s, 1)

            @b.vector
            def _(dve):
                link = linker(dve, dve_link)
                dve.memset(eps_col[:, :], EPS)
                dve.memset(pih_col[:, :], math.pi / 2)
                link(dve.memset(b_pre[:, :, :, :], 0.0))
                dve.wait_ge(par_in.s, par_in.at(16 * len(n_loads)))
                dve.tensor_copy(ident_b[:, :], ident[:, :])
                link(dve.tensor_scalar(neg_sink[:, :], sink_b[:, :], -1.0, None, ALU.mult))
                dve.wait_ge(turned_in.s, turned_in.at(2))
                for a, root in enumerate((CD ** 0.5, AD ** 0.5)):
                    dve.scalar_tensor_tensor(brow[:, a, 0:512], ps[0:AH, 2, :], root, neg_rows[:, a, 0:512], ALU.mult, ALU.add)
                    ins = dve.scalar_tensor_tensor(brow[:, a, 512:BX], ps[0:AH, 3, 0:BX - 512], root, neg_rows[:, a, 512:BX],
                                                   ALU.mult, ALU.add)
                ins.then_inc(brow_ready.s, 1)
                dve.wait_ge(brow_ready.s, brow_ready.at(1))

                tt = lambda o, a, x, op: link(dve.tensor_tensor(o, a, x, op))
                ts = lambda o, a, s1, s2, op0, op1: link(dve.tensor_scalar(o, a, s1, s2, op0, op1))
                r = lambda i: R[:, i, :]

                def exp_parts(z, power, frac, tmp):
                    ts(tmp, z, -87.0, 88.0, ALU.max, ALU.min)
                    ts(power, tmp, 1.0 / math.log(2), MAGIC, ALU.mult, ALU.add)
                    ts(power, power, -MAGIC, None, ALU.add, ALU.bypass)
                    link(dve.scalar_tensor_tensor(tmp, power, -0.693359375, tmp, ALU.mult, ALU.add))
                    link(dve.scalar_tensor_tensor(tmp, power, 2.12194440e-4, tmp, ALU.mult, ALU.add))
                    ts(frac, tmp, 1.0 / 9, 1.0, ALU.mult, ALU.add)
                    for k in range(8, 1, -1):
                        tt(frac, frac, tmp, ALU.mult)
                        ts(frac, frac, 1.0 / k, 1.0, ALU.mult, ALU.add)
                    tt(frac, frac, tmp, ALU.mult)
                    ts(RI[:, :], power, 127.0, None, ALU.add, ALU.bypass)
                    ts(RI[:, :], RI[:, :], 23, None, ALU.logical_shift_left, ALU.bypass)
                    link(dve.tensor_copy(power, RI[:, :].bitcast(F32)))

                a_re, a_im = a_rows[:, 0, :], a_rows[:, 1, :]
                link(dve.tensor_copy(r(0).rearrange("j (g p) -> j g p", g=2), dtl[:, :].unsqueeze(2).to_broadcast([16, 2, 64])))
                exp_parts(r(0), r(1), r(2), r(3))
                tt(r(4), r(1), r(2), ALU.mult)
                tt(r(4), r(4), r(1), ALU.add)
                tt(r(5), a_re, r(4), ALU.mult)
                exp_parts(r(5), r(6), r(7), r(3))
                tt(r(8), r(6), r(7), ALU.mult)
                tt(par[:, 0, :], r(8), r(6), ALU.add)
                ts(r(9), r(6), -1.0, None, ALU.add, ALU.bypass)
                tt(r(9), r(9), r(8), ALU.add)
                tt(r(10), a_im, r(4), ALU.mult)
                ts(r(10), r(10), 1.0 / (2 * math.pi), None, ALU.mult, ALU.bypass)
                ts(r(11), r(10), MAGIC, -MAGIC, ALU.add, ALU.add)
                tt(par[:, 1, :], r(10), r(11), ALU.subtract)
                dve.tensor_copy(r(11), par[:, 1, :]).then_inc(dt_in.s, 1)
                dve.wait_ge(dt_in.s, dt_in.at(3))
                tt(r(14), r(13), r(13), ALU.mult)
                ts(r(14), r(14), -2.0, None, ALU.mult, ALU.bypass)
                tt(r(15), r(9), r(14), ALU.mult)
                tt(r(15), r(15), r(9), ALU.add)
                tt(r(15), r(15), r(14), ALU.add)
                tt(r(16), par[:, 0, :], r(12), ALU.mult)
                tt(r(17), a_re, a_re, ALU.mult)
                tt(r(18), a_im, a_im, ALU.mult)
                tt(r(17), r(17), r(18), ALU.add)
                link(dve.reciprocal(r(17), r(17)))
                tt(r(19), r(15), a_re, ALU.mult)
                tt(r(20), r(16), a_im, ALU.mult)
                tt(r(19), r(19), r(20), ALU.add)
                tt(par[:, 2, :], r(19), r(17), ALU.mult)
                tt(r(21), r(16), a_re, ALU.mult)
                tt(r(22), r(15), a_im, ALU.mult)
                tt(r(21), r(21), r(22), ALU.subtract)
                dve.tensor_tensor(par[:, 3, :], r(21), r(17), ALU.mult).then_inc(brow_ready.s, 1)
                dve.wait_ge(turned_in.s, turned_in.at(3))
                link(dve.tensor_copy(col[:, C_MAG:C_COLS], ps[:, 1, 0:4 * ST]))
                fre = col[:, C_FRE:C_FRE + ST].unsqueeze(2).to_broadcast([P, ST, GH])
                fim = col[:, C_FIM:C_FIM + ST].unsqueeze(2).to_broadcast([P, ST, GH])
                b_re, b_im = b_in[:, 0, :, :], b_in[:, 1, :, :]
                tt(bb[:, 0, :, :], fre, b_re, ALU.mult)
                tt(b_tmp[:, :, :], fim, b_im, ALU.mult)
                tt(bb[:, 0, :, :], bb[:, 0, :, :], b_tmp[:, :, :], ALU.subtract)
                tt(bb[:, 1, :, :], fre, b_im, ALU.mult)
                tt(b_tmp[:, :, :], fim, b_re, ALU.mult)
                tt(bb[:, 1, :, :], bb[:, 1, :, :], b_tmp[:, :, :], ALU.add)
                for part in range(2):
                    for g in range(2):
                        for j in range(4):
                            ins = dve.tensor_copy(b_pre[64 * g:64 * g + 64, part, :, 32 * j + 16 * g:32 * j + 16 * g + 16],
                                                  bb[64 * g:64 * g + 64, part, j::4, :])
                            if (part, g, j) != (1, 1, 3):
                                link(ins)
                ins.then_inc(bb_ready.s, 1)

        for s_, n in ((zeroed, 1), (par_in, 16 * len(n_loads)), (brow_ready, 2), (rows_stored, 32), (turned_in, 5),
                      (par_done, 7), (dt_in, 3), (bb_ready, 1), (loads_in, 16)):
            s_.passed(n)

        def normalize(src, n_tiles, gain, hi, lo):
            with ExitStack() as c:
                st = lambda name, shape, dt=F32: c.enter_context(nc.sbuf_tensor(nc.get_next_instruction_name() + name, shape, dt))
                normed = st("normed", [P, n_tiles, D])
                junk = st("junk", [P, D])
                stat = st("stat", [P, 3 * T])
                b = c.enter_context(stage())
                root_ready, normed_ready, hi_ready = sg["a_ready"], sg["b_ready"], sg["c_ready"]
                n = n_tiles * P

                @b.sync
                def _(sp):
                    W.load(sp, W.at_use - 1)

                @b.gpsimd
                def _(pool):
                    W.split(pool, W.at_use)

                @b.scalar
                def _(act):
                    link = linker(act, act_link)
                    for i in range(n_tiles):
                        link(act.activation(junk[:, :], src[:, i, :], ACT.Square, accum_out=stat[:, i:i + 1]))
                    act.activation(stat[:, T:T + n_tiles], stat[:, 0:n_tiles], ACT.Sqrt, scale=1.0 / D,
                                   bias=eps_col[:, 0:1]).then_inc(root_ready.s, 1)
                    for k in range(KD):
                        act.wait_ge(mm_done.s, mm_done.at(k + 1))
                        act.activation(hi[:, k, 0:n], ps[:, k, 0:n], ACT.Copy, scale=col[:, gain + k:gain + k + 1]).then_inc(hi_ready.s, 1)

                @b.vector
                def _(dve):
                    link = linker(dve, dve_link)
                    dve.wait_ge(root_ready.s, root_ready.at(1))
                    link(dve.reciprocal(stat[:, 2 * T:2 * T + n_tiles], stat[:, T:T + n_tiles]))
                    for i in range(n_tiles):
                        dve.tensor_scalar(normed[:, i, :], src[:, i, :], stat[:, 2 * T + i:2 * T + i + 1], None,
                                          ALU.mult).then_inc(normed_ready.s, 1)
                    for k in range(KD):
                        dve.wait_ge(hi_ready.s, hi_ready.at(k + 1))
                        dve.scalar_tensor_tensor(lo[:, k, 0:n], ps[:, k, 0:n], col[:, gain + k:gain + k + 1],
                                                 hi[:, k, 0:n].bitcast(F32), ALU.mult, ALU.subtract)

                @b.tensor
                def _(pe):
                    pe.wait_ge(normed_ready.s, normed_ready.at(n_tiles))
                    for k in range(KD):
                        for i in range(n_tiles):
                            mm = pe.transpose(ps[:, k, i * P:(i + 1) * P], normed[:, i, k * P:(k + 1) * P], ident[:, :])
                        mm.then_inc(mm_done.s, 1)

            for s_, k in ((root_ready, 1), (normed_ready, n_tiles), (hi_ready, KD), (mm_done, KD)):
                s_.passed(k)

        W.at_use = 0

        def project(jobs, xs, n, extra=None):
            NBANK = 8
            plan = []
            for first, width, kind, evacuate in jobs:
                for i, c0 in enumerate(range(0, width, 256)):
                    cols = min(256, width - c0)
                    if kind == "turned":
                        for j in range(cols // P):
                            plan.append((first + i, j, kind, None, evacuate, 2 * i + j, cols))
                    else:
                        for tt_ in range(n // P):
                            plan.append((first + i, 0, kind, tt_, evacuate, i, cols))
            last = max(p[0] for p in plan)
            ends = [m == len(plan) - 1 or plan[m + 1][0] != plan[m][0] for m in range(len(plan))]
            told = [m + 1 - sum(ends[:m + 1]) for m in range(len(plan))]
            with ExitStack() as c:
                b = c.enter_context(stage())

                @b.sync
                def _(sp):
                    W.load(sp, last)

                @b.gpsimd
                def _(pool):
                    W.split(pool, last + 1)

                @b.tensor
                def _(pe):
                    for m, (slot, j, kind, tile, _, _, cols) in enumerate(plan):
                        if m == 0 or plan[m - 1][0] != slot:
                            pe.wait_ge(W.split_done, slot + 1)
                        if m >= NBANK:
                            pe.wait_ge(bank_free.s, bank_free.at(m - NBANK + 1))
                        hi, lo = W.parts(slot)
                        for k in range(KD):
                            if kind == "turned":
                                w = [v[:, k, j * P:(j + 1) * P] for v in (hi, lo)]
                                mm = product(pe, ps[:, m % NBANK, 0:n], w, [v[:, k, 0:n] for v in xs], k == 0, k == KD - 1, False)
                            else:
                                w = [v[:, k, 0:cols] for v in (hi, lo)]
                                x = [v[:, k, tile * P:(tile + 1) * P] for v in xs]
                                mm = product(pe, ps[:, m % NBANK, 0:cols], w, x, k == 0, k == KD - 1, True)
                        mm.then_inc(W.used if ends[m] else mm_done.s, 1)

                @b.scalar
                def _(act):
                    for m, (slot, j, kind, tile, evacuate, i, cols) in enumerate(plan):
                        if ends[m]:
                            act.wait_ge(W.used, slot + 1)
                        else:
                            act.wait_ge(mm_done.s, mm_done.at(told[m]))
                        if kind == "turned":
                            evacuate(act, i, ps[:, m % NBANK, 0:n]).then_inc(bank_free.s, 1)
                        else:
                            evacuate(act, tile, i, ps[:, m % NBANK, 0:cols]).then_inc(bank_free.s, 1)

            mm_done.passed(told[-1])
            bank_free.passed(len(plan))
            W.at_use = last + 1

        def head_norm(parts_, d_head, sel):
            per = P // d_head
            n_rows = per * len(parts_)
            which = 0 if d_head == 64 else 1
            with ExitStack() as c:
                st = lambda name, shape, dt=F32: c.enter_context(nc.sbuf_tensor(nc.get_next_instruction_name() + name, shape, dt))
                sq = st("sq", [P, 2, S])
                inv = st("inv", [12, S])
                b = c.enter_context(stage())
                squared, summed, root_ready, inv_ready = sg["a_ready"], sg["b_ready"], sg["c_ready"], sg["d_ready"]

                @b.sync
                def _(sp):
                    W.load(sp, W.at_use - 1)

                @b.gpsimd
                def _(pool):
                    W.split(pool, W.at_use)

                @b.scalar
                def _(act):
                    for i, (x, _) in enumerate(parts_):
                        if i >= 2:
                            act.wait_ge(summed.s, summed.at(i - 1))
                        act.activation(sq[:, i % 2, :], x, ACT.Square).then_inc(squared.s, 1)
                    act.wait_ge(summed.s, summed.at(len(parts_)))
                    act.activation(inv[0:n_rows, :], ps[0:n_rows, 0, :], ACT.Sqrt, bias=eps_col[0:n_rows, 0:1]).then_inc(root_ready.s, 1)

                @b.tensor
                def _(pe):
                    for i in range(len(parts_)):
                        pe.wait_ge(squared.s, squared.at(i + 1))
                        c0 = 20 - per * i
                        pe.matmul(ps[0:n_rows, 0, :], head_sum[:, which, c0:c0 + n_rows], sq[:, i % 2, :],
                                  start=i == 0, stop=i == len(parts_) - 1).then_inc(summed.s, 1)
                    pe.wait_ge(inv_ready.s, inv_ready.at(1))
                    for i in range(len(parts_)):
                        if i >= 6:
                            pe.wait_ge(bank_free.s, bank_free.at(i - 5))
                        pe.matmul(ps[:, 1 + i % 6, :], sel[0:n_rows, i * P:(i + 1) * P], inv[0:n_rows, :],
                                  start=True, stop=True).then_inc(mm_done.s, 1)

                @b.vector
                def _(dve):
                    dve.wait_ge(root_ready.s, root_ready.at(1))
                    dve.reciprocal(inv[0:n_rows, :], inv[0:n_rows, :]).then_inc(inv_ready.s, 1)
                    for i, (x, gain) in enumerate(parts_):
                        dve.wait_ge(mm_done.s, mm_done.at(i + 1))
                        dve.scalar_tensor_tensor(x, x, col[:, gain:gain + 1], ps[:, 1 + i % 6, :],
                                                 ALU.mult, ALU.mult).then_inc(bank_free.s, 1)

            k = len(parts_)
            for s_, n in ((squared, k), (summed, k), (root_ready, 1), (inv_ready, 1), (mm_done, k), (bank_free, k)):
                s_.passed(n)

        def attention(heads, keys, scale, finish, sinks=None, bias_of=None, add=None, adds=lambda qb: True,
                      n_pair=2, bias_load=None):
            nh = len(heads)
            units = [(hd, qb) for hd in range(nh) for qb in range(T)]
            with ExitStack() as c:
                st = lambda name, shape, dt=F32: c.enter_context(nc.sbuf_tensor(nc.get_next_instruction_name() + name, shape, dt))
                L = st("L", [P, 3, S])
                PT = st("PT", [P, 2, T, S])
                stat = st("stat", [P, 3, 4])
                b = c.enter_context(stage())
                scores_done, logits_ready, probs_ready, probs_scaled = (sg[x] for x in ("scores_done", "logits_ready", "probs_ready", "probs_scaled"))
                turned, turned_copied, pv_done, out_free = (sg[x] for x in ("turned", "turned_copied", "pv_done", "out_free"))

                @b.sync
                def _(sp):
                    W.load(sp, W.at_use - 1)
                    if bias_load:
                        for hd in range(nh):
                            if hd >= 2:
                                sp.wait_ge(logits_ready.s, logits_ready.at(T * (hd - 1)))
                            bias_load(sp, hd)

                @b.gpsimd
                def _(pool):
                    W.split(pool, W.at_use)

                def width(qb):
                    k0, k1 = keys(qb)
                    return (k1 - k0) * P

                @b.tensor
                def _(pe):
                    def scores(u):
                        hd, qb = units[u]
                        q, k, _ = heads[hd]
                        k0, k1 = keys(qb)
                        if u >= 2:
                            pe.wait_ge(logits_ready.s, logits_ready.at(u - 1))
                        o = ps[:, u % 2, 0:width(qb)]
                        more = add is not None and adds(qb)
                        mm = pe.matmul(o, q[:, qb * P:(qb + 1) * P], k[:, k0 * P:k1 * P], start=True, stop=not more)
                        if more:
                            mm = add(pe, hd, qb, o)
                        mm.then_inc(scores_done.s, 1)

                    def turn(u):
                        hd, qb = units[u]
                        pe.wait_ge(probs_scaled.s, probs_scaled.at(u + 1))
                        if u >= 2:
                            pe.wait_ge(turned_copied.s, turned_copied.at(u - 1))
                        k0, k1 = keys(qb)
                        for i in range(k1 - k0):
                            mm = pe.transpose(ps[:, 2 + u % 2, i * P:(i + 1) * P], L[:, u % 3, i * P:(i + 1) * P], ident[:, :])
                        mm.then_inc(turned.s, 1)

                    def values(hd):
                        pe.wait_ge(turned_copied.s, turned_copied.at(T * (hd + 1)))
                        pair = hd // n_pair
                        if pair >= 2 and hd % n_pair == 0:
                            pe.wait_ge(out_free.s, out_free.at(pair - 1))
                        _, _, v = heads[hd]
                        d = v(0).shape[1]
                        p0 = d * (hd % n_pair)
                        kt = max(keys(qb)[1] for qb in range(T))
                        for kb in range(kt):
                            qs = [qb for qb in range(T) if keys(qb)[0] <= kb < keys(qb)[1]]
                            a, z = qs[0] * P, (qs[-1] + 1) * P
                            mm = pe.matmul(ps[p0:p0 + d, 4 + pair % 2, a:z], v(kb), PT[:, hd % 2, kb, a:z],
                                           start=kb == 0, stop=kb == kt - 1, skip_group_check=True)
                        mm.then_inc(pv_done.s, 1)

                    scores(0)
                    for u in range(len(units)):
                        if u + 1 < len(units):
                            scores(u + 1)
                        turn(u)
                        if u % T == 0 and u > 0:
                            values(u // T - 1)
                    values(nh - 1)

                @b.vector
                def _(dve):
                    link = linker(dve, dve_link)

                    def logits(u):
                        hd, qb = units[u]
                        if u >= 3:
                            dve.wait_ge(turned.s, turned.at(u - 2))
                        dve.wait_ge(scores_done.s, scores_done.at(u + 1))
                        if bias_load and qb == 0:
                            arrived = bias_in[hd % 2]
                            dve.wait_ge(arrived.s, arrived.at(16 * (hd // 2 + 1)))
                        w = width(qb)
                        init = BIG if sinks is None else sinks[:, hd:hd + 1]
                        dve.tensor_tensor_reduce(out=L[:, u % 3, 0:w], in0=ps[:, u % 2, 0:w], in1=bias_of(hd, qb, w), scale=-scale,
                                                 scalar=init, op0=ALU.add, op1=ALU.min,
                                                 accum_out=stat[:, u % 3, 0:1]).then_inc(logits_ready.s, 1)

                    def scaled(u):
                        hd, qb = units[u]
                        dve.wait_ge(probs_ready.s, probs_ready.at(u + 1))
                        if sinks is not None:
                            link(dve.tensor_tensor(stat[:, u % 3, 1:2], stat[:, u % 3, 1:2], stat[:, u % 3, 3:4], ALU.add))
                        link(dve.reciprocal(stat[:, u % 3, 2:3], stat[:, u % 3, 1:2]))
                        w = width(qb)
                        dve.tensor_scalar(L[:, u % 3, 0:w], L[:, u % 3, 0:w], stat[:, u % 3, 2:3], None,
                                          ALU.mult).then_inc(probs_scaled.s, 1)

                    logits(0)
                    for u in range(len(units)):
                        if u + 1 < len(units):
                            logits(u + 1)
                        scaled(u)
                        if u % T == 2 and u > T and (u // T) % n_pair == 0:
                            finish(dve, u // T // n_pair - 1, link)
                    finish(dve, nh // n_pair - 1, link)

                @b.scalar
                def _(act):
                    def probs(u):
                        hd, qb = units[u]
                        act.wait_ge(logits_ready.s, logits_ready.at(u + 1))
                        w = width(qb)
                        if sinks is not None:
                            act.activation(stat[:, u % 3, 3:4], sinks[:, hd:hd + 1], ACT.Exp, scale=-1.0,
                                           bias=stat[:, u % 3, 0:1])
                        act.activation(L[:, u % 3, 0:w], L[:, u % 3, 0:w], ACT.Exp, scale=-1.0, bias=stat[:, u % 3, 0:1],
                                       accum_out=stat[:, u % 3, 1:2]).then_inc(probs_ready.s, 1)

                    def copy(u):
                        hd, qb = units[u]
                        if hd >= 2 and qb == 0:
                            act.wait_ge(pv_done.s, pv_done.at(hd - 1))
                        act.wait_ge(turned.s, turned.at(u + 1))
                        k0, k1 = keys(qb)
                        act.activation(PT[:, hd % 2, k0:k1, qb * P:(qb + 1) * P],
                                       ps[:, 2 + u % 2, 0:(k1 - k0) * P].rearrange("p (k q) -> p k q", q=P),
                                       ACT.Copy).then_inc(turned_copied.s, 1)

                    probs(0)
                    for u in range(len(units)):
                        if u + 1 < len(units):
                            probs(u + 1)
                        copy(u)

            n = len(units)
            for s_, k in ((scores_done, n), (logits_ready, n), (probs_ready, n), (probs_scaled, n), (turned, n),
                          (turned_copied, n), (pv_done, nh), (out_free, nh // n_pair)):
                s_.passed(k)
            if bias_load:
                for s_ in bias_in:
                    s_.passed(16 * (nh // 2))

        def out_view(pair):
            return ps[:, 4 + pair % 2, :]

        def split_out(pair0, gate=None, n_pair=2):
            def finish(dve, pair, link):
                pv_done, out_free = sg["pv_done"], sg["out_free"]
                dve.wait_ge(pv_done.s, pv_done.at(n_pair * (pair + 1)))
                hi, lo, o = x_hi[:, pair0 + pair, :], x_lo[:, pair0 + pair, :], out_view(pair)
                if gate is None:
                    link(dve.tensor_copy(hi, o))
                    dve.tensor_tensor(lo, o, hi.bitcast(F32), ALU.subtract).then_inc(out_free.s, 1)
                else:
                    g = gate[:, pair, :]
                    link(dve.tensor_tensor(g, o, g, ALU.mult))
                    link(dve.tensor_copy(hi, g))
                    dve.tensor_tensor(lo, g, hi.bitcast(F32), ALU.subtract).then_inc(out_free.s, 1)
            return finish

        def add_to_h(first, xs, k_tiles):
            groups = [(k, min(4, k_tiles - k)) for k in range(0, k_tiles, 4)]
            with ExitStack() as c:
                b = c.enter_context(stage())
                last = first + 2 * len(groups) - 1

                @b.sync
                def _(sp):
                    W.load(sp, last)

                @b.gpsimd
                def _(pool):
                    W.split(pool, last + 1)

                @b.tensor
                def _(pe):
                    for half in range(2):
                        for i, (k0, kk) in enumerate(groups):
                            slot = first + half * len(groups) + i
                            pe.wait_ge(W.split_done, slot + 1)
                            hi, lo = W.parts(slot)
                            for tile in range(T):
                                for k in range(kk):
                                    x = [v[:, k0 + k, tile * P:(tile + 1) * P] for v in xs]
                                    mm = product(pe, ps[:, 4 * half + tile, :], [v[:, k, :] for v in (hi, lo)], x,
                                                 k0 + k == 0, k0 + k == k_tiles - 1, True)
                                if tile == T - 1:
                                    mm.then_inc(W.used, 1)
                                if k0 + kk == k_tiles and tile < T - 1:
                                    mm.then_inc(mm_done.s, 1)

                @b.vector
                def _(dve):
                    for half in range(2):
                        for tile in range(T):
                            if tile < T - 1:
                                dve.wait_ge(mm_done.s, mm_done.at(3 * half + tile + 1))
                            else:
                                dve.wait_ge(W.used, first + (half + 1) * len(groups))
                            hv = h[:, tile, half * 512:half * 512 + 512]
                            dve.tensor_tensor(hv, hv, ps[:, 4 * half + tile, :], ALU.add)

            mm_done.passed(6)
            W.at_use = last + 1

        def copy_to(dst):
            return lambda act, i, o: act.activation(dst(i), o, ACT.Copy)

        def silu_to(dst):
            return lambda act, i, o: act.activation(dst(i), o, ACT.Silu)

        tokens_to = lambda dst: (lambda act, tile, i, o: act.activation(dst[:, tile, 256 * i:256 * i + o.shape[1]], o, ACT.Copy))
        xs = (x_hi, x_lo)
        causal_keys = lambda qb: (0, qb + 1)
        by_x = lambda m, qb, w: m[:, (3 - qb) * P:(3 - qb) * P + w]

        W.at_use = 0
        normalize(h, T, C_NORM_G, x_hi, x_lo)
        with ExitStack() as c:
            st = lambda name, shape, dt=F32: c.enter_context(nc.sbuf_tensor(name, shape, dt))
            u = st("ssm_u", [P, 4, S])
            gate_b = st("gate_b", [P, 4, S])
            attention_memory = ExitStack()
            sa = lambda name, shape: attention_memory.enter_context(nc.sbuf_tensor(name, shape, F32))
            qk = sa("ev_qk", [P, 6, S])
            v = sa("ev_v", [P, T, 2 * AD])
            gate_a = sa("gate_a", [P, 4, S])
            project([(w_ev_q, AW, "turned", copy_to(lambda i: qk[:, i, :])),
                     (w_ev_k, 256, "turned", copy_to(lambda i: qk[:, 4 + i, :])),
                     (w_ev_v, 128, "tokens", tokens_to(v)),
                     (w_ev_rest, 512, "turned", silu_to(lambda i: gate_a[:, i, :])),
                     (w_ev_rest + 2, 512, "turned", copy_to(lambda i: u[:, i, :])),
                     (w_ev_rest + 4, 512, "turned", silu_to(lambda i: gate_b[:, i, :]))], xs, S)
            head_norm([(qk[:, i, :], C_EQ if i < 4 else C_EK) for i in range(6)], AD, sel64)

            with ExitStack() as c2:
                window = c2.enter_context(nc.sbuf_tensor("window_bias", [P, AH, 2 * P], F32))
                with ExitStack() as c3:
                    b = c3.enter_context(stage())
                    win_in = sg["b_ready"]

                    @b.sync
                    def _(sp):
                        sp.dma_start(window[:, :, :], bass.AP(bias_rows, AH * P * BX + 127 + 256, [[BX - 1, P], [P * BX, AH], [1, 2 * P]])).then_inc(win_in.s, 16)
                        sp.wait_ge(win_in.s, win_in.at(16))
                win_in.passed(16)
                heads = []
                for i in range(AH):
                    p0 = 64 * (i % 2)
                    kv = i // (AH // AKV)
                    heads.append((qk[p0:p0 + 64, i // 2, :], qk[p0:p0 + 64, 4 + kv, :],
                                  (lambda kv: lambda kb: v[:, kb, kv * AD:(kv + 1) * AD])(kv)))
                attention(heads, lambda qb: (max(qb - 1, 0), qb + 1), AD ** -0.5, split_out(0, gate_a), sinks=neg_sink,
                          bias_of=lambda hd, qb, w: window[:, hd, 2 * P - w:2 * P])

            attention_memory.close()

            with ExitStack() as c2:
                s2 = lambda name, shape, dt=F32: c2.enter_context(nc.sbuf_tensor(name, shape, dt))
                time = s2("time", [P, S])
                wrk = s2("phase", [P, 2, S])
                cs = s2("cos_sin", [P, 2, 2, S])
                vb = s2("v_parts", [P, 4, S])
                z = s2("z", [P, 2, 2, S])
                pr = s2("products", [P, 2, 4, S])
                b = c2.enter_context(stage())
                time_in, turns_ready, table_ready, z_ready, pr_ready = (sg[x] for x in ("b_ready", "a_ready", "c_ready", "d_ready", "e_ready"))
                bu_done, bu_free, y_ready, gelu_done = sg["scores_done"], sg["logits_ready"], sg["pv_done"], sg["out_free"]
                pr_used = sg["turned"]

                @b.sync
                def _(sp):
                    sp.dma_start(time[:, :], t["c_time"]).then_inc(time_in.s, 16)
                    W.load(sp, W.at_use - 1)

                @b.gpsimd
                def _(pool):
                    W.split(pool, W.at_use)
                    for j in range(ST):
                        pool.wait_ge(z_ready.s, z_ready.at(2 * (j + 1)))
                        if j >= 2:
                            pool.wait_ge(pr_used.s, pr_used.at(j - 1))
                        for i, (a, x) in enumerate(((0, 0), (1, 1), (1, 0), (0, 1))):
                            pool.tensor_tensor(pr[:, j % 2, i, :], cs[:, j % 2, a, :], z[:, j % 2, x, :], ALU.mult).then_inc(pr_ready.s, 1)

                @b.scalar
                def _(act):
                    link = linker(act, act_link)
                    for j in range(ST):
                        act.wait_ge(turns_ready.s, turns_ready.at(j + 1))
                        if j >= 2:
                            act.wait_ge(pr_ready.s, pr_ready.at(4 * (j - 1)))
                        act.activation(cs[:, j % 2, 1, :], wrk[:, j % 2, :], ACT.Sin, scale=6.283185)
                        link(act.activation(wrk[:, j % 2, :], wrk[:, j % 2, :], ACT.Abs))
                        act.activation(cs[:, j % 2, 0, :], wrk[:, j % 2, :], ACT.Sin, scale=-6.283185,
                                       bias=pih_col[:, 0:1]).then_inc(table_ready.s, 1)
                    for k in range(4):
                        act.wait_ge(y_ready.s, y_ready.at(k + 1))
                        act.activation(u[:, k, :], u[:, k, :], ACT.Gelu_apprx_tanh).then_inc(gelu_done.s, 1)

                @b.tensor
                def _(pe):
                    def input_products(j):
                        if j >= 2:
                            pe.wait_ge(bu_free.s, bu_free.at(j - 1))
                        p0 = 32 * (j % 4)
                        for part in range(2):
                            mm = pe.matmul(ps[:, 2 * (j % 2) + part, :], ssm_bt[p0:p0 + 32, part, j // 4, :],
                                           u[p0:p0 + 32, j // 4, :], start=True, stop=True)
                        mm.then_inc(bu_done.s, 1)

                    def output_products(j):
                        pe.wait_ge(pr_ready.s, pr_ready.at(4 * (j + 1)))
                        p0 = 32 * (j % 4)
                        for i, part in enumerate((0, 1, 2, 2)):
                            mm = pe.matmul(ps[p0:p0 + 32, 4 + j // 4, :], ssm_ct[:, part, j // 4, p0:p0 + 32],
                                           pr[:, j % 2, i, :], start=i == 0, stop=i == 3)
                        mm.then_inc(pr_used.s, 1)

                    input_products(0)
                    input_products(1)
                    for j in range(ST):
                        output_products(j)
                        if j + 2 < ST:
                            input_products(j + 2)

                @b.vector
                def _(dve):
                    link = linker(dve, dve_link)

                    def turns(j):
                        r = col[:, C_TURN + j:C_TURN + j + 1]
                        if j >= 2:
                            dve.wait_ge(table_ready.s, table_ready.at(j - 1))
                        w = wrk[:, j % 2, :]
                        link(dve.tensor_scalar(w, time[:, :], r, MAGIC, ALU.mult, ALU.add))
                        link(dve.tensor_scalar(w, w, -MAGIC, None, ALU.add, ALU.bypass))
                        dve.scalar_tensor_tensor(w, time[:, :], r, w, ALU.mult, ALU.subtract).then_inc(turns_ready.s, 1)

                    dve.wait_ge(time_in.s, time_in.at(16))
                    turns(0)
                    turns(1)
                    for j in range(ST):
                        dve.wait_ge(table_ready.s, table_ready.at(j + 1))
                        dve.wait_ge(bu_done.s, bu_done.at(j + 1))
                        re, im = ps[:, 2 * (j % 2), :], ps[:, 2 * (j % 2) + 1, :]
                        cos, sin = cs[:, j % 2, 0, :], cs[:, j % 2, 1, :]
                        link(dve.tensor_tensor(vb[:, 0, :], re, cos, ALU.mult))
                        link(dve.tensor_tensor(vb[:, 1, :], im, sin, ALU.mult))
                        link(dve.tensor_tensor(vb[:, 2, :], im, cos, ALU.mult))
                        dve.tensor_tensor(vb[:, 3, :], re, sin, ALU.mult).then_inc(bu_free.s, 1)
                        dve.wait_ge(bu_free.s, bu_free.at(j + 1))
                        link(dve.tensor_tensor(vb[:, 0, :], vb[:, 0, :], vb[:, 1, :], ALU.add))
                        link(dve.tensor_tensor(vb[:, 2, :], vb[:, 2, :], vb[:, 3, :], ALU.subtract))
                        if j >= 2:
                            dve.wait_ge(pr_ready.s, pr_ready.at(4 * (j - 1)))
                        mag = col[:, C_MAG + j:C_MAG + j + 1].to_broadcast([P, S])
                        dve.tensor_tensor_scan(z[:, j % 2, 0, :], mag, vb[:, 0, :], 0.0, ALU.mult, ALU.add).then_inc(z_ready.s, 1)
                        dve.tensor_tensor_scan(z[:, j % 2, 1, :], mag, vb[:, 2, :], 0.0, ALU.mult, ALU.add).then_inc(z_ready.s, 1)
                        dve.wait_ge(z_ready.s, z_ready.at(2 * (j + 1)))
                        if j + 2 < ST:
                            turns(j + 2)
                    dve.wait_ge(pr_used.s, pr_used.at(ST))
                    for k in range(4):
                        ins = dve.scalar_tensor_tensor(u[:, k, :], u[:, k, :], col[:, C_SKIP + k:C_SKIP + k + 1],
                                                       ps[:, 4 + k, :], ALU.mult, ALU.add)
                        ins.then_inc(y_ready.s, 1)
                    for k in range(4):
                        dve.wait_ge(gelu_done.s, gelu_done.at(k + 1))
                        link(dve.tensor_copy(x_hi[:, 4 + k, :], u[:, k, :]))
                        dve.tensor_tensor(x_lo[:, 4 + k, :], u[:, k, :], x_hi[:, 4 + k, :].bitcast(F32), ALU.subtract)
            for s_, n in ((time_in, 16), (turns_ready, ST), (table_ready, ST), (z_ready, 2 * ST), (pr_ready, 4 * ST),
                          (bu_done, ST), (bu_free, ST), (y_ready, 4), (gelu_done, 4), (pr_used, ST)):
                s_.passed(n)

            with ExitStack() as c2:
                val = c2.enter_context(nc.sbuf_tensor("glu_val", [P, 4, S], F32))
                gat = c2.enter_context(nc.sbuf_tensor("glu_gate", [P, 4, S], F32))
                b = c2.enter_context(stage())
                glu_ready = sg["a_ready"]

                @b.sync
                def _(sp):
                    W.load(sp, w_glu + 1)

                @b.gpsimd
                def _(pool):
                    W.split(pool, w_glu + 2)

                @b.tensor
                def _(pe):
                    for half in range(2):
                        pe.wait_ge(W.split_done, w_glu + half + 1)
                        hi, lo = W.parts(w_glu + half)
                        for i in range(4):
                            for k in range(4):
                                mm = product(pe, ps[:, 4 * half + i, :], [w[:, k, i * P:(i + 1) * P] for w in (hi, lo)],
                                             [x[:, 4 + k, :] for x in xs], k == 0, k == 3, False)
                            mm.then_inc(W.used if i == 3 else mm_done.s, 1)

                @b.scalar
                def _(act):
                    for half, (dst, func) in enumerate(((val, ACT.Identity), (gat, ACT.Sigmoid))):
                        for i in range(4):
                            if i < 3:
                                act.wait_ge(mm_done.s, mm_done.at(3 * half + i + 1))
                            else:
                                act.wait_ge(W.used, w_glu + half + 1)
                            bias = col[:, C_GLU + 4 * half + i:C_GLU + 4 * half + i + 1]
                            act.activation(dst[:, i, :], ps[:, 4 * half + i, :], func, bias=bias).then_inc(glu_ready.s, 1)

                @b.vector
                def _(dve):
                    link = linker(dve, dve_link)
                    dve.wait_ge(W.used, w_glu + 2)
                    for i in range(4):
                        dve.wait_ge(glu_ready.s, glu_ready.at(4 + i + 1))
                        link(dve.tensor_tensor(val[:, i, :], val[:, i, :], gat[:, i, :], ALU.mult))
                        link(dve.tensor_tensor(val[:, i, :], val[:, i, :], gate_b[:, i, :], ALU.mult))
                        link(dve.tensor_copy(x_hi[:, 4 + i, :], val[:, i, :]))
                        dve.tensor_tensor(x_lo[:, 4 + i, :], val[:, i, :], x_hi[:, 4 + i, :].bitcast(F32), ALU.subtract)
            mm_done.passed(6)
            glu_ready.passed(8)
            W.at_use = w_glu + 2
        add_to_h(w_ev_out, xs, KD)

        normalize(h, T, C_NORM_G + 8, x_hi, x_lo)
        with ExitStack() as c:
            st = lambda name, shape, dt=F32: c.enter_context(nc.sbuf_tensor(name, shape, dt))
            qk = st("od_qk", [P, 10, S])
            v = st("od_v", [P, T, 2 * CD])
            gate = st("od_gate", [P, 8, S])
            unseen = st("unseen", [P, T, S], BF16)
            with ExitStack() as c2:
                s2 = lambda name, shape, dt=F32: c2.enter_context(nc.sbuf_tensor(name, shape, dt))
                qi = s2("qi", [P, 4, S])
                ki = s2("ki", [P, S])
                wi = s2("wi", [P, T, IH])
                project([(w_od_q, CW, "turned", copy_to(lambda i: qk[:, i, :])),
                         (w_od_k, 256, "turned", copy_to(lambda i: qk[:, 8 + i, :])),
                         (w_od_v, 256, "tokens", tokens_to(v)),
                         (w_od_gate, CW, "turned", silu_to(lambda i: gate[:, i, :])),
                         (w_od_qi, IH * ID, "turned", copy_to(lambda i: qi[:, i, :])),
                         (w_od_ki, 128, "turned", copy_to(lambda i: ki[:, :])),
                         (w_od_wi, IH, "tokens", lambda act, tile, i, o: act.activation(wi[:, tile, :], o, ACT.Copy,
                                                                                     scale=(IH * ID) ** -0.5))], xs, S)
                head_norm([(qk[:, i, :], C_OQ if i < 8 else C_OK) for i in range(10)], CD, sel128)

                seen = s2("seen", [P, 4, S])
                score = s2("score", [P, 2, S])
                top = s2("top", [P, 8])
                b = c2.enter_context(stage())
                dots_done, seen_ready, seen_used = sg["scores_done"], sg["a_ready"], sg["b_ready"]
                index_units = [(qb, i) for qb in range(1, T) for i in range(IH)]

                @b.sync
                def _(sp):
                    W.load(sp, W.at_use - 1)

                @b.gpsimd
                def _(pool):
                    W.split(pool, W.at_use)

                @b.tensor
                def _(pe):
                    for m, (qb, i) in enumerate(index_units):
                        if m >= 4:
                            pe.wait_ge(seen_ready.s, seen_ready.at(m - 3))
                        p0 = 64 * (i % 2)
                        pe.matmul(ps[:, m % 4, 0:(qb + 1) * P], qi[p0:p0 + 64, i // 2, qb * P:(qb + 1) * P],
                                  ki[p0:p0 + 64, 0:(qb + 1) * P], start=True, stop=True).then_inc(dots_done.s, 1)

                @b.scalar
                def _(act):
                    for m, (qb, i) in enumerate(index_units):
                        act.wait_ge(dots_done.s, dots_done.at(m + 1))
                        if m >= 4:
                            act.wait_ge(seen_used.s, seen_used.at(m - 3))
                        w = (qb + 1) * P
                        act.activation(seen[:, m % 4, 0:w], ps[:, m % 4, 0:w], ACT.Relu).then_inc(seen_ready.s, 1)

                @b.vector
                def _(dve):
                    link = linker(dve, dve_link)
                    for m, (qb, i) in enumerate(index_units):
                        w = (qb + 1) * P
                        dve.wait_ge(seen_ready.s, seen_ready.at(m + 1))
                        before = by_x(causal, qb, w) if i == 0 else score[:, (i - 1) % 2, 0:w]
                        dve.scalar_tensor_tensor(score[:, i % 2, 0:w], seen[:, m % 4, 0:w], wi[:, qb, i:i + 1], before,
                                                 ALU.mult, ALU.add).then_inc(seen_used.s, 1)
                        dve.wait_ge(seen_used.s, seen_used.at(m + 1))
                        if i == IH - 1:
                            work = score[:, 1, 0:w]
                            for _ in range(TOPK // 8):
                                link(dve.max(top[:, :], work))
                                link(dve.match_replace(out=work, in_to_replace=top[:, :], in_values=work, imm_value=-BIG))
                            link(dve.tensor_scalar(unseen[:, qb, 0:w], work, -1e35, NEG, ALU.is_gt, ALU.mult))
            n = len(index_units)
            for s_ in (dots_done, seen_ready, seen_used):
                s_.passed(n)

            with ExitStack() as c2:
                far = c2.enter_context(nc.sbuf_tensor("head_bias", [P, 2, S], F32))
                heads = [(qk[:, i, :], qk[:, 8 + i // 4, :], (lambda kv: lambda kb: v[:, kb, kv * CD:(kv + 1) * CD])(i // 4))
                         for i in range(CH)]

                def load_bias(sp, hd):
                    sp.dma_start(far[:, hd % 2, :], bass.AP(bias_rows, hd * P * BX + 127, [[BX - 1, P], [1, S]])).then_inc(bias_in[hd % 2].s, 16)

                def add_unseen(pe, hd, qb, o):
                    return pe.matmul(o, ident_b[:, :], unseen[:, qb, 0:(qb + 1) * P], start=False, stop=True)

                attention(heads, causal_keys, CD ** -0.5, split_out(0, gate, 1),
                          bias_of=lambda hd, qb, w: by_x(far[:, hd % 2, :], qb, w), add=add_unseen, adds=lambda qb: qb > 0,
                          n_pair=1, bias_load=load_bias)
        add_to_h(w_od_out, xs, KD)

        for layer in range(2):
            with ExitStack() as c:
                st = lambda name, shape, dt=F32: c.enter_context(nc.sbuf_tensor(f"{name}{layer}", shape, dt))
                km = st("km", [P, 2, MT])
                vm = st("vm", [P, 2, MH * FD])
                with ExitStack() as c2:
                    mem = c2.enter_context(nc.sbuf_tensor(f"mem{layer}", [P, 2, D], F32))
                    m_hi = c2.enter_context(nc.sbuf_tensor(f"m_hi{layer}", [P, KD, MT], F32R))
                    m_lo = c2.enter_context(nc.sbuf_tensor(f"m_lo{layer}", [P, KD, MT], F32R))
                    with ExitStack() as c3:
                        b = c3.enter_context(stage())

                        @b.sync
                        def _(sp):
                            sp.dma_start(mem[:, :, :], t["mem_2"][0].rearrange("(t p) d -> p t d", p=P)).then_inc(loads_in.s, 16)
                            sp.wait_ge(loads_in.s, loads_in.at(16))
                    loads_in.passed(16)
                    normalize(mem, 2, C_MEM + 8 * layer, m_hi, m_lo)
                    project([(w_mem_k[layer], 256, "turned", copy_to(lambda i: km[:, i, :])),
                             (w_mem_v[layer], 256, "tokens", tokens_to(vm))], (m_hi, m_lo), MT)
                normalize(h, T, C_MIX + 8 * layer, x_hi, x_lo)
                q = st("q", [P, 6, S])
                k = st("k", [P, 6, S])
                v = st("v", [P, T, FH * FD])
                qm = st("qm", [P, 2, S])
                jobs = [(w_q[layer], FW, "turned", copy_to(lambda i: q[:, i, :])),
                        (w_k[layer], FW, "turned", copy_to(lambda i: k[:, i, :])),
                        (w_v[layer], FW, "tokens", tokens_to(v))]
                if layer == 0:
                    fl = st("forget_logit", [P, T, FH])
                    jobs.append((w_forget, FH, "tokens", lambda act, tile, i, o: act.activation(fl[:, tile, :], o, ACT.Copy)))
                jobs.append((w_qm[layer], 256, "turned", copy_to(lambda i: qm[:, i, :])))
                project(jobs, xs, S)

                if layer == 0:
                    cum = st("cum", [FH, S])
                    with ExitStack() as c2:
                        s2 = lambda name, shape, dt=F32: c2.enter_context(nc.sbuf_tensor(name, shape, dt))
                        fz, fa, b_f = s2("fz", [FH, S]), s2("fa", [FH, S]), s2("b_f", [FH, 1])
                        b = c2.enter_context(stage())
                        bf_in, z_ready, soft_ready = sg["b_ready"], sg["a_ready"], sg["c_ready"]

                        @b.sync
                        def _(sp):
                            W.load(sp, W.at_use - 1)

                        @b.gpsimd
                        def _(pool):
                            W.split(pool, W.at_use)

                        @b.tensor
                        def _(pe):
                            for i in range(T):
                                mm = pe.transpose(ps[0:FH, 0, i * P:(i + 1) * P], fl[:, i, :], ident[:, :])
                            mm.then_inc(mm_done.s, 1)

                        @b.scalar
                        def _(act):
                            act.dma_start(b_f[:, :], t["b_forget_2"].rearrange("a h -> h a")).then_inc(bf_in.s, 16)
                            link = linker(act, act_link)
                            act.wait_ge(z_ready.s, z_ready.at(1))
                            link(act.activation(fa[:, :], fz[:, :], ACT.Abs))
                            link(act.activation(fa[:, :], fa[:, :], ACT.Exp, scale=-1.0))
                            act.activation(fa[:, :], fa[:, :], ACT.Ln, bias=1.0).then_inc(soft_ready.s, 1)

                        @b.vector
                        def _(dve):
                            link = linker(dve, dve_link)
                            dve.wait_ge(mm_done.s, mm_done.at(1))
                            dve.wait_ge(bf_in.s, bf_in.at(16))
                            dve.tensor_scalar(fz[:, :], ps[0:FH, 0, :], b_f[:, 0:1], None, ALU.add).then_inc(z_ready.s, 1)
                            dve.wait_ge(soft_ready.s, soft_ready.at(1))
                            link(dve.scalar_tensor_tensor(fz[:, :], fz[:, :], 0.0, fa[:, :], ALU.min, ALU.subtract))
                            link(dve.memset(fa[:, :], 1.0))
                            link(dve.tensor_tensor_scan(cum[:, :], fa[:, :], fz[:, :], 0.0, ALU.mult, ALU.add))
                            dve.tensor_scalar(cum[:, :], cum[:, :], -FD ** 0.5, None, ALU.mult)
                    for s_, n in ((bf_in, 16), (z_ready, 1), (soft_ready, 1), (mm_done, 1)):
                        s_.passed(n)
                else:
                    with ExitStack() as c2:
                        s2 = lambda name, shape, dt=F32: c2.enter_context(nc.sbuf_tensor(name, shape, dt))
                        cos, sin, swap = s2("rope_cos", [P, S]), s2("rope_sin", [P, S]), s2("rope_swap", [P, P])
                        tmp = s2("rope_tmp", [P, 2, S])
                        b = c2.enter_context(stage())
                        rope_in, rot_used = sg["b_ready"], sg["a_ready"]
                        tiles_ = [q[:, i, :] for i in range(6)] + [k[:, i, :] for i in range(6)]

                        @b.sync
                        def _(sp):
                            for dst, src in ((cos, "c_rope_cos"), (sin, "c_rope_sin"), (swap, "c_rope_swap")):
                                sp.dma_start(dst[:, :], t[src]).then_inc(rope_in.s, 16)
                            W.load(sp, W.at_use - 1)

                        @b.gpsimd
                        def _(pool):
                            W.split(pool, W.at_use)

                        @b.tensor
                        def _(pe):
                            pe.wait_ge(rope_in.s, rope_in.at(48))
                            for i, x in enumerate(tiles_):
                                if i >= 8:
                                    pe.wait_ge(rot_used.s, rot_used.at(i - 7))
                                pe.matmul(ps[:, i % 8, :], swap[:, :], x, start=True, stop=True).then_inc(mm_done.s, 1)

                        @b.vector
                        def _(dve):
                            link = linker(dve, dve_link)
                            dve.wait_ge(rope_in.s, rope_in.at(48))
                            for i, x in enumerate(tiles_):
                                dve.wait_ge(mm_done.s, mm_done.at(i + 1))
                                dve.tensor_tensor(tmp[:, i % 2, :], ps[:, i % 8, :], sin[:, :], ALU.mult).then_inc(rot_used.s, 1)
                                link(dve.tensor_tensor(x, x, cos[:, :], ALU.mult))
                                link(dve.tensor_tensor(x, x, tmp[:, i % 2, :], ALU.add))
                    rope_in.passed(48)
                    rot_used.passed(12)
                    mm_done.passed(12)

                def head_list(q_, k_, v_, n, d=FD):
                    return [(q_[64 * (i % 2):64 * (i % 2) + 64, i // 2, :], k_[64 * (i % 2):64 * (i % 2) + 64, i // 2, :],
                             (lambda i: lambda kb: v_[:, kb, i * d:(i + 1) * d])(i)) for i in range(n)]

                with ExitStack() as c2:
                    mask = c2.enter_context(nc.sbuf_tensor(f"mask{layer}", [P, S], F32))
                    with ExitStack() as c3:
                        b = c3.enter_context(stage())

                        @b.sync
                        def _(sp):
                            if layer == 1:
                                sp.dma_start(mask[:, :], t["c_dilated"]).then_inc(loads_in.s, 16)
                                sp.wait_ge(loads_in.s, loads_in.at(16))

                        @b.vector
                        def _(dve):
                            if layer == 0:
                                dve.memset(mask[:, :], 0.0)
                    if layer == 1:
                        loads_in.passed(16)
                    if layer == 0:
                        def add_decay(pe, hd, qb, o):
                            return pe.matmul(o, sel128[0:FH, hd * P:(hd + 1) * P], cum[:, 0:(qb + 1) * P], start=False, stop=True)
                        attention(head_list(q, k, v, FH), causal_keys, FD ** -0.5, split_out(0),
                                  bias_of=lambda hd, qb, w: by_x(causal, qb, w), add=add_decay)
                    else:
                        attention(head_list(q, k, v, FH), causal_keys, FD ** -0.5, split_out(0),
                                  bias_of=lambda hd, qb, w: by_x(mask, qb, w))
                    with ExitStack() as c3:
                        zero = c3.enter_context(nc.sbuf_tensor(f"zero{layer}", [P, MT], F32))
                        with ExitStack() as c4:
                            b = c4.enter_context(stage())

                            @b.vector
                            def _(dve):
                                dve.memset(zero[:, :], 0.0)
                        attention(head_list(qm, km, vm, MH), lambda qb: (0, 2), FD ** -0.5, split_out(6),
                                  bias_of=lambda hd, qb, w: zero[:, 0:w])
            add_to_h(w_out[layer], xs, KD)

            normalize(h, T, C_FFN + 8 * layer, x_hi, x_lo)
            for part in range(2):
                with ExitStack() as c:
                    st = lambda name, shape, dt=F32: c.enter_context(nc.sbuf_tensor(f"{name}{layer}{part}", shape, dt))
                    a_hi, a_lo = st("a_hi", [P, HALF, S], F32R), st("a_lo", [P, HALF, S], F32R)
                    with ExitStack() as c2:
                        cv = c2.enter_context(nc.sbuf_tensor(f"cv{layer}{part}", [P, 3, 2, S], F32))
                        b = c2.enter_context(stage())
                        first = w_up[layer, part]
                        base_ready, conv_done, silu_done, cv_free = sg["a_ready"], sg["b_ready"], sg["c_ready"], sg["d_ready"]
                        tap = lambda j, half, i: col[:, C_CONV + 176 * layer + 44 * j + FC * half + part * HALF + i:][:, 0:1]

                        @b.sync
                        def _(sp):
                            W.load(sp, first + HALF - 1)

                        @b.gpsimd
                        def _(pool):
                            W.split(pool, first + HALF)

                        @b.tensor
                        def _(pe):
                            for i in range(HALF):
                                pe.wait_ge(W.split_done, first + i + 1)
                                hi, lo = W.parts(first + i)
                                if i >= 4:
                                    pe.wait_ge(bank_free.s, bank_free.at(i - 3))
                                for half in range(2):
                                    for kt in range(KD):
                                        mm = product(pe, ps[:, (2 * i + half) % 8, :], [w[:, kt, half * P:half * P + P] for w in (hi, lo)],
                                                     [x[:, kt, :] for x in xs], kt == 0, kt == KD - 1, False)
                                mm.then_inc(W.used, 1)

                        @b.scalar
                        def _(act):
                            def base(i):
                                act.wait_ge(W.used, first + i + 1)
                                if i >= 3:
                                    act.wait_ge(cv_free.s, cv_free.at(i - 2))
                                for half in range(2):
                                    act.activation(cv[:, i % 3, half, :], ps[:, (2 * i + half) % 8, :], ACT.Identity,
                                                   scale=tap(2, half, i), bias=tap(3, half, i)).then_inc(base_ready.s, 1)

                            def gate_silu(i):
                                act.wait_ge(conv_done.s, conv_done.at(i + 1))
                                act.activation(cv[:, i % 3, 1, :], cv[:, i % 3, 1, :], ACT.Silu).then_inc(silu_done.s, 1)

                            base(0)
                            for i in range(HALF):
                                if i + 1 < HALF:
                                    base(i + 1)
                                gate_silu(i)

                        @b.vector
                        def _(dve):
                            link = linker(dve, dve_link)

                            def conv(i):
                                dve.wait_ge(base_ready.s, base_ready.at(2 * i + 2))
                                for back, j in ((1, 1), (2, 0)):
                                    for half in range(2):
                                        o = cv[:, i % 3, half, back:S]
                                        ins = dve.scalar_tensor_tensor(o, ps[:, (2 * i + half) % 8, 0:S - back], tap(j, half, i), o,
                                                                       ALU.mult, ALU.add)
                                        if back == 1:
                                            link(ins)
                                        elif half == 0:
                                            link(ins)
                                ins.then_inc(bank_free.s, 1)
                                dve.wait_ge(bank_free.s, bank_free.at(i + 1))
                                dve.sem_inc(conv_done.s, 1)

                            def join(i):
                                dve.wait_ge(silu_done.s, silu_done.at(i + 1))
                                a = cv[:, i % 3, 0, :]
                                link(dve.tensor_tensor(a, a, cv[:, i % 3, 1, :], ALU.mult))
                                link(dve.tensor_copy(a_hi[:, i, :], a))
                                dve.tensor_tensor(a_lo[:, i, :], a, a_hi[:, i, :].bitcast(F32), ALU.subtract).then_inc(cv_free.s, 1)

                            conv(0)
                            for i in range(HALF):
                                if i + 1 < HALF:
                                    conv(i + 1)
                                join(i)

                    for s_, n in ((bank_free, HALF), (base_ready, 2 * HALF), (conv_done, HALF), (silu_done, HALF), (cv_free, HALF)):
                        s_.passed(n)
                    W.at_use = first + HALF
                    add_to_h(w_down[layer, part], (a_hi, a_lo), HALF)

        with ExitStack() as c:
            st = lambda name, shape, dt=F32: c.enter_context(nc.sbuf_tensor(name, shape, dt))
            gain = st("final_gain", [P, D])
            res = st("res", [P, T, D])
            stat = st("final_stat", [P, 3 * T])
            b = c.enter_context(stage())
            gain_in, root_ready, res_ready, stored = sg["b_ready"], sg["a_ready"], sg["c_ready"], sg["stored"]

            @b.sync
            def _(sp):
                sp.dma_start(gain[:, :], t["norm_final_2"].rearrange("(a d) -> a d", a=1).to_broadcast([P, D])).then_inc(gain_in.s, 16)
                for i in range(T):
                    sp.wait_ge(res_ready.s, res_ready.at(i + 1))
                    sp.dma_start(out[0, i * P:(i + 1) * P, :], res[:, i, :]).then_inc(stored.s, 16)
                sp.wait_ge(stored.s, stored.at(16 * T))

            @b.scalar
            def _(act):
                link = linker(act, act_link)
                for i in range(T):
                    link(act.activation(res[:, i, :], h[:, i, :], ACT.Square, accum_out=stat[:, i:i + 1]))
                act.activation(stat[:, T:2 * T], stat[:, 0:T], ACT.Sqrt, scale=1.0 / D, bias=eps_col[:, 0:1]).then_inc(root_ready.s, 1)

            @b.vector
            def _(dve):
                link = linker(dve, dve_link)
                dve.wait_ge(gain_in.s, gain_in.at(16))
                dve.wait_ge(root_ready.s, root_ready.at(1))
                link(dve.reciprocal(stat[:, 2 * T:3 * T], stat[:, T:2 * T]))
                for i in range(T):
                    dve.scalar_tensor_tensor(res[:, i, :], h[:, i, :], stat[:, 2 * T + i:2 * T + i + 1], gain[:, :],
                                             ALU.mult, ALU.mult).then_inc(res_ready.s, 1)


def constants():
    f = np.float32
    p, x = np.arange(P)[:, None], np.arange(S)[None, :]
    dist = p - x + 384
    causal = np.where(dist >= 0, f(0), f(NEG)).astype(f)
    n = np.maximum(511 - np.arange(BX), 0)
    nf = np.maximum(n, 1).astype(f)
    large = NB // 2 + (np.log(nf / f(NB // 2)) / f(math.log(1024 / (NB // 2))) * f(NB - NB // 2)).astype(np.int32)
    bucket_of = np.where(n < NB // 2, n, np.minimum(large, NB - 1))
    bucket = (bucket_of[None, :] == np.arange(NB)[:, None]).astype(f)
    d = 511 - np.arange(BX)
    neg = np.zeros((AH, 2, BX), f)
    neg[:, 0, :] = np.where(d < 0, f(NEG), f(0))
    neg[:, 1, :] = np.where((d < 0) | (d >= P), f(NEG), f(0))
    count = (dist >= 0) * ((dist <= 128).astype(int) + (dist % 4 == 0) + (dist % 16 == 0))
    dilated = np.where(count > 0, np.log(np.maximum(count, 1)) * math.sqrt(FD), NEG).astype(f)
    head_sum = np.zeros((P, 2, 40), f)
    head_sum[:64, 0, 20] = head_sum[64:, 0, 21] = 1 / 64
    head_sum[:, 1, 20] = 1 / 128
    sel64 = np.zeros((12, 6 * P), f)
    sel128 = np.zeros((12, 12 * P), f)
    for r in range(12):
        sel64[r, 64 * r:64 * r + 64] = 1
        sel128[r, P * r:P * r + P] = 1
    inv = f(1) / (f(10000.0) ** (np.arange(0, 64, 2, dtype=f) / f(64)))
    ang = np.arange(S, dtype=f)[:, None] * inv[None, :]
    cos, sin = (np.tile(g(ang).astype(f).T, (4, 1)) for g in (np.cos, np.sin))
    swap = np.zeros((P, P), f)
    for m in range(P):
        swap[m + 32 if m % 64 < 32 else m - 32, m] = -1 if m % 64 < 32 else 1
    time = np.tile(np.arange(S, dtype=f)[None, :], (P, 1))
    return {"c_causal": causal, "c_bucket": bucket, "c_neg_rows": neg, "c_dilated": dilated, "c_head_sum": head_sum,
            "c_sel64": sel64, "c_sel128": sel128, "c_rope_cos": np.ascontiguousarray(cos), "c_rope_sin": np.ascontiguousarray(sin),
            "c_rope_swap": swap, "c_time": time, "c_ident": np.eye(P, dtype=f)}


def kernel(**inputs):
    import concourse.bacc as bacc
    from concourse.bass_utils import run_bass_kernel_spmd

    nc = bacc.Bacc("TRN2", target_bir_lowering=False, num_devices=1)
    arrays = {name: np.ascontiguousarray(a) for name, a in inputs.items()}
    arrays.update(constants())
    views = {name: nc.dram_tensor(name, a.shape, mybir.dt.from_np(a.dtype), kind="ExternalInput").ap()
             for name, a in arrays.items()}
    out = nc.dram_tensor("y", (1, S, D), F32, kind="ExternalOutput").ap()
    block_kernel(nc, views, out)
    result = run_bass_kernel_spmd(nc, [arrays], core_ids=[0])
    return result.results[0]["y"]
```

```python
import math
from contextlib import ExitStack

import numpy as np

import concourse.bass as bass
from concourse import mybir

F32 = mybir.dt.float32
F32R = mybir.dt.float32r
BF16 = mybir.dt.bfloat16
I32 = mybir.dt.int32
ALU = mybir.AluOpType
ACT = mybir.ActivationFunctionType

P = 128
S = 512
T = S // P
D = 1024
KD = D // P
EPS = 1e-6
NEG = -1e30
BIG = 3e38
MAGIC = 12582912.0

AH, AD, AKV = 8, 64, 2
CH, CD, CKV = 8, 128, 2
IH, ID = 8, 64
TOPK = 128
G, GH, GP = 32, 16, 64
ST = G * GP // P
FH, FD = 12, 64
MH, MT = 4, 256
DFF = 2816
FC = DFF // P
NB = 32
BX = 640

C_NORM_G, C_MIX, C_MEM, C_FFN, C_GLU, C_SKIP, C_EQ, C_EK, C_OQ, C_OK = 0, 16, 32, 48, 64, 72, 76, 77, 78, 79
C_ROWS = 80
C_CONV = C_ROWS
C_MAG = C_CONV + 2 * 176
C_TURN, C_FRE, C_FIM = C_MAG + ST, C_MAG + 2 * ST, C_MAG + 3 * ST
C_COLS = C_MAG + 4 * ST

RAW, SPLIT, SLOT = 2, 3, 2048


class Signal:

    def __init__(self, ctx, nc, name):
        self.s = ctx.enter_context(nc.semaphore(name))
        self.base = 0

    def at(self, n):
        return self.base + n

    def passed(self, n):
        self.base += n


class Weights:

    def __init__(self, ctx, nc):
        self.slots = []
        self.raw = ctx.enter_context(nc.sbuf_tensor("w_raw", [P, RAW, SLOT], F32))
        self.hi = ctx.enter_context(nc.sbuf_tensor("w_hi", [P, SPLIT, SLOT], F32R))
        self.lo = ctx.enter_context(nc.sbuf_tensor("w_lo", [P, SPLIT, SLOT], F32R))
        self.loaded = [ctx.enter_context(nc.semaphore(f"w_loaded{i}")) for i in range(RAW)]
        self.hi_done = ctx.enter_context(nc.semaphore("w_hi_done"))
        self.split_done = ctx.enter_context(nc.semaphore("w_split_done"))
        self.used = ctx.enter_context(nc.semaphore("w_used"))
        self.sent = 0
        self.cut = 0
        self.arrived = [0] * RAW
        self.need = []

    def add(self, kk, nn, pieces):
        self.slots.append((kk, nn, pieces))
        r = (len(self.slots) - 1) % RAW
        self.arrived[r] += 16 * len(pieces)
        self.need.append(self.arrived[r])

    def load(self, sp, until):
        for n in range(self.sent, min(len(self.slots), until + RAW + SPLIT)):
            kk, nn, pieces = self.slots[n]
            if n >= RAW:
                sp.wait_ge(self.split_done, n - RAW + 1)
            dst = self.raw[:, n % RAW, 0:kk * nn].rearrange("p (k n) -> p k n", k=kk)
            for c, src in pieces:
                sp.dma_start(dst[:, :, c:c + src.shape[2]], src).then_inc(self.loaded[n % RAW], 16)
            self.sent = n + 1

    def split(self, pool, until):
        for n in range(self.cut, min(len(self.slots), until + SPLIT)):
            kk, nn, _ = self.slots[n]
            size = kk * nn
            raw, hi, lo = self.raw[:, n % RAW, 0:size], self.hi[:, n % SPLIT, 0:size], self.lo[:, n % SPLIT, 0:size]
            pool.wait_ge(self.loaded[n % RAW], self.need[n])
            if n >= SPLIT:
                pool.wait_ge(self.used, n - SPLIT + 1)
            pool.tensor_scalar(hi, raw, 1.0, 1.0, ALU.mult, ALU.mult).then_inc(self.hi_done, 1)
            pool.wait_ge(self.hi_done, n + 1)
            pool.tensor_tensor(lo, raw, hi.bitcast(F32), ALU.subtract).then_inc(self.split_done, 1)
            self.cut = n + 1

    def parts(self, n):
        kk, nn, _ = self.slots[n]
        view = lambda t: t[:, n % SPLIT, 0:kk * nn].rearrange("p (k n) -> p k n", k=kk)
        return view(self.hi), view(self.lo)


def block_kernel(nc, t, out):
    ctx = ExitStack()
    with ctx:
        sb = lambda name, shape, dt=F32: ctx.enter_context(nc.sbuf_tensor(name, shape, dt))
        sig = lambda name: Signal(ctx, nc, name)
        W = Weights(ctx, nc)

        def tiles(w, k0, kk):
            return w[k0 * P:(k0 + kk) * P, :].rearrange("(k p) n -> p k n", p=P)

        def wide(w, c0, width, kd=KD):
            first = len(W.slots)
            for c in range(c0, c0 + width, 256):
                n = min(256, c0 + width - c)
                W.add(kd, n, [(0, tiles(w, 0, kd)[:, :, c:c + n])])
            return first

        def deep(w, k_first, k_tiles):
            first = len(W.slots)
            for half in range(2):
                for k in range(k_first, k_first + k_tiles, 4):
                    kk = min(4, k_first + k_tiles - k)
                    W.add(kk, 512, [(0, tiles(w, k, kk)[:, :, half * 512:half * 512 + 512])])
            return first

        ev, od, fox, dil = t["ev_w_in"][0], t["od_w_in"][0], t["w_in_fox_2"][0], t["w_in_dil_2"][0]
        AW, CW, FW = AH * AD, CH * CD, FH * FD
        w_ev_q = wide(ev, 0, AW)
        w_ev_k = len(W.slots)
        W.add(KD, 4 * AD, [(64 * i, tiles(ev, 0, KD)[:, :, AW + 64 * (i // 2):AW + 64 * (i // 2) + 64]) for i in range(4)])
        w_ev_v = wide(ev, AW + 128, 128)
        w_ev_rest = wide(ev, AW + 256, 3 * 512)
        w_glu = len(W.slots)
        for half in range(2):
            W.add(4, 512, [(0, tiles(t["ev_glu_w"][0], 0, 4)[:, :, half * 512:half * 512 + 512])])
        w_ev_out = deep(t["ev_w_out"][0], 0, KD)
        w_od_q = wide(od, 0, CW)
        w_od_k = wide(od, CW, 256)
        w_od_v = wide(od, CW + 256, 256)
        w_od_gate = wide(od, CW + 512, CW)
        w_od_qi = wide(od, 2 * CW + 512, IH * ID)
        w_od_ki = len(W.slots)
        ki0 = 2 * CW + 512 + IH * ID
        W.add(KD, 2 * ID, [(64 * i, tiles(od, 0, KD)[:, :, ki0:ki0 + 64]) for i in range(2)])
        w_od_wi = wide(od, ki0 + 64, IH)
        w_od_out = deep(t["od_w_out"][0], 0, KD)
        w_mem_k, w_mem_v, w_q, w_k, w_v, w_qm, w_out = ([0, 0] for _ in range(7))
        HALF = FC // 2
        w_up, w_down = {}, {}
        for layer in range(2):
            w_mem_k[layer] = wide(t["w_mem_kv_2"][layer], 0, 256)
            w_mem_v[layer] = wide(t["w_mem_kv_2"][layer], 256, 256)
            w_in = (fox, dil)[layer]
            w_q[layer] = wide(w_in, 0, FW)
            w_k[layer] = wide(w_in, FW, FW)
            w_v[layer] = wide(w_in, 2 * FW, FW)
            if layer == 0:
                w_forget = wide(w_in, 3 * FW, FH)
            w_qm[layer] = wide(w_in, 3 * FW + (FH if layer == 0 else 0), 256)
            w_out[layer] = deep(t["w_out_2"][layer], 0, KD)
            for part in range(2):
                first = len(W.slots)
                for i in range(part * HALF, (part + 1) * HALF):
                    up = tiles(t["w_up_2"][layer], 0, KD)
                    W.add(KD, 256, [(0, up[:, :, i * P:(i + 1) * P]), (P, up[:, :, DFF + i * P:DFF + (i + 1) * P])])
                w_up[layer, part] = first
                w_down[layer, part] = deep(t["w_down_2"][layer], part * HALF, HALF)

        h = sb("h", [P, T, D])
        x_hi = sb("x_hi", [P, KD, S], F32R)
        x_lo = sb("x_lo", [P, KD, S], F32R)
        col = sb("col", [P, C_COLS])
        ident = sb("ident", [P, P])
        ident_b = sb("ident_b", [P, P], BF16)
        causal = sb("causal", [P, S])
        head_sum = sb("head_sum", [P, 2, 40])
        sel128 = sb("sel128", [12, 12 * P])
        eps_col = sb("eps_col", [P, 1])
        pih_col = sb("pih_col", [P, 1])
        norm_stat = sb("norm_stat", [P, 3 * T])
        neg_sink = sb("neg_sink", [P, AH])
        ssm_bt = sb("ssm_bt", [P, 2, 4, P])
        ssm_ct = sb("ssm_ct", [P, 3, 4, P])
        ps = ctx.enter_context(nc.psum_tensor("ps", [P, 8, 512], F32))
        bias_rows = nc.dram_tensor("bias_rows", [2, AH, P, BX], F32, kind="Internal")

        dve_link, act_link = sig("dve_link"), sig("act_link")
        names = ("mm_done", "bank_free", "loads_in", "a_ready", "b_ready", "c_ready", "d_ready", "e_ready",
                 "scores_done", "logits_ready", "probs_ready", "probs_scaled", "turned", "turned_copied",
                 "pv_done", "out_free", "bias_in", "bias_in2", "dt_in", "stored",
                 "n_root", "n_normed", "n_hi", "n_turned", "n_x", "added")
        sg = {n: sig(n) for n in names}
        mm_done, bank_free, loads_in = sg["mm_done"], sg["bank_free"], sg["loads_in"]
        bias_in = (sg["bias_in"], sg["bias_in2"])

        def linker(eng, link):
            def run(ins):
                link.passed(1)
                ins.then_inc(link.s, 1)
                eng.wait_ge(link.s, link.base)
            return run

        def stage():
            return nc.Block()

        def product(pe, o, w, x, start, stop, token_major):
            for i, (a, b) in enumerate(((w[0], x[0]), (w[0], x[1]), (w[1], x[0]))):
                l, r = (b, a) if token_major else (a, b)
                mm = pe.matmul(o, l, r, start=start and i == 0, stop=stop and i == 2)
            return mm

        with ExitStack() as c:
            st = lambda name, shape, dt=F32: c.enter_context(nc.sbuf_tensor(name, shape, dt))
            rows = st("rows", [C_ROWS, P])
            conv_rows = st("conv_rows", [88, 4, P])
            bucket = st("bucket", [NB, BX])
            rel = st("rel", [NB, AH])
            neg_rows = st("neg_rows", [AH, 2, BX])
            brow = st("brow", [AH, 2, BX])
            a_rows = st("a_rows", [16, 2, P])
            dtl = st("dtl", [16, 2])
            R = st("R", [16, 26, P])
            RI = st("RI", [16, P], I32)
            par = st("par", [16, 4, P])
            b_in = st("b_in", [P, 2, ST, GH])
            bb = st("bb", [P, 2, ST, GH])
            b_tmp = st("b_tmp", [P, ST, GH])
            b_pre = st("b_pre", [P, 2, 4, P])
            c_pre = st("c_pre", [P, 2, 4, P])
            sink_b = st("sink_b", [P, AH])
            b = c.enter_context(stage())
            zeroed, par_in, brow_ready, rows_stored = sg["a_ready"], sg["b_ready"], sg["c_ready"], sg["d_ready"]
            turned_in, par_done, dt_in, bb_ready = sg["turned"], sg["probs_ready"], sg["dt_in"], sg["e_ready"]
            n_loads = []

            @b.sync
            def _(sp):
                sp.dma_start(h[:, :, :], t["x"][0].rearrange("(t p) d -> p t d", p=P)).then_inc(loads_in.s, 16)
                W.load(sp, -SPLIT)
                sp.wait_ge(brow_ready.s, brow_ready.at(1))
                for a in range(2):
                    sp.dma_start(bias_rows[a, :, :, :], brow[:, a, :].unsqueeze(1).to_broadcast([AH, P, BX])).then_inc(rows_stored.s, 16)
                sp.wait_ge(rows_stored.s, rows_stored.at(32))
                sp.wait_ge(loads_in.s, loads_in.at(16))

            @b.gpsimd
            def _(pool):
                pool.memset(c_pre[:, :, :, :], 0.0).then_inc(zeroed.s, 1)

            @b.scalar
            def _(act):
                def load(dst, src):
                    act.dma_start(dst, src).then_inc(par_in.s, 16)
                    n_loads.append(1)
                for l in range(2):
                    for name, c0 in (("norm_g", C_NORM_G), ("norm_mix_2", C_MIX), ("norm_mem_2", C_MEM), ("norm_ffn_2", C_FFN)):
                        load(rows[c0 + 8 * l:c0 + 8 * l + 8, :], t[name][l].rearrange("(k p) -> k p", p=P))
                    for j in range(2):
                        load(conv_rows[44 * j:44 * j + 44, 2 * l, :], t["conv_w_2"][l, j].rearrange("(k p) -> k p", p=P))
                    load(conv_rows[0:44, 2 * l + 1, :], t["conv_w_2"][l, 2].rearrange("(k p) -> k p", p=P))
                    load(conv_rows[44:88, 2 * l + 1, :], t["conv_b_2"][l].rearrange("(k p) -> k p", p=P))
                load(rows[C_GLU:C_GLU + 8, :], t["ev_glu_b"][0].rearrange("(k p) -> k p", p=P))
                load(rows[C_SKIP:C_SKIP + 4, :], t["ev_ssm_d"][0].rearrange("(k g) h -> k (g h)", k=4))
                for c0, name in ((C_EQ, "ev_q_norm_g"), (C_EK, "ev_k_norm_g")):
                    for i in range(2):
                        load(rows[c0:c0 + 1, 64 * i:64 * i + 64], t[name])
                load(rows[C_OQ:C_OQ + 1, :], t["od_q_norm_g"])
                load(rows[C_OK:C_OK + 1, :], t["od_k_norm_g"])
                load(dtl[:, :], t["ev_ssm_log_dt"][0].rearrange("(j g) -> j g", g=2))
                load(a_rows[:, 0, :], t["ev_ssm_a_re"][0].rearrange("(j g) p -> j (g p)", g=2))
                load(a_rows[:, 1, :], t["ev_ssm_a_im"][0].rearrange("(j g) p -> j (g p)", g=2))
                load(b_in[:, 0, :, :], t["ev_ssm_b_re"][0].rearrange("(j g) p h -> (g p) j h", g=2))
                load(b_in[:, 1, :, :], t["ev_ssm_b_im"][0].rearrange("(j g) p h -> (g p) j h", g=2))
                load(rel[:, :], t["rel_bias"])
                load(bucket[:, :], t["c_bucket"])
                load(neg_rows[:, :, :], t["c_neg_rows"])
                load(ident[:, :], t["c_ident"])
                load(causal[:, :], t["c_causal"])
                load(head_sum[:, :, :], t["c_head_sum"])
                load(sel128[:, :], t["c_sel128"])
                load(sink_b[:, :], t["ev_sinks"].to_broadcast([P, AH]))
                act.wait_ge(zeroed.s, zeroed.at(1))
                for part, name in enumerate(("ev_ssm_c_re", "ev_ssm_c_im")):
                    for g in range(8):
                        src = t[name][0].rearrange("(c g) h p -> g h c p", g=8)[g]
                        load(c_pre[16 * g:16 * g + 16, part, :, 64 * (g % 2):64 * (g % 2) + 64], src)
                act.wait_ge(dt_in.s, dt_in.at(1))
                act.activation(R[:, 12, :], R[:, 11, :], ACT.Sin, scale=6.283185).then_inc(dt_in.s, 1)
                act.activation(R[:, 13, :], R[:, 11, :], ACT.Sin, scale=3.1415925).then_inc(dt_in.s, 1)
                act.wait_ge(turned_in.s, turned_in.at(1))
                act.activation(col[:, 0:C_ROWS], ps[:, 0, 0:C_ROWS], ACT.Copy).then_inc(par_done.s, 1)
                act.activation(col[:, C_CONV:C_CONV + 352], ps[:, 1, 0:352], ACT.Copy).then_inc(par_done.s, 1)
                act.wait_ge(turned_in.s, turned_in.at(4))
                for i, (part, sign) in enumerate(((0, 1.0), (0, -1.0), (1, -1.0))):
                    act.activation(ssm_ct[:, i, :, :], ps[:, 4 + part, :].rearrange("p (c n) -> p c n", c=4),
                                   ACT.Copy, scale=sign).then_inc(par_done.s, 1)
                act.wait_ge(turned_in.s, turned_in.at(5))
                for part in range(2):
                    act.activation(ssm_bt[:, part, :, :], ps[:, 6 + part, :].rearrange("p (c n) -> p c n", c=4),
                                   ACT.Copy).then_inc(par_done.s, 1)

            @b.tensor
            def _(pe):
                pe.wait_ge(par_in.s, par_in.at(16 * len(n_loads)))
                pe.transpose(ps[:, 0, 0:C_ROWS], rows[:, :], ident[0:C_ROWS, 0:C_ROWS])
                for i in range(4):
                    mm = pe.transpose(ps[:, 1, 88 * i:88 * i + 88], conv_rows[:, i, :], ident[0:88, 0:88])
                mm.then_inc(turned_in.s, 1)
                pe.matmul(ps[0:AH, 2, :], rel[:, :], bucket[:, 0:512], start=True, stop=True)
                pe.matmul(ps[0:AH, 3, 0:BX - 512], rel[:, :], bucket[:, 512:BX], start=True, stop=True).then_inc(turned_in.s, 1)
                pe.wait_ge(par_done.s, par_done.at(2))
                pe.wait_ge(brow_ready.s, brow_ready.at(2))
                for i in range(4):
                    mm = pe.transpose(ps[:, 1, 16 * i:16 * i + 16], par[:, i, :], ident[0:16, 0:16])
                mm.then_inc(turned_in.s, 1)
                for part in range(2):
                    for k in range(4):
                        mm = pe.transpose(ps[:, 4 + part, k * P:(k + 1) * P], c_pre[:, part, k, :], ident[:, :])
                mm.then_inc(turned_in.s, 1)
                pe.wait_ge(bb_ready.s, bb_ready.at(1))
                for part in range(2):
                    for k in range(4):
                        mm = pe.transpose(ps[:, 6 + part, k * P:(k + 1) * P], b_pre[:, part, k, :], ident[:, :])
                mm.then_inc(turned_in.s, 1)

            @b.vector
            def _(dve):
                link = linker(dve, dve_link)
                dve.memset(eps_col[:, :], EPS)
                dve.memset(pih_col[:, :], math.pi / 2)
                link(dve.memset(b_pre[:, :, :, :], 0.0))
                dve.wait_ge(par_in.s, par_in.at(16 * len(n_loads)))
                dve.tensor_copy(ident_b[:, :], ident[:, :])
                link(dve.tensor_scalar(neg_sink[:, :], sink_b[:, :], -1.0, None, ALU.mult))
                dve.wait_ge(turned_in.s, turned_in.at(2))
                for a, root in enumerate((CD ** 0.5, AD ** 0.5)):
                    dve.scalar_tensor_tensor(brow[:, a, 0:512], ps[0:AH, 2, :], root, neg_rows[:, a, 0:512], ALU.mult, ALU.add)
                    ins = dve.scalar_tensor_tensor(brow[:, a, 512:BX], ps[0:AH, 3, 0:BX - 512], root, neg_rows[:, a, 512:BX],
                                                   ALU.mult, ALU.add)
                ins.then_inc(brow_ready.s, 1)
                dve.wait_ge(brow_ready.s, brow_ready.at(1))

                tt = lambda o, a, x, op: link(dve.tensor_tensor(o, a, x, op))
                ts = lambda o, a, s1, s2, op0, op1: link(dve.tensor_scalar(o, a, s1, s2, op0, op1))
                r = lambda i: R[:, i, :]

                def exp_parts(z, power, frac, tmp):
                    ts(tmp, z, -87.0, 88.0, ALU.max, ALU.min)
                    ts(power, tmp, 1.0 / math.log(2), MAGIC, ALU.mult, ALU.add)
                    ts(power, power, -MAGIC, None, ALU.add, ALU.bypass)
                    link(dve.scalar_tensor_tensor(tmp, power, -0.693359375, tmp, ALU.mult, ALU.add))
                    link(dve.scalar_tensor_tensor(tmp, power, 2.12194440e-4, tmp, ALU.mult, ALU.add))
                    ts(frac, tmp, 1.0 / 9, 1.0, ALU.mult, ALU.add)
                    for k in range(8, 1, -1):
                        tt(frac, frac, tmp, ALU.mult)
                        ts(frac, frac, 1.0 / k, 1.0, ALU.mult, ALU.add)
                    tt(frac, frac, tmp, ALU.mult)
                    ts(RI[:, :], power, 127.0, None, ALU.add, ALU.bypass)
                    ts(RI[:, :], RI[:, :], 23, None, ALU.logical_shift_left, ALU.bypass)
                    link(dve.tensor_copy(power, RI[:, :].bitcast(F32)))

                a_re, a_im = a_rows[:, 0, :], a_rows[:, 1, :]
                link(dve.tensor_copy(r(0).rearrange("j (g p) -> j g p", g=2), dtl[:, :].unsqueeze(2).to_broadcast([16, 2, 64])))
                exp_parts(r(0), r(1), r(2), r(3))
                tt(r(4), r(1), r(2), ALU.mult)
                tt(r(4), r(4), r(1), ALU.add)
                tt(r(5), a_re, r(4), ALU.mult)
                exp_parts(r(5), r(6), r(7), r(3))
                tt(r(8), r(6), r(7), ALU.mult)
                tt(par[:, 0, :], r(8), r(6), ALU.add)
                ts(r(9), r(6), -1.0, None, ALU.add, ALU.bypass)
                tt(r(9), r(9), r(8), ALU.add)
                tt(r(10), a_im, r(4), ALU.mult)
                ts(r(10), r(10), 1.0 / (2 * math.pi), None, ALU.mult, ALU.bypass)
                ts(r(11), r(10), MAGIC, -MAGIC, ALU.add, ALU.add)
                tt(par[:, 1, :], r(10), r(11), ALU.subtract)
                dve.tensor_copy(r(11), par[:, 1, :]).then_inc(dt_in.s, 1)
                dve.wait_ge(dt_in.s, dt_in.at(3))
                tt(r(14), r(13), r(13), ALU.mult)
                ts(r(14), r(14), -2.0, None, ALU.mult, ALU.bypass)
                tt(r(15), r(9), r(14), ALU.mult)
                tt(r(15), r(15), r(9), ALU.add)
                tt(r(15), r(15), r(14), ALU.add)
                tt(r(16), par[:, 0, :], r(12), ALU.mult)
                tt(r(17), a_re, a_re, ALU.mult)
                tt(r(18), a_im, a_im, ALU.mult)
                tt(r(17), r(17), r(18), ALU.add)
                link(dve.reciprocal(r(17), r(17)))
                tt(r(19), r(15), a_re, ALU.mult)
                tt(r(20), r(16), a_im, ALU.mult)
                tt(r(19), r(19), r(20), ALU.add)
                tt(par[:, 2, :], r(19), r(17), ALU.mult)
                tt(r(21), r(16), a_re, ALU.mult)
                tt(r(22), r(15), a_im, ALU.mult)
                tt(r(21), r(21), r(22), ALU.subtract)
                dve.tensor_tensor(par[:, 3, :], r(21), r(17), ALU.mult).then_inc(brow_ready.s, 1)
                dve.wait_ge(turned_in.s, turned_in.at(3))
                link(dve.tensor_copy(col[:, C_MAG:C_COLS], ps[:, 1, 0:4 * ST]))
                fre = col[:, C_FRE:C_FRE + ST].unsqueeze(2).to_broadcast([P, ST, GH])
                fim = col[:, C_FIM:C_FIM + ST].unsqueeze(2).to_broadcast([P, ST, GH])
                b_re, b_im = b_in[:, 0, :, :], b_in[:, 1, :, :]
                tt(bb[:, 0, :, :], fre, b_re, ALU.mult)
                tt(b_tmp[:, :, :], fim, b_im, ALU.mult)
                tt(bb[:, 0, :, :], bb[:, 0, :, :], b_tmp[:, :, :], ALU.subtract)
                tt(bb[:, 1, :, :], fre, b_im, ALU.mult)
                tt(b_tmp[:, :, :], fim, b_re, ALU.mult)
                tt(bb[:, 1, :, :], bb[:, 1, :, :], b_tmp[:, :, :], ALU.add)
                for part in range(2):
                    for g in range(2):
                        for j in range(4):
                            ins = dve.tensor_copy(b_pre[64 * g:64 * g + 64, part, :, 32 * j + 16 * g:32 * j + 16 * g + 16],
                                                  bb[64 * g:64 * g + 64, part, j::4, :])
                            if (part, g, j) != (1, 1, 3):
                                link(ins)
                ins.then_inc(bb_ready.s, 1)

        for s_, n in ((zeroed, 1), (par_in, 16 * len(n_loads)), (brow_ready, 2), (rows_stored, 32), (turned_in, 5),
                      (par_done, 7), (dt_in, 3), (bb_ready, 1), (loads_in, 16)):
            s_.passed(n)

        class Norm:

            def __init__(self, src, n_tiles, gain, hi, lo, normed, stat):
                self.src, self.n_tiles, self.gain, self.hi, self.lo = src, n_tiles, gain, hi, lo
                self.normed, self.stat, self.n = normed, stat, n_tiles * P
                self.root_ready, self.normed_ready, self.hi_ready = sg["n_root"], sg["n_normed"], sg["n_hi"]
                self.turned, self.x_ready = sg["n_turned"], sg["n_x"]

            def scalar(self, act):
                link, n = linker(act, act_link), self.n
                for i in range(self.n_tiles):
                    link(act.activation(ps[:, 6:8, :].rearrange("p a b -> p (a b)"), self.src[:, i, :], ACT.Square,
                                        accum_out=self.stat[:, i:i + 1]))
                    act.activation(self.stat[:, T + i:T + i + 1], self.stat[:, i:i + 1], ACT.Sqrt, scale=1.0 / D,
                                   bias=eps_col[:, 0:1]).then_inc(self.root_ready.s, 1)
                for k in range(KD):
                    act.wait_ge(self.turned.s, self.turned.at(k + 1))
                    act.activation(self.hi[:, k, 0:n], ps[:, k, 0:n], ACT.Copy,
                                   scale=col[:, self.gain + k:self.gain + k + 1]).then_inc(self.hi_ready.s, 1)

            def vector(self, dve):
                link, n, stat = linker(dve, dve_link), self.n, self.stat
                for i in range(self.n_tiles):
                    dve.wait_ge(self.root_ready.s, self.root_ready.at(i + 1))
                    link(dve.reciprocal(stat[:, 2 * T + i:2 * T + i + 1], stat[:, T + i:T + i + 1]))
                    dve.tensor_scalar(self.normed[:, i, :], self.src[:, i, :], stat[:, 2 * T + i:2 * T + i + 1], None,
                                      ALU.mult).then_inc(self.normed_ready.s, 1)
                for k in range(KD):
                    dve.wait_ge(self.hi_ready.s, self.hi_ready.at(k + 1))
                    dve.scalar_tensor_tensor(self.lo[:, k, 0:n], ps[:, k, 0:n], col[:, self.gain + k:self.gain + k + 1],
                                             self.hi[:, k, 0:n].bitcast(F32), ALU.mult, ALU.subtract).then_inc(self.x_ready.s, 1)

            def tensor(self, pe):
                for i in range(self.n_tiles):
                    pe.wait_ge(self.normed_ready.s, self.normed_ready.at(i + 1))
                    for k in range(KD):
                        if k == 6 and i < self.n_tiles - 1:
                            pe.wait_ge(self.root_ready.s, self.root_ready.at(self.n_tiles))
                        mm = pe.transpose(ps[:, k, i * P:(i + 1) * P], self.normed[:, i, k * P:(k + 1) * P], ident[:, :])
                        if i == self.n_tiles - 1:
                            mm.then_inc(self.turned.s, 1)

            def wait_x(self, pe, k):
                pe.wait_ge(self.x_ready.s, self.x_ready.at(k + 1))

            def passed(self):
                for s_, k in ((self.root_ready, self.n_tiles), (self.normed_ready, self.n_tiles), (self.hi_ready, KD),
                              (self.turned, KD), (self.x_ready, KD)):
                    s_.passed(k)

        W.at_use = 0

        def project(jobs, norm, n):
            xs = (norm.hi, norm.lo)
            NBANK = 8
            plan = []
            for first, width, kind, evacuate in jobs:
                for i, c0 in enumerate(range(0, width, 256)):
                    cols = min(256, width - c0)
                    if kind == "turned":
                        for j in range(cols // P):
                            plan.append((first + i, j, kind, None, evacuate, 2 * i + j, cols))
                    else:
                        for tt_ in range(n // P):
                            plan.append((first + i, 0, kind, tt_, evacuate, i, cols))
            last = max(p[0] for p in plan)
            ends = [m == len(plan) - 1 or plan[m + 1][0] != plan[m][0] for m in range(len(plan))]
            told = [m + 1 - sum(ends[:m + 1]) for m in range(len(plan))]
            with ExitStack() as c:
                b = c.enter_context(stage())

                @b.sync
                def _(sp):
                    W.load(sp, last)

                @b.gpsimd
                def _(pool):
                    W.split(pool, last + 1)

                @b.vector
                def _(dve):
                    norm.vector(dve)

                @b.tensor
                def _(pe):
                    norm.tensor(pe)
                    for m, (slot, j, kind, tile, _, _, cols) in enumerate(plan):
                        if m == 0 or plan[m - 1][0] != slot:
                            pe.wait_ge(W.split_done, slot + 1)
                        if m >= NBANK:
                            pe.wait_ge(bank_free.s, bank_free.at(m - NBANK + 1))
                        hi, lo = W.parts(slot)
                        for k in range(KD):
                            if m == 0:
                                norm.wait_x(pe, k)
                            if kind == "turned":
                                w = [v[:, k, j * P:(j + 1) * P] for v in (hi, lo)]
                                mm = product(pe, ps[:, m % NBANK, 0:n], w, [v[:, k, 0:n] for v in xs], k == 0, k == KD - 1, False)
                            else:
                                w = [v[:, k, 0:cols] for v in (hi, lo)]
                                x = [v[:, k, tile * P:(tile + 1) * P] for v in xs]
                                mm = product(pe, ps[:, m % NBANK, 0:cols], w, x, k == 0, k == KD - 1, True)
                        mm.then_inc(W.used if ends[m] else mm_done.s, 1)

                @b.scalar
                def _(act):
                    norm.scalar(act)
                    for m, (slot, j, kind, tile, evacuate, i, cols) in enumerate(plan):
                        if ends[m]:
                            act.wait_ge(W.used, slot + 1)
                        else:
                            act.wait_ge(mm_done.s, mm_done.at(told[m]))
                        if kind == "turned":
                            evacuate(act, i, ps[:, m % NBANK, 0:n]).then_inc(bank_free.s, 1)
                        else:
                            evacuate(act, tile, i, ps[:, m % NBANK, 0:cols]).then_inc(bank_free.s, 1)

            norm.passed()
            mm_done.passed(told[-1])
            bank_free.passed(len(plan))
            W.at_use = last + 1

        def head_norm(parts_, d_head):
            per = P // d_head
            n_rows = per * len(parts_)
            which = 0 if d_head == 64 else 1
            with ExitStack() as c:
                st = lambda name, shape, dt=F32: c.enter_context(nc.sbuf_tensor(nc.get_next_instruction_name() + name, shape, dt))
                sq = st("sq", [P, 2, S])
                inv = st("inv", [12, S])
                sel = sel128 if d_head == 128 else st("sel64", [12, 6 * P])
                b = c.enter_context(stage())
                squared, summed, root_ready, inv_ready = sg["a_ready"], sg["b_ready"], sg["c_ready"], sg["d_ready"]

                @b.sync
                def _(sp):
                    if d_head == 64:
                        sp.dma_start(sel[:, :], t["c_sel64"]).then_inc(loads_in.s, 16)
                    W.load(sp, W.at_use - 1)

                @b.gpsimd
                def _(pool):
                    W.split(pool, W.at_use)

                @b.scalar
                def _(act):
                    for i, (x, _) in enumerate(parts_):
                        if i >= 2:
                            act.wait_ge(summed.s, summed.at(i - 1))
                        act.activation(sq[:, i % 2, :], x, ACT.Square).then_inc(squared.s, 1)
                    act.wait_ge(summed.s, summed.at(len(parts_)))
                    act.activation(inv[0:n_rows, :], ps[0:n_rows, 0, :], ACT.Sqrt, bias=eps_col[0:n_rows, 0:1]).then_inc(root_ready.s, 1)

                @b.tensor
                def _(pe):
                    for i in range(len(parts_)):
                        pe.wait_ge(squared.s, squared.at(i + 1))
                        c0 = 20 - per * i
                        pe.matmul(ps[0:n_rows, 0, :], head_sum[:, which, c0:c0 + n_rows], sq[:, i % 2, :],
                                  start=i == 0, stop=i == len(parts_) - 1).then_inc(summed.s, 1)
                    if d_head == 64:
                        pe.wait_ge(loads_in.s, loads_in.at(16))
                    pe.wait_ge(inv_ready.s, inv_ready.at(1))
                    for i in range(len(parts_)):
                        if i >= 6:
                            pe.wait_ge(bank_free.s, bank_free.at(i - 5))
                        pe.matmul(ps[:, 1 + i % 6, :], sel[0:n_rows, i * P:(i + 1) * P], inv[0:n_rows, :],
                                  start=True, stop=True).then_inc(mm_done.s, 1)

                @b.vector
                def _(dve):
                    dve.wait_ge(root_ready.s, root_ready.at(1))
                    dve.reciprocal(inv[0:n_rows, :], inv[0:n_rows, :]).then_inc(inv_ready.s, 1)
                    for i, (x, gain) in enumerate(parts_):
                        dve.wait_ge(mm_done.s, mm_done.at(i + 1))
                        dve.scalar_tensor_tensor(x, x, col[:, gain:gain + 1], ps[:, 1 + i % 6, :],
                                                 ALU.mult, ALU.mult).then_inc(bank_free.s, 1)

            if d_head == 64:
                loads_in.passed(16)
            k = len(parts_)
            for s_, n in ((squared, k), (summed, k), (root_ready, 1), (inv_ready, 1), (mm_done, k), (bank_free, k)):
                s_.passed(n)

        def attention(heads, keys, scale, finish, sinks=None, bias_of=None, add=None, adds=lambda qb: True,
                      n_pair=2, bias_load=None):
            nh = len(heads)
            units = [(hd, qb) for hd in range(nh) for qb in range(T)]
            AHEAD, LEAD, NL = 3, 2, 4
            with ExitStack() as c:
                st = lambda name, shape, dt=F32: c.enter_context(nc.sbuf_tensor(nc.get_next_instruction_name() + name, shape, dt))
                L = st("L", [P, NL, S])
                PT = st("PT", [P, 2, T, S])
                stat = st("stat", [P, NL, 4])
                b = c.enter_context(stage())
                scores_done, logits_ready, probs_ready, probs_scaled = (sg[x] for x in ("scores_done", "logits_ready", "probs_ready", "probs_scaled"))
                turned, turned_copied, pv_done, out_free = (sg[x] for x in ("turned", "turned_copied", "pv_done", "out_free"))

                @b.sync
                def _(sp):
                    W.load(sp, W.at_use - 1)
                    if bias_load:
                        for hd in range(nh):
                            if hd >= 2:
                                sp.wait_ge(logits_ready.s, logits_ready.at(T * (hd - 1)))
                            bias_load(sp, hd)

                @b.gpsimd
                def _(pool):
                    W.split(pool, W.at_use)

                def width(qb):
                    k0, k1 = keys(qb)
                    return (k1 - k0) * P

                @b.tensor
                def _(pe):
                    def scores(u):
                        hd, qb = units[u]
                        q, k, _ = heads[hd]
                        k0, k1 = keys(qb)
                        if u >= AHEAD + 1:
                            pe.wait_ge(logits_ready.s, logits_ready.at(u - AHEAD))
                        o = ps[:, u % (AHEAD + 1), 0:width(qb)]
                        more = add is not None and adds(qb)
                        mm = pe.matmul(o, q[:, qb * P:(qb + 1) * P], k[:, k0 * P:k1 * P], start=True, stop=not more)
                        if more:
                            mm = add(pe, hd, qb, o)
                        mm.then_inc(scores_done.s, 1)

                    def turn(u):
                        hd, qb = units[u]
                        pe.wait_ge(probs_scaled.s, probs_scaled.at(u + 1))
                        if u >= 2:
                            pe.wait_ge(turned_copied.s, turned_copied.at(u - 1))
                        k0, k1 = keys(qb)
                        for i in range(k1 - k0):
                            mm = pe.transpose(ps[:, 4 + u % 2, i * P:(i + 1) * P], L[:, u % NL, i * P:(i + 1) * P], ident[:, :])
                        mm.then_inc(turned.s, 1)

                    def values(hd):
                        pe.wait_ge(turned_copied.s, turned_copied.at(T * (hd + 1)))
                        pair = hd // n_pair
                        if pair >= 2 and hd % n_pair == 0:
                            pe.wait_ge(out_free.s, out_free.at(pair - 1))
                        _, _, v = heads[hd]
                        d = v(0).shape[1]
                        p0 = d * (hd % n_pair)
                        kt = max(keys(qb)[1] for qb in range(T))
                        for kb in range(kt):
                            qs = [qb for qb in range(T) if keys(qb)[0] <= kb < keys(qb)[1]]
                            a, z = qs[0] * P, (qs[-1] + 1) * P
                            mm = pe.matmul(ps[p0:p0 + d, 6 + pair % 2, a:z], v(kb), PT[:, hd % 2, kb, a:z],
                                           start=kb == 0, stop=kb == kt - 1, skip_group_check=True)
                        mm.then_inc(pv_done.s, 1)

                    for u in range(AHEAD):
                        scores(u)
                    for u in range(len(units)):
                        if u + AHEAD < len(units):
                            scores(u + AHEAD)
                        turn(u)
                        if u % T == 0 and u > 0:
                            values(u // T - 1)
                    values(nh - 1)

                @b.vector
                def _(dve):
                    link = linker(dve, dve_link)

                    def logits(u):
                        hd, qb = units[u]
                        if u >= NL:
                            dve.wait_ge(turned.s, turned.at(u - NL + 1))
                        dve.wait_ge(scores_done.s, scores_done.at(u + 1))
                        if bias_load and qb == 0:
                            arrived = bias_in[hd % 2]
                            dve.wait_ge(arrived.s, arrived.at(16 * (hd // 2 + 1)))
                        w = width(qb)
                        init = BIG if sinks is None else sinks[:, hd:hd + 1]
                        dve.tensor_tensor_reduce(out=L[:, u % NL, 0:w], in0=ps[:, u % (AHEAD + 1), 0:w], in1=bias_of(hd, qb, w), scale=-scale,
                                                 scalar=init, op0=ALU.add, op1=ALU.min,
                                                 accum_out=stat[:, u % NL, 0:1]).then_inc(logits_ready.s, 1)

                    def scaled(u):
                        hd, qb = units[u]
                        dve.wait_ge(probs_ready.s, probs_ready.at(u + 1))
                        if sinks is not None:
                            link(dve.tensor_tensor(stat[:, u % NL, 1:2], stat[:, u % NL, 1:2], stat[:, u % NL, 3:4], ALU.add))
                        link(dve.reciprocal(stat[:, u % NL, 2:3], stat[:, u % NL, 1:2]))
                        w = width(qb)
                        dve.tensor_scalar(L[:, u % NL, 0:w], L[:, u % NL, 0:w], stat[:, u % NL, 2:3], None,
                                          ALU.mult).then_inc(probs_scaled.s, 1)

                    for u in range(LEAD):
                        logits(u)
                    for u in range(len(units)):
                        if u + LEAD < len(units):
                            logits(u + LEAD)
                        scaled(u)
                        if u % T == 2 and u > T and (u // T) % n_pair == 0:
                            finish(dve, u // T // n_pair - 1, link)
                    finish(dve, nh // n_pair - 1, link)

                @b.scalar
                def _(act):
                    def probs(u):
                        hd, qb = units[u]
                        act.wait_ge(logits_ready.s, logits_ready.at(u + 1))
                        w = width(qb)
                        if sinks is not None:
                            act.activation(stat[:, u % NL, 3:4], sinks[:, hd:hd + 1], ACT.Exp, scale=-1.0,
                                           bias=stat[:, u % NL, 0:1])
                        act.activation(L[:, u % NL, 0:w], L[:, u % NL, 0:w], ACT.Exp, scale=-1.0, bias=stat[:, u % NL, 0:1],
                                       accum_out=stat[:, u % NL, 1:2]).then_inc(probs_ready.s, 1)

                    def copy(u):
                        hd, qb = units[u]
                        if hd >= 2 and qb == 0:
                            act.wait_ge(pv_done.s, pv_done.at(hd - 1))
                        act.wait_ge(turned.s, turned.at(u + 1))
                        k0, k1 = keys(qb)
                        act.activation(PT[:, hd % 2, k0:k1, qb * P:(qb + 1) * P],
                                       ps[:, 4 + u % 2, 0:(k1 - k0) * P].rearrange("p (k q) -> p k q", q=P),
                                       ACT.Copy).then_inc(turned_copied.s, 1)

                    for u in range(LEAD):
                        probs(u)
                    for u in range(len(units)):
                        if u + LEAD < len(units):
                            probs(u + LEAD)
                        copy(u)

            n = len(units)
            for s_, k in ((scores_done, n), (logits_ready, n), (probs_ready, n), (probs_scaled, n), (turned, n),
                          (turned_copied, n), (pv_done, nh), (out_free, nh // n_pair)):
                s_.passed(k)
            if bias_load:
                for s_ in bias_in:
                    s_.passed(16 * (nh // 2))

        def out_view(pair):
            return ps[:, 6 + pair % 2, :]

        def split_out(pair0, gate=None, n_pair=2):
            def finish(dve, pair, link):
                pv_done, out_free = sg["pv_done"], sg["out_free"]
                dve.wait_ge(pv_done.s, pv_done.at(n_pair * (pair + 1)))
                hi, lo, o = x_hi[:, pair0 + pair, :], x_lo[:, pair0 + pair, :], out_view(pair)
                if gate is None:
                    link(dve.tensor_copy(hi, o))
                    dve.tensor_tensor(lo, o, hi.bitcast(F32), ALU.subtract).then_inc(out_free.s, 1)
                else:
                    g = gate[:, pair, :]
                    link(dve.tensor_tensor(g, o, g, ALU.mult))
                    link(dve.tensor_copy(hi, g))
                    dve.tensor_tensor(lo, g, hi.bitcast(F32), ALU.subtract).then_inc(out_free.s, 1)
            return finish

        def add_to_h(first, xs, k_tiles):
            groups = [(k, min(4, k_tiles - k)) for k in range(0, k_tiles, 4)]
            with ExitStack() as c:
                b = c.enter_context(stage())
                last = first + 2 * len(groups) - 1

                @b.sync
                def _(sp):
                    W.load(sp, last)

                @b.gpsimd
                def _(pool):
                    W.split(pool, last + 1)

                @b.tensor
                def _(pe):
                    for half in range(2):
                        for i, (k0, kk) in enumerate(groups):
                            slot = first + half * len(groups) + i
                            pe.wait_ge(W.split_done, slot + 1)
                            hi, lo = W.parts(slot)
                            for tile in range(T):
                                for k in range(kk):
                                    x = [v[:, k0 + k, tile * P:(tile + 1) * P] for v in xs]
                                    mm = product(pe, ps[:, 4 * half + tile, :], [v[:, k, :] for v in (hi, lo)], x,
                                                 k0 + k == 0, k0 + k == k_tiles - 1, True)
                                if tile == T - 1:
                                    mm.then_inc(W.used, 1)
                                if k0 + kk == k_tiles and tile < T - 1:
                                    mm.then_inc(mm_done.s, 1)

                @b.vector
                def _(dve):
                    for half in range(2):
                        for tile in range(T):
                            if tile < T - 1:
                                dve.wait_ge(mm_done.s, mm_done.at(3 * half + tile + 1))
                            else:
                                dve.wait_ge(W.used, first + (half + 1) * len(groups))
                            hv = h[:, tile, half * 512:half * 512 + 512]
                            dve.tensor_tensor(hv, hv, ps[:, 4 * half + tile, :], ALU.add)

            mm_done.passed(6)
            W.at_use = last + 1

        def copy_to(dst):
            return lambda act, i, o: act.activation(dst(i), o, ACT.Copy)

        def silu_to(dst):
            return lambda act, i, o: act.activation(dst(i), o, ACT.Silu)

        tokens_to = lambda dst: (lambda act, tile, i, o: act.activation(dst[:, tile, 256 * i:256 * i + o.shape[1]], o, ACT.Copy))
        xs = (x_hi, x_lo)
        as_rows = lambda tiles_: tiles_[:, 0:8, :].rearrange("p (t a) s -> p t (a s)", a=2)
        causal_keys = lambda qb: (0, qb + 1)
        by_x = lambda m, qb, w: m[:, (3 - qb) * P:(3 - qb) * P + w]

        W.at_use = 0
        with ExitStack() as c:
            st = lambda name, shape, dt=F32: c.enter_context(nc.sbuf_tensor(name, shape, dt))
            u = st("ssm_u", [P, 4, S])
            gate_b = st("gate_b", [P, 4, S])
            attention_memory = ExitStack()
            sa = lambda name, shape: attention_memory.enter_context(nc.sbuf_tensor(name, shape, F32))
            qk = sa("ev_qk", [P, 6, S])
            v = sa("ev_v", [P, T, 2 * AD])
            gate_a = sa("gate_a", [P, 4, S])
            with ExitStack() as c2:
              normed = c2.enter_context(nc.sbuf_tensor("ev_normed", [P, T, D], F32))
              project([(w_ev_q, AW, "turned", copy_to(lambda i: qk[:, i, :])),
                     (w_ev_k, 256, "turned", copy_to(lambda i: qk[:, 4 + i, :])),
                     (w_ev_v, 128, "tokens", tokens_to(v)),
                     (w_ev_rest, 512, "turned", silu_to(lambda i: gate_a[:, i, :])),
                     (w_ev_rest + 2, 512, "turned", copy_to(lambda i: u[:, i, :])),
                     (w_ev_rest + 4, 512, "turned", silu_to(lambda i: gate_b[:, i, :]))],
                      Norm(h, T, C_NORM_G, x_hi, x_lo, normed, norm_stat), S)
            head_norm([(qk[:, i, :], C_EQ if i < 4 else C_EK) for i in range(6)], AD)

            with ExitStack() as c2:
                window = c2.enter_context(nc.sbuf_tensor("window_bias", [P, AH, 2 * P], F32))
                with ExitStack() as c3:
                    b = c3.enter_context(stage())
                    win_in = sg["b_ready"]

                    @b.sync
                    def _(sp):
                        sp.dma_start(window[:, :, :], bass.AP(bias_rows, AH * P * BX + 127 + 256, [[BX - 1, P], [P * BX, AH], [1, 2 * P]])).then_inc(win_in.s, 16)
                        sp.wait_ge(win_in.s, win_in.at(16))
                win_in.passed(16)
                heads = []
                for i in range(AH):
                    p0 = 64 * (i % 2)
                    kv = i // (AH // AKV)
                    heads.append((qk[p0:p0 + 64, i // 2, :], qk[p0:p0 + 64, 4 + kv, :],
                                  (lambda kv: lambda kb: v[:, kb, kv * AD:(kv + 1) * AD])(kv)))
                attention(heads, lambda qb: (max(qb - 1, 0), qb + 1), AD ** -0.5, split_out(0, gate_a), sinks=neg_sink,
                          bias_of=lambda hd, qb, w: window[:, hd, 2 * P - w:2 * P])

            attention_memory.close()

            with ExitStack() as c2:
                s2 = lambda name, shape, dt=F32: c2.enter_context(nc.sbuf_tensor(name, shape, dt))
                time = s2("time", [P, S])
                wrk = s2("phase", [P, 2, S])
                cs = s2("cos_sin", [P, 2, 2, S])
                vb = s2("v_parts", [P, 4, S])
                z = s2("z", [P, 2, 2, S])
                pr = s2("products", [P, 2, 4, S])
                b = c2.enter_context(stage())
                time_in, turns_ready, table_ready, z_ready, pr_ready = (sg[x] for x in ("b_ready", "a_ready", "c_ready", "d_ready", "e_ready"))
                bu_done, bu_free, y_ready, gelu_done = sg["scores_done"], sg["logits_ready"], sg["pv_done"], sg["out_free"]
                pr_used = sg["turned"]

                @b.sync
                def _(sp):
                    sp.dma_start(time[:, :], t["c_time"]).then_inc(time_in.s, 16)
                    W.load(sp, W.at_use - 1)

                @b.gpsimd
                def _(pool):
                    W.split(pool, W.at_use)
                    for j in range(ST):
                        pool.wait_ge(z_ready.s, z_ready.at(2 * (j + 1)))
                        if j >= 2:
                            pool.wait_ge(pr_used.s, pr_used.at(j - 1))
                        for i, (a, x) in enumerate(((0, 0), (1, 1), (1, 0), (0, 1))):
                            pool.tensor_tensor(pr[:, j % 2, i, :], cs[:, j % 2, a, :], z[:, j % 2, x, :], ALU.mult).then_inc(pr_ready.s, 1)

                @b.scalar
                def _(act):
                    link = linker(act, act_link)
                    for j in range(ST):
                        act.wait_ge(turns_ready.s, turns_ready.at(j + 1))
                        if j >= 2:
                            act.wait_ge(pr_ready.s, pr_ready.at(4 * (j - 1)))
                        act.activation(cs[:, j % 2, 1, :], wrk[:, j % 2, :], ACT.Sin, scale=6.283185)
                        link(act.activation(wrk[:, j % 2, :], wrk[:, j % 2, :], ACT.Abs))
                        act.activation(cs[:, j % 2, 0, :], wrk[:, j % 2, :], ACT.Sin, scale=-6.283185,
                                       bias=pih_col[:, 0:1]).then_inc(table_ready.s, 1)
                    for k in range(4):
                        act.wait_ge(y_ready.s, y_ready.at(k + 1))
                        act.activation(u[:, k, :], u[:, k, :], ACT.Gelu_apprx_tanh).then_inc(gelu_done.s, 1)

                @b.tensor
                def _(pe):
                    def input_products(j):
                        if j >= 2:
                            pe.wait_ge(bu_free.s, bu_free.at(j - 1))
                        p0 = 32 * (j % 4)
                        for part in range(2):
                            mm = pe.matmul(ps[:, 2 * (j % 2) + part, :], ssm_bt[p0:p0 + 32, part, j // 4, :],
                                           u[p0:p0 + 32, j // 4, :], start=True, stop=True)
                        mm.then_inc(bu_done.s, 1)

                    def output_products(j):
                        pe.wait_ge(pr_ready.s, pr_ready.at(4 * (j + 1)))
                        p0 = 32 * (j % 4)
                        for i, part in enumerate((0, 1, 2, 2)):
                            mm = pe.matmul(ps[p0:p0 + 32, 4 + j // 4, :], ssm_ct[:, part, j // 4, p0:p0 + 32],
                                           pr[:, j % 2, i, :], start=i == 0, stop=i == 3)
                        mm.then_inc(pr_used.s, 1)

                    input_products(0)
                    input_products(1)
                    for j in range(ST):
                        output_products(j)
                        if j + 2 < ST:
                            input_products(j + 2)

                @b.vector
                def _(dve):
                    link = linker(dve, dve_link)

                    def turns(j):
                        r = col[:, C_TURN + j:C_TURN + j + 1]
                        if j >= 2:
                            dve.wait_ge(table_ready.s, table_ready.at(j - 1))
                        w = wrk[:, j % 2, :]
                        link(dve.tensor_scalar(w, time[:, :], r, MAGIC, ALU.mult, ALU.add))
                        link(dve.tensor_scalar(w, w, -MAGIC, None, ALU.add, ALU.bypass))
                        dve.scalar_tensor_tensor(w, time[:, :], r, w, ALU.mult, ALU.subtract).then_inc(turns_ready.s, 1)

                    dve.wait_ge(time_in.s, time_in.at(16))
                    turns(0)
                    turns(1)
                    for j in range(ST):
                        dve.wait_ge(table_ready.s, table_ready.at(j + 1))
                        dve.wait_ge(bu_done.s, bu_done.at(j + 1))
                        re, im = ps[:, 2 * (j % 2), :], ps[:, 2 * (j % 2) + 1, :]
                        cos, sin = cs[:, j % 2, 0, :], cs[:, j % 2, 1, :]
                        link(dve.tensor_tensor(vb[:, 0, :], re, cos, ALU.mult))
                        link(dve.tensor_tensor(vb[:, 1, :], im, sin, ALU.mult))
                        link(dve.tensor_tensor(vb[:, 2, :], im, cos, ALU.mult))
                        dve.tensor_tensor(vb[:, 3, :], re, sin, ALU.mult).then_inc(bu_free.s, 1)
                        dve.wait_ge(bu_free.s, bu_free.at(j + 1))
                        link(dve.tensor_tensor(vb[:, 0, :], vb[:, 0, :], vb[:, 1, :], ALU.add))
                        link(dve.tensor_tensor(vb[:, 2, :], vb[:, 2, :], vb[:, 3, :], ALU.subtract))
                        if j >= 2:
                            dve.wait_ge(pr_ready.s, pr_ready.at(4 * (j - 1)))
                        mag = col[:, C_MAG + j:C_MAG + j + 1].to_broadcast([P, S])
                        dve.tensor_tensor_scan(z[:, j % 2, 0, :], mag, vb[:, 0, :], 0.0, ALU.mult, ALU.add).then_inc(z_ready.s, 1)
                        dve.tensor_tensor_scan(z[:, j % 2, 1, :], mag, vb[:, 2, :], 0.0, ALU.mult, ALU.add).then_inc(z_ready.s, 1)
                        dve.wait_ge(z_ready.s, z_ready.at(2 * (j + 1)))
                        if j + 2 < ST:
                            turns(j + 2)
                    dve.wait_ge(pr_used.s, pr_used.at(ST))
                    for k in range(4):
                        ins = dve.scalar_tensor_tensor(u[:, k, :], u[:, k, :], col[:, C_SKIP + k:C_SKIP + k + 1],
                                                       ps[:, 4 + k, :], ALU.mult, ALU.add)
                        ins.then_inc(y_ready.s, 1)
                    for k in range(4):
                        dve.wait_ge(gelu_done.s, gelu_done.at(k + 1))
                        link(dve.tensor_copy(x_hi[:, 4 + k, :], u[:, k, :]))
                        dve.tensor_tensor(x_lo[:, 4 + k, :], u[:, k, :], x_hi[:, 4 + k, :].bitcast(F32), ALU.subtract)
            for s_, n in ((time_in, 16), (turns_ready, ST), (table_ready, ST), (z_ready, 2 * ST), (pr_ready, 4 * ST),
                          (bu_done, ST), (bu_free, ST), (y_ready, 4), (gelu_done, 4), (pr_used, ST)):
                s_.passed(n)

            with ExitStack() as c2:
                val = c2.enter_context(nc.sbuf_tensor("glu_val", [P, 4, S], F32))
                gat = c2.enter_context(nc.sbuf_tensor("glu_gate", [P, 4, S], F32))
                b = c2.enter_context(stage())
                glu_ready = sg["a_ready"]

                @b.sync
                def _(sp):
                    W.load(sp, w_glu + 1)

                @b.gpsimd
                def _(pool):
                    W.split(pool, w_glu + 2)

                @b.tensor
                def _(pe):
                    for half in range(2):
                        pe.wait_ge(W.split_done, w_glu + half + 1)
                        hi, lo = W.parts(w_glu + half)
                        for i in range(4):
                            for k in range(4):
                                mm = product(pe, ps[:, 4 * half + i, :], [w[:, k, i * P:(i + 1) * P] for w in (hi, lo)],
                                             [x[:, 4 + k, :] for x in xs], k == 0, k == 3, False)
                            mm.then_inc(W.used if i == 3 else mm_done.s, 1)

                @b.scalar
                def _(act):
                    for half, (dst, func) in enumerate(((val, ACT.Identity), (gat, ACT.Sigmoid))):
                        for i in range(4):
                            if i < 3:
                                act.wait_ge(mm_done.s, mm_done.at(3 * half + i + 1))
                            else:
                                act.wait_ge(W.used, w_glu + half + 1)
                            bias = col[:, C_GLU + 4 * half + i:C_GLU + 4 * half + i + 1]
                            act.activation(dst[:, i, :], ps[:, 4 * half + i, :], func, bias=bias).then_inc(glu_ready.s, 1)

                @b.vector
                def _(dve):
                    link = linker(dve, dve_link)
                    dve.wait_ge(W.used, w_glu + 2)
                    for i in range(4):
                        dve.wait_ge(glu_ready.s, glu_ready.at(4 + i + 1))
                        link(dve.tensor_tensor(val[:, i, :], val[:, i, :], gat[:, i, :], ALU.mult))
                        link(dve.tensor_tensor(val[:, i, :], val[:, i, :], gate_b[:, i, :], ALU.mult))
                        link(dve.tensor_copy(x_hi[:, 4 + i, :], val[:, i, :]))
                        dve.tensor_tensor(x_lo[:, 4 + i, :], val[:, i, :], x_hi[:, 4 + i, :].bitcast(F32), ALU.subtract)
            mm_done.passed(6)
            glu_ready.passed(8)
            W.at_use = w_glu + 2
        add_to_h(w_ev_out, xs, KD)

        with ExitStack() as c:
            st = lambda name, shape, dt=F32: c.enter_context(nc.sbuf_tensor(name, shape, dt))
            qk = st("od_qk", [P, 10, S])
            v = st("od_v", [P, T, 2 * CD])
            gate = st("od_gate", [P, 8, S])
            unseen = st("unseen", [P, T, S], BF16)
            with ExitStack() as c2:
                s2 = lambda name, shape, dt=F32: c2.enter_context(nc.sbuf_tensor(name, shape, dt))
                qi = s2("qi", [P, 4, S])
                ki = s2("ki", [P, S])
                wi = s2("wi", [P, T, IH])
                project([(w_od_q, CW, "turned", copy_to(lambda i: qk[:, i, :])),
                         (w_od_k, 256, "turned", copy_to(lambda i: qk[:, 8 + i, :])),
                         (w_od_v, 256, "tokens", tokens_to(v)),
                         (w_od_gate, CW, "turned", silu_to(lambda i: gate[:, i, :])),
                         (w_od_qi, IH * ID, "turned", copy_to(lambda i: qi[:, i, :])),
                         (w_od_ki, 128, "turned", copy_to(lambda i: ki[:, :])),
                         (w_od_wi, IH, "tokens", lambda act, tile, i, o: act.activation(wi[:, tile, :], o, ACT.Copy,
                                                                                     scale=(IH * ID) ** -0.5))],
                        Norm(h, T, C_NORM_G + 8, x_hi, x_lo, as_rows(qk), norm_stat), S)
                head_norm([(qk[:, i, :], C_OQ if i < 8 else C_OK) for i in range(10)], CD)

                seen = s2("seen", [P, 4, S])
                score = s2("score", [P, 2, S])
                top = s2("top", [P, 8])
                b = c2.enter_context(stage())
                dots_done, seen_ready, seen_used = sg["scores_done"], sg["a_ready"], sg["b_ready"]
                index_units = [(qb, i) for qb in range(1, T) for i in range(IH)]

                @b.sync
                def _(sp):
                    W.load(sp, W.at_use - 1)

                @b.gpsimd
                def _(pool):
                    W.split(pool, W.at_use)

                @b.tensor
                def _(pe):
                    for m, (qb, i) in enumerate(index_units):
                        if m >= 4:
                            pe.wait_ge(seen_ready.s, seen_ready.at(m - 3))
                        p0 = 64 * (i % 2)
                        pe.matmul(ps[:, m % 4, 0:(qb + 1) * P], qi[p0:p0 + 64, i // 2, qb * P:(qb + 1) * P],
                                  ki[p0:p0 + 64, 0:(qb + 1) * P], start=True, stop=True).then_inc(dots_done.s, 1)

                @b.scalar
                def _(act):
                    for m, (qb, i) in enumerate(index_units):
                        act.wait_ge(dots_done.s, dots_done.at(m + 1))
                        if m >= 4:
                            act.wait_ge(seen_used.s, seen_used.at(m - 3))
                        w = (qb + 1) * P
                        act.activation(seen[:, m % 4, 0:w], ps[:, m % 4, 0:w], ACT.Relu).then_inc(seen_ready.s, 1)

                @b.vector
                def _(dve):
                    link = linker(dve, dve_link)
                    for m, (qb, i) in enumerate(index_units):
                        w = (qb + 1) * P
                        dve.wait_ge(seen_ready.s, seen_ready.at(m + 1))
                        before = by_x(causal, qb, w) if i == 0 else score[:, (i - 1) % 2, 0:w]
                        dve.scalar_tensor_tensor(score[:, i % 2, 0:w], seen[:, m % 4, 0:w], wi[:, qb, i:i + 1], before,
                                                 ALU.mult, ALU.add).then_inc(seen_used.s, 1)
                        dve.wait_ge(seen_used.s, seen_used.at(m + 1))
                        if i == IH - 1:
                            work = score[:, 1, 0:w]
                            for _ in range(TOPK // 8):
                                link(dve.max(top[:, :], work))
                                link(dve.match_replace(out=work, in_to_replace=top[:, :], in_values=work, imm_value=-BIG))
                            link(dve.tensor_scalar(unseen[:, qb, 0:w], work, -1e35, NEG, ALU.is_gt, ALU.mult))
            n = len(index_units)
            for s_ in (dots_done, seen_ready, seen_used):
                s_.passed(n)

            with ExitStack() as c2:
                far = c2.enter_context(nc.sbuf_tensor("head_bias", [P, 2, S], F32))
                heads = [(qk[:, i, :], qk[:, 8 + i // 4, :], (lambda kv: lambda kb: v[:, kb, kv * CD:(kv + 1) * CD])(i // 4))
                         for i in range(CH)]

                def load_bias(sp, hd):
                    sp.dma_start(far[:, hd % 2, :], bass.AP(bias_rows, hd * P * BX + 127, [[BX - 1, P], [1, S]])).then_inc(bias_in[hd % 2].s, 16)

                def add_unseen(pe, hd, qb, o):
                    return pe.matmul(o, ident_b[:, :], unseen[:, qb, 0:(qb + 1) * P], start=False, stop=True)

                attention(heads, causal_keys, CD ** -0.5, split_out(0, gate, 1),
                          bias_of=lambda hd, qb, w: by_x(far[:, hd % 2, :], qb, w), add=add_unseen, adds=lambda qb: qb > 0,
                          n_pair=1, bias_load=load_bias)
        add_to_h(w_od_out, xs, KD)

        for layer in range(2):
            with ExitStack() as c:
                st = lambda name, shape, dt=F32: c.enter_context(nc.sbuf_tensor(f"{name}{layer}", shape, dt))
                km = st("km", [P, 2, MT])
                vm = st("vm", [P, 2, MH * FD])
                with ExitStack() as c2:
                    mem = c2.enter_context(nc.sbuf_tensor(f"mem{layer}", [P, 2, D], F32))
                    m_hi = c2.enter_context(nc.sbuf_tensor(f"m_hi{layer}", [P, KD, MT], F32R))
                    m_lo = c2.enter_context(nc.sbuf_tensor(f"m_lo{layer}", [P, KD, MT], F32R))
                    with ExitStack() as c3:
                        b = c3.enter_context(stage())

                        @b.sync
                        def _(sp):
                            sp.dma_start(mem[:, :, :], t["mem_2"][0].rearrange("(t p) d -> p t d", p=P)).then_inc(loads_in.s, 16)
                            sp.wait_ge(loads_in.s, loads_in.at(16))
                    loads_in.passed(16)
                    project([(w_mem_k[layer], 256, "turned", copy_to(lambda i: km[:, i, :])),
                             (w_mem_v[layer], 256, "tokens", tokens_to(vm))],
                            Norm(mem, 2, C_MEM + 8 * layer, m_hi, m_lo, mem, norm_stat), MT)
                q = st("q", [P, 6, S])
                k = st("k", [P, 6, S])
                v = st("v", [P, T, FH * FD])
                qm = st("qm", [P, 2, S])
                jobs = [(w_q[layer], FW, "turned", copy_to(lambda i: q[:, i, :])),
                        (w_k[layer], FW, "turned", copy_to(lambda i: k[:, i, :])),
                        (w_v[layer], FW, "tokens", tokens_to(v))]
                if layer == 0:
                    fl = st("forget_logit", [P, T, FH])
                    jobs.append((w_forget, FH, "tokens", lambda act, tile, i, o: act.activation(fl[:, tile, :], o, ACT.Copy)))
                jobs.append((w_qm[layer], 256, "turned", copy_to(lambda i: qm[:, i, :])))
                with ExitStack() as c2:
                    normed = c2.enter_context(nc.sbuf_tensor(f"normed{layer}", [P, T, D], F32))
                    project(jobs, Norm(h, T, C_MIX + 8 * layer, x_hi, x_lo, normed, norm_stat), S)

                if layer == 0:
                    cum = st("cum", [FH, S])
                    with ExitStack() as c2:
                        s2 = lambda name, shape, dt=F32: c2.enter_context(nc.sbuf_tensor(name, shape, dt))
                        fz, fa, b_f = s2("fz", [FH, S]), s2("fa", [FH, S]), s2("b_f", [FH, 1])
                        b = c2.enter_context(stage())
                        bf_in, z_ready, soft_ready = sg["b_ready"], sg["a_ready"], sg["c_ready"]

                        @b.sync
                        def _(sp):
                            W.load(sp, W.at_use - 1)

                        @b.gpsimd
                        def _(pool):
                            W.split(pool, W.at_use)

                        @b.tensor
                        def _(pe):
                            for i in range(T):
                                mm = pe.transpose(ps[0:FH, 0, i * P:(i + 1) * P], fl[:, i, :], ident[:, :])
                            mm.then_inc(mm_done.s, 1)

                        @b.scalar
                        def _(act):
                            act.dma_start(b_f[:, :], t["b_forget_2"].rearrange("a h -> h a")).then_inc(bf_in.s, 16)
                            link = linker(act, act_link)
                            act.wait_ge(z_ready.s, z_ready.at(1))
                            link(act.activation(fa[:, :], fz[:, :], ACT.Abs))
                            link(act.activation(fa[:, :], fa[:, :], ACT.Exp, scale=-1.0))
                            act.activation(fa[:, :], fa[:, :], ACT.Ln, bias=1.0).then_inc(soft_ready.s, 1)

                        @b.vector
                        def _(dve):
                            link = linker(dve, dve_link)
                            dve.wait_ge(mm_done.s, mm_done.at(1))
                            dve.wait_ge(bf_in.s, bf_in.at(16))
                            dve.tensor_scalar(fz[:, :], ps[0:FH, 0, :], b_f[:, 0:1], None, ALU.add).then_inc(z_ready.s, 1)
                            dve.wait_ge(soft_ready.s, soft_ready.at(1))
                            link(dve.scalar_tensor_tensor(fz[:, :], fz[:, :], 0.0, fa[:, :], ALU.min, ALU.subtract))
                            link(dve.memset(fa[:, :], 1.0))
                            link(dve.tensor_tensor_scan(cum[:, :], fa[:, :], fz[:, :], 0.0, ALU.mult, ALU.add))
                            dve.tensor_scalar(cum[:, :], cum[:, :], -FD ** 0.5, None, ALU.mult)
                    for s_, n in ((bf_in, 16), (z_ready, 1), (soft_ready, 1), (mm_done, 1)):
                        s_.passed(n)
                else:
                    with ExitStack() as c2:
                        s2 = lambda name, shape, dt=F32: c2.enter_context(nc.sbuf_tensor(name, shape, dt))
                        cos, sin, swap = s2("rope_cos", [P, S]), s2("rope_sin", [P, S]), s2("rope_swap", [P, P])
                        tmp = s2("rope_tmp", [P, 2, S])
                        b = c2.enter_context(stage())
                        rope_in, rot_used = sg["b_ready"], sg["a_ready"]
                        tiles_ = [q[:, i, :] for i in range(6)] + [k[:, i, :] for i in range(6)]

                        @b.sync
                        def _(sp):
                            for dst, src in ((cos, "c_rope_cos"), (sin, "c_rope_sin"), (swap, "c_rope_swap")):
                                sp.dma_start(dst[:, :], t[src]).then_inc(rope_in.s, 16)
                            W.load(sp, W.at_use - 1)

                        @b.gpsimd
                        def _(pool):
                            W.split(pool, W.at_use)

                        @b.tensor
                        def _(pe):
                            pe.wait_ge(rope_in.s, rope_in.at(48))
                            for i, x in enumerate(tiles_):
                                if i >= 8:
                                    pe.wait_ge(rot_used.s, rot_used.at(i - 7))
                                pe.matmul(ps[:, i % 8, :], swap[:, :], x, start=True, stop=True).then_inc(mm_done.s, 1)

                        @b.vector
                        def _(dve):
                            link = linker(dve, dve_link)
                            dve.wait_ge(rope_in.s, rope_in.at(48))
                            for i, x in enumerate(tiles_):
                                dve.wait_ge(mm_done.s, mm_done.at(i + 1))
                                dve.tensor_tensor(tmp[:, i % 2, :], ps[:, i % 8, :], sin[:, :], ALU.mult).then_inc(rot_used.s, 1)
                                link(dve.tensor_tensor(x, x, cos[:, :], ALU.mult))
                                link(dve.tensor_tensor(x, x, tmp[:, i % 2, :], ALU.add))
                    rope_in.passed(48)
                    rot_used.passed(12)
                    mm_done.passed(12)

                def head_list(q_, k_, v_, n, d=FD):
                    return [(q_[64 * (i % 2):64 * (i % 2) + 64, i // 2, :], k_[64 * (i % 2):64 * (i % 2) + 64, i // 2, :],
                             (lambda i: lambda kb: v_[:, kb, i * d:(i + 1) * d])(i)) for i in range(n)]

                with ExitStack() as c2:
                    mask = c2.enter_context(nc.sbuf_tensor(f"mask{layer}", [P, S], F32))
                    with ExitStack() as c3:
                        b = c3.enter_context(stage())

                        @b.sync
                        def _(sp):
                            if layer == 1:
                                sp.dma_start(mask[:, :], t["c_dilated"]).then_inc(loads_in.s, 16)
                                sp.wait_ge(loads_in.s, loads_in.at(16))

                        @b.vector
                        def _(dve):
                            if layer == 0:
                                dve.memset(mask[:, :], 0.0)
                    if layer == 1:
                        loads_in.passed(16)
                    if layer == 0:
                        def add_decay(pe, hd, qb, o):
                            return pe.matmul(o, sel128[0:FH, hd * P:(hd + 1) * P], cum[:, 0:(qb + 1) * P], start=False, stop=True)
                        attention(head_list(q, k, v, FH), causal_keys, FD ** -0.5, split_out(0),
                                  bias_of=lambda hd, qb, w: by_x(causal, qb, w), add=add_decay)
                    else:
                        attention(head_list(q, k, v, FH), causal_keys, FD ** -0.5, split_out(0),
                                  bias_of=lambda hd, qb, w: by_x(mask, qb, w))
                    with ExitStack() as c3:
                        zero = c3.enter_context(nc.sbuf_tensor(f"zero{layer}", [P, MT], F32))
                        with ExitStack() as c4:
                            b = c4.enter_context(stage())

                            @b.vector
                            def _(dve):
                                dve.memset(zero[:, :], 0.0)
                        attention(head_list(qm, km, vm, MH), lambda qb: (0, 2), FD ** -0.5, split_out(6),
                                  bias_of=lambda hd, qb, w: zero[:, 0:w])
            add_to_h(w_out[layer], xs, KD)

            with ExitStack() as c:
                st = lambda name, shape, dt=F32: c.enter_context(nc.sbuf_tensor(f"{name}{layer}", shape, dt))
                a_hi, a_lo = st("a_hi", [P, HALF, S], F32R), st("a_lo", [P, HALF, S], F32R)
                cv = st("cv", [P, 4, 2, S])
                norm = Norm(h, T, C_FFN + 8 * layer, x_hi, x_lo, cv[:, :, :, :].rearrange("p b v s -> p b (v s)"), norm_stat)
                base_ready, conv_done, silu_done, joined = sg["a_ready"], sg["b_ready"], sg["c_ready"], sg["d_ready"]
                banks_read, added = sg["bank_free"], sg["added"]
                units = [(part, i) for part in range(2) for i in range(HALF)]
                groups = [(k, min(4, HALF - k)) for k in range(0, HALF, 4)]
                tap = lambda j, half, u: col[:, C_CONV + 176 * layer + 44 * j + FC * half + u:][:, 0:1]
                up_slot = lambda u: w_up[layer, u // HALF] + u % HALF
                down_bank = lambda half, tile: (6 + 4 * half + tile) % 8
                up_bank = lambda i, half: (2 * i + half) % 8
                b = c.enter_context(stage())

                @b.sync
                def _(sp):
                    W.load(sp, w_down[layer, 1] + 2 * len(groups) - 1)

                @b.gpsimd
                def _(pool):
                    W.split(pool, w_down[layer, 1] + 2 * len(groups))

                @b.tensor
                def _(pe):
                    norm.tensor(pe)
                    for part in range(2):
                        for i in range(HALF):
                            u = part * HALF + i
                            pe.wait_ge(W.split_done, up_slot(u) + 1)
                            hi, lo = W.parts(up_slot(u))
                            if i >= 4:
                                pe.wait_ge(banks_read.s, banks_read.at(u - 3))
                            elif part == 1:
                                pe.wait_ge(added.s, added.at(min(8, 4 + 2 * i)))
                            for half in range(2):
                                for kt in range(KD):
                                    if u == 0 and half == 0:
                                        norm.wait_x(pe, kt)
                                    mm = product(pe, ps[:, up_bank(i, half), :], [w[:, kt, half * P:half * P + P] for w in (hi, lo)],
                                                 [x[:, kt, :] for x in xs], kt == 0, kt == KD - 1, False)
                            mm.then_inc(W.used, 1)
                        for half in range(2):
                            pe.wait_ge(banks_read.s, banks_read.at(HALF * part + (9 if half == 0 else HALF)))
                            for g, (k0, kk) in enumerate(groups):
                                slot = w_down[layer, part] + half * len(groups) + g
                                pe.wait_ge(W.split_done, slot + 1)
                                pe.wait_ge(joined.s, joined.at(HALF * part + k0 + kk))
                                hi, lo = W.parts(slot)
                                for tile in range(T):
                                    for kt in range(kk):
                                        x = [v[:, k0 + kt, tile * P:(tile + 1) * P] for v in (a_hi, a_lo)]
                                        mm = product(pe, ps[:, down_bank(half, tile), :], [v[:, kt, :] for v in (hi, lo)], x,
                                                     k0 + kt == 0, k0 + kt == HALF - 1, True)
                                    if tile == T - 1:
                                        mm.then_inc(W.used, 1)
                                    elif g == len(groups) - 1:
                                        mm.then_inc(mm_done.s, 1)

                @b.scalar
                def _(act):
                    norm.scalar(act)

                    def base(u):
                        act.wait_ge(W.used, up_slot(u) + 1)
                        if u >= 4:
                            act.wait_ge(joined.s, joined.at(u - 3))
                        for half in range(2):
                            act.activation(cv[:, u % 4, half, :], ps[:, up_bank(u % HALF, half), :], ACT.Identity,
                                           scale=tap(2, half, u), bias=tap(3, half, u)).then_inc(base_ready.s, 1)

                    def gate_silu(u):
                        act.wait_ge(conv_done.s, conv_done.at(u + 1))
                        act.activation(cv[:, u % 4, 1, :], cv[:, u % 4, 1, :], ACT.Silu).then_inc(silu_done.s, 1)

                    for part in range(2):
                        base(part * HALF)
                        for u in range(part * HALF, (part + 1) * HALF):
                            if u + 1 < (part + 1) * HALF:
                                base(u + 1)
                            gate_silu(u)

                @b.vector
                def _(dve):
                    norm.vector(dve)
                    link = linker(dve, dve_link)

                    def conv(u):
                        dve.wait_ge(base_ready.s, base_ready.at(2 * u + 2))
                        for back, j in ((1, 1), (2, 0)):
                            for half in range(2):
                                o = cv[:, u % 4, half, back:S]
                                ins = dve.scalar_tensor_tensor(o, ps[:, up_bank(u % HALF, half), 0:S - back], tap(j, half, u), o,
                                                               ALU.mult, ALU.add)
                                if (back, half) != (2, 1):
                                    link(ins)
                        ins.then_inc(banks_read.s, 1)
                        dve.wait_ge(banks_read.s, banks_read.at(u + 1))
                        dve.sem_inc(conv_done.s, 1)

                    def join(u):
                        part, i = units[u]
                        dve.wait_ge(silu_done.s, silu_done.at(u + 1))
                        if u == HALF:
                            dve.wait_ge(W.used, w_down[layer, 0] + 2 * len(groups))
                        a = cv[:, u % 4, 0, :]
                        link(dve.tensor_tensor(a, a, cv[:, u % 4, 1, :], ALU.mult))
                        link(dve.tensor_copy(a_hi[:, i, :], a))
                        dve.tensor_tensor(a_lo[:, i, :], a, a_hi[:, i, :].bitcast(F32), ALU.subtract).then_inc(joined.s, 1)

                    for part in range(2):
                        conv(part * HALF)
                        for u in range(part * HALF, (part + 1) * HALF):
                            if u + 1 < (part + 1) * HALF:
                                conv(u + 1)
                            join(u)
                        for half in range(2):
                            for tile in range(T):
                                if tile < T - 1:
                                    dve.wait_ge(mm_done.s, mm_done.at(6 * part + 3 * half + tile + 1))
                                else:
                                    dve.wait_ge(W.used, w_down[layer, part] + (half + 1) * len(groups))
                                hv = h[:, tile, half * 512:half * 512 + 512]
                                dve.tensor_tensor(hv, hv, ps[:, down_bank(half, tile), :], ALU.add).then_inc(added.s, 1)

                norm.passed()
                n = len(units)
                for s_, k_ in ((banks_read, n), (base_ready, 2 * n), (conv_done, n), (silu_done, n), (joined, n),
                               (added, 16), (mm_done, 12)):
                    s_.passed(k_)
                W.at_use = w_down[layer, 1] + 2 * len(groups)

        with ExitStack() as c:
            st = lambda name, shape, dt=F32: c.enter_context(nc.sbuf_tensor(name, shape, dt))
            gain = st("final_gain", [P, D])
            res = st("res", [P, T, D])
            stat = st("final_stat", [P, 3 * T])
            b = c.enter_context(stage())
            gain_in, root_ready, res_ready, stored = sg["b_ready"], sg["a_ready"], sg["c_ready"], sg["stored"]

            @b.sync
            def _(sp):
                sp.dma_start(gain[:, :], t["norm_final_2"].rearrange("(a d) -> a d", a=1).to_broadcast([P, D])).then_inc(gain_in.s, 16)
                for i in range(T):
                    sp.wait_ge(res_ready.s, res_ready.at(i + 1))
                    sp.dma_start(out[0, i * P:(i + 1) * P, :], res[:, i, :]).then_inc(stored.s, 16)
                sp.wait_ge(stored.s, stored.at(16 * T))

            @b.scalar
            def _(act):
                link = linker(act, act_link)
                for i in range(T):
                    link(act.activation(res[:, i, :], h[:, i, :], ACT.Square, accum_out=stat[:, i:i + 1]))
                act.activation(stat[:, T:2 * T], stat[:, 0:T], ACT.Sqrt, scale=1.0 / D, bias=eps_col[:, 0:1]).then_inc(root_ready.s, 1)

            @b.vector
            def _(dve):
                link = linker(dve, dve_link)
                dve.wait_ge(gain_in.s, gain_in.at(16))
                dve.wait_ge(root_ready.s, root_ready.at(1))
                link(dve.reciprocal(stat[:, 2 * T:3 * T], stat[:, T:2 * T]))
                for i in range(T):
                    dve.scalar_tensor_tensor(res[:, i, :], h[:, i, :], stat[:, 2 * T + i:2 * T + i + 1], gain[:, :],
                                             ALU.mult, ALU.mult).then_inc(res_ready.s, 1)


def constants():
    f = np.float32
    p, x = np.arange(P)[:, None], np.arange(S)[None, :]
    dist = p - x + 384
    causal = np.where(dist >= 0, f(0), f(NEG)).astype(f)
    n = np.maximum(511 - np.arange(BX), 0)
    nf = np.maximum(n, 1).astype(f)
    large = NB // 2 + (np.log(nf / f(NB // 2)) / f(math.log(1024 / (NB // 2))) * f(NB - NB // 2)).astype(np.int32)
    bucket_of = np.where(n < NB // 2, n, np.minimum(large, NB - 1))
    bucket = (bucket_of[None, :] == np.arange(NB)[:, None]).astype(f)
    d = 511 - np.arange(BX)
    neg = np.zeros((AH, 2, BX), f)
    neg[:, 0, :] = np.where(d < 0, f(NEG), f(0))
    neg[:, 1, :] = np.where((d < 0) | (d >= P), f(NEG), f(0))
    count = (dist >= 0) * ((dist <= 128).astype(int) + (dist % 4 == 0) + (dist % 16 == 0))
    dilated = np.where(count > 0, np.log(np.maximum(count, 1)) * math.sqrt(FD), NEG).astype(f)
    head_sum = np.zeros((P, 2, 40), f)
    head_sum[:64, 0, 20] = head_sum[64:, 0, 21] = 1 / 64
    head_sum[:, 1, 20] = 1 / 128
    sel64 = np.zeros((12, 6 * P), f)
    sel128 = np.zeros((12, 12 * P), f)
    for r in range(12):
        sel64[r, 64 * r:64 * r + 64] = 1
        sel128[r, P * r:P * r + P] = 1
    inv = f(1) / (f(10000.0) ** (np.arange(0, 64, 2, dtype=f) / f(64)))
    ang = np.arange(S, dtype=f)[:, None] * inv[None, :]
    cos, sin = (np.tile(g(ang).astype(f).T, (4, 1)) for g in (np.cos, np.sin))
    swap = np.zeros((P, P), f)
    for m in range(P):
        swap[m + 32 if m % 64 < 32 else m - 32, m] = -1 if m % 64 < 32 else 1
    time = np.tile(np.arange(S, dtype=f)[None, :], (P, 1))
    return {"c_causal": causal, "c_bucket": bucket, "c_neg_rows": neg, "c_dilated": dilated, "c_head_sum": head_sum,
            "c_sel64": sel64, "c_sel128": sel128, "c_rope_cos": np.ascontiguousarray(cos), "c_rope_sin": np.ascontiguousarray(sin),
            "c_rope_swap": swap, "c_time": time, "c_ident": np.eye(P, dtype=f)}


def kernel(**inputs):
    import concourse.bacc as bacc
    from concourse.bass_utils import run_bass_kernel_spmd

    nc = bacc.Bacc("TRN2", target_bir_lowering=False, num_devices=1)
    arrays = {name: np.ascontiguousarray(a) for name, a in inputs.items()}
    arrays.update(constants())
    views = {name: nc.dram_tensor(name, a.shape, mybir.dt.from_np(a.dtype), kind="ExternalInput").ap()
             for name, a in arrays.items()}
    out = nc.dram_tensor("y", (1, S, D), F32, kind="ExternalOutput").ap()
    block_kernel(nc, views, out)
    result = run_bass_kernel_spmd(nc, [arrays], core_ids=[0])
    return result.results[0]["y"]
```

```python
import math
from contextlib import ExitStack

import numpy as np

import concourse.bass as bass
from concourse import mybir

F32 = mybir.dt.float32
F32R = mybir.dt.float32r
BF16 = mybir.dt.bfloat16
I32 = mybir.dt.int32
ALU = mybir.AluOpType
ACT = mybir.ActivationFunctionType

P = 128
S = 512
T = S // P
D = 1024
KD = D // P
EPS = 1e-6
NEG = -1e30
BIG = 3e38
MAGIC = 12582912.0

AH, AD, AKV = 8, 64, 2
CH, CD, CKV = 8, 128, 2
IH, ID = 8, 64
TOPK = 128
G, GH, GP = 32, 16, 64
ST = G * GP // P
FH, FD = 12, 64
LO = 96
MH, MT = 4, 256
DFF = 2816
FC = DFF // P
NB = 32
BX = 640

C_NORM_G, C_MIX, C_MEM, C_FFN, C_GLU, C_SKIP, C_EQ, C_EK, C_OQ, C_OK = 0, 16, 32, 48, 64, 72, 76, 77, 78, 79
C_ROWS = 80
C_CONV = C_ROWS
C_MAG = C_CONV + 2 * 176
C_TURN, C_FRE, C_FIM = C_MAG + ST, C_MAG + 2 * ST, C_MAG + 3 * ST
C_COLS = C_MAG + 4 * ST

RAW, SPLIT, SLOT = 2, 3, 2048


class Signal:

    def __init__(self, ctx, nc, name):
        self.s = ctx.enter_context(nc.semaphore(name))
        self.base = 0

    def at(self, n):
        return self.base + n

    def passed(self, n):
        self.base += n


class Weights:

    def __init__(self, ctx, nc):
        self.slots = []
        self.raw = ctx.enter_context(nc.sbuf_tensor("w_raw", [P, RAW, SLOT], F32))
        self.hi = ctx.enter_context(nc.sbuf_tensor("w_hi", [P, SPLIT, SLOT], F32R))
        self.lo = ctx.enter_context(nc.sbuf_tensor("w_lo", [P, SPLIT, SLOT], F32R))
        self.loaded = [ctx.enter_context(nc.semaphore(f"w_loaded{i}")) for i in range(RAW)]
        self.hi_done = ctx.enter_context(nc.semaphore("w_hi_done"))
        self.split_done = ctx.enter_context(nc.semaphore("w_split_done"))
        self.used = ctx.enter_context(nc.semaphore("w_used"))
        self.sent = 0
        self.cut = 0
        self.arrived = [0] * RAW
        self.need = []

    def add(self, kk, nn, pieces):
        self.slots.append((kk, nn, pieces))
        r = (len(self.slots) - 1) % RAW
        self.arrived[r] += 16 * len(pieces)
        self.need.append(self.arrived[r])

    def load(self, sp, until):
        for n in range(self.sent, min(len(self.slots), until + RAW + SPLIT)):
            kk, nn, pieces = self.slots[n]
            if n >= RAW:
                sp.wait_ge(self.split_done, n - RAW + 1)
            dst = self.raw[:, n % RAW, 0:kk * nn].rearrange("p (k n) -> p k n", k=kk)
            for c, src in pieces:
                sp.dma_start(dst[:, :, c:c + src.shape[2]], src).then_inc(self.loaded[n % RAW], 16)
            self.sent = n + 1

    def split(self, pool, until):
        for n in range(self.cut, min(len(self.slots), until + SPLIT)):
            kk, nn, _ = self.slots[n]
            size = kk * nn
            raw, hi, lo = self.raw[:, n % RAW, 0:size], self.hi[:, n % SPLIT, 0:size], self.lo[:, n % SPLIT, 0:size]
            pool.wait_ge(self.loaded[n % RAW], self.need[n])
            if n >= SPLIT:
                pool.wait_ge(self.used, n - SPLIT + 1)
            pool.tensor_scalar(hi, raw, 1.0, 1.0, ALU.mult, ALU.mult).then_inc(self.hi_done, 1)
            pool.wait_ge(self.hi_done, n + 1)
            pool.tensor_tensor(lo, raw, hi.bitcast(F32), ALU.subtract).then_inc(self.split_done, 1)
            self.cut = n + 1

    def parts(self, n):
        kk, nn, _ = self.slots[n]
        view = lambda t: t[:, n % SPLIT, 0:kk * nn].rearrange("p (k n) -> p k n", k=kk)
        return view(self.hi), view(self.lo)


def block_kernel(nc, t, out):
    ctx = ExitStack()
    with ctx:
        sb = lambda name, shape, dt=F32: ctx.enter_context(nc.sbuf_tensor(name, shape, dt))
        sig = lambda name: Signal(ctx, nc, name)
        W = Weights(ctx, nc)

        def tiles(w, k0, kk):
            return w[k0 * P:(k0 + kk) * P, :].rearrange("(k p) n -> p k n", p=P)

        def wide(w, c0, width, kd=KD):
            first = len(W.slots)
            for c in range(c0, c0 + width, 256):
                n = min(256, c0 + width - c)
                W.add(kd, n, [(0, tiles(w, 0, kd)[:, :, c:c + n])])
            return first

        def deep(w, k_first, k_tiles):
            first = len(W.slots)
            for half in range(2):
                for k in range(k_first, k_first + k_tiles, 4):
                    kk = min(4, k_first + k_tiles - k)
                    W.add(kk, 512, [(0, tiles(w, k, kk)[:, :, half * 512:half * 512 + 512])])
            return first

        ev, od, fox, dil = t["ev_w_in"][0], t["od_w_in"][0], t["w_in_fox_2"][0], t["w_in_dil_2"][0]
        AW, CW, FW = AH * AD, CH * CD, FH * FD
        w_ev_q = wide(ev, 0, AW)
        w_ev_k = len(W.slots)
        W.add(KD, 4 * AD, [(64 * i, tiles(ev, 0, KD)[:, :, AW + 64 * (i // 2):AW + 64 * (i // 2) + 64]) for i in range(4)])
        w_ev_v = wide(ev, AW + 128, 128)
        w_ev_rest = wide(ev, AW + 256, 3 * 512)
        w_glu = len(W.slots)
        for half in range(2):
            W.add(4, 512, [(0, tiles(t["ev_glu_w"][0], 0, 4)[:, :, half * 512:half * 512 + 512])])
        w_ev_out = deep(t["ev_w_out"][0], 0, KD)
        w_od_qi = wide(od, 2 * CW + 512, IH * ID)
        w_od_ki = len(W.slots)
        ki0 = 2 * CW + 512 + IH * ID
        W.add(KD, 256, [(64 * i, tiles(od, 0, KD)[:, :, ki0:ki0 + 64]) for i in range(2)]
              + [(P, tiles(od, 0, KD)[:, :, ki0 + 64 + IH - P:ki0 + 64 + IH])])
        w_od_q = wide(od, 0, CW)
        w_od_k = wide(od, CW, 256)
        w_od_v = wide(od, CW + 256, 256)
        w_od_gate = wide(od, CW + 512, CW)
        w_od_out = deep(t["od_w_out"][0], 0, KD)
        w_mem_k, w_mem_v, w_q, w_k, w_v, w_qm, w_out = ([0, 0] for _ in range(7))
        HALF = FC // 2
        w_up, w_down = {}, {}
        for layer in range(2):
            w_mem_k[layer] = wide(t["w_mem_kv_2"][layer], 0, 256)
            w_mem_v[layer] = wide(t["w_mem_kv_2"][layer], 256, 256)
            w_in = (fox, dil)[layer]
            if layer == 0:
                w_forget = wide(w_in, 3 * FW, P)
            w_q[layer] = wide(w_in, 0, FW)
            w_k[layer] = wide(w_in, FW, FW)
            w_v[layer] = wide(w_in, 2 * FW, FW)
            w_qm[layer] = wide(w_in, 3 * FW + (FH if layer == 0 else 0), 256)
            w_out[layer] = deep(t["w_out_2"][layer], 0, KD)
            for part in range(2):
                first = len(W.slots)
                for i in range(part * HALF, (part + 1) * HALF):
                    up = tiles(t["w_up_2"][layer], 0, KD)
                    W.add(KD, 256, [(0, up[:, :, i * P:(i + 1) * P]), (P, up[:, :, DFF + i * P:DFF + (i + 1) * P])])
                w_up[layer, part] = first
                w_down[layer, part] = deep(t["w_down_2"][layer], part * HALF, HALF)

        h = sb("h", [P, T, D])
        x_hi = sb("x_hi", [P, KD, S], F32R)
        x_lo = sb("x_lo", [P, KD, S], F32R)
        col = sb("col", [P, C_COLS])
        ident = sb("ident", [P, P])
        ident_b = sb("ident_b", [P, P], BF16)
        causal = sb("causal", [P, S])
        head_sum = sb("head_sum", [P, 2, 40])
        eps_col = sb("eps_col", [P, 1])
        pih_col = sb("pih_col", [P, 1])
        norm_stat = sb("norm_stat", [P, 3 * T])
        neg_sink = sb("neg_sink", [P, AH])
        ssm_bt = sb("ssm_bt", [P, 2, 4, P])
        ssm_ct = sb("ssm_ct", [P, 3, 4, P])
        ps = ctx.enter_context(nc.psum_tensor("ps", [P, 8, 512], F32))
        bias_rows = nc.dram_tensor("bias_rows", [2, AH, P, BX], F32, kind="Internal")

        dve_link, act_link = sig("dve_link"), sig("act_link")
        names = ("mm_done", "bank_free", "loads_in", "a_ready", "b_ready", "c_ready", "d_ready", "e_ready",
                 "scores_done", "logits_ready", "probs_ready", "probs_scaled", "turned", "turned_copied",
                 "pv_done", "out_free", "bias_in", "bias_in2", "dt_in", "stored",
                 "n_root", "n_normed", "n_hi", "n_turned", "n_x", "n_in0", "n_in1", "added", "h_squared", "h_summed", "h_root", "h_inv",
                 "h_spread", "h_used")
        sg = {n: sig(n) for n in names}
        mm_done, bank_free, loads_in = sg["mm_done"], sg["bank_free"], sg["loads_in"]
        bias_in = (sg["bias_in"], sg["bias_in2"])

        def linker(eng, link):
            def run(ins):
                link.passed(1)
                ins.then_inc(link.s, 1)
                eng.wait_ge(link.s, link.base)
            return run

        def stage():
            return nc.Block()

        def product(pe, o, w, x, start, stop, token_major):
            for i, (a, b) in enumerate(((w[0], x[0]), (w[0], x[1]), (w[1], x[0]))):
                l, r = (b, a) if token_major else (a, b)
                mm = pe.matmul(o, l, r, start=start and i == 0, stop=stop and i == 2)
            return mm

        with ExitStack() as c:
            st = lambda name, shape, dt=F32: c.enter_context(nc.sbuf_tensor(name, shape, dt))
            rows = st("rows", [C_ROWS, P])
            conv_rows = st("conv_rows", [88, 4, P])
            bucket = st("bucket", [NB, BX])
            rel = st("rel", [NB, AH])
            neg_rows = st("neg_rows", [AH, 2, BX])
            brow = st("brow", [AH, 2, BX])
            a_rows = st("a_rows", [16, 2, P])
            dtl = st("dtl", [16, 2])
            R = st("R", [16, 26, P])
            RI = st("RI", [16, P], I32)
            par = st("par", [16, 4, P])
            b_in = st("b_in", [P, 2, ST, GH])
            bb = st("bb", [P, 2, ST, GH])
            b_tmp = st("b_tmp", [P, ST, GH])
            b_pre = st("b_pre", [P, 2, 4, P])
            c_pre = st("c_pre", [P, 2, 4, P])
            sink_b = st("sink_b", [P, AH])
            b = c.enter_context(stage())
            zeroed, par_in, brow_ready, rows_stored = sg["a_ready"], sg["b_ready"], sg["c_ready"], sg["d_ready"]
            turned_in, par_done, dt_in, bb_ready = sg["turned"], sg["probs_ready"], sg["dt_in"], sg["e_ready"]
            a_in, c_in, rel_in, b_in_ready = sg["n_root"], sg["n_normed"], sg["n_hi"], sg["n_x"]
            bias_made = sg["n_turned"]
            n_loads = {}

            @b.sync
            def _(sp):
                sp.dma_start(dtl[:, :], t["ev_ssm_log_dt"][0].rearrange("(j g) -> j g", g=2)).then_inc(a_in.s, 16)
                sp.dma_start(a_rows[:, 0, :], t["ev_ssm_a_re"][0].rearrange("(j g) p -> j (g p)", g=2)).then_inc(a_in.s, 16)
                sp.dma_start(a_rows[:, 1, :], t["ev_ssm_a_im"][0].rearrange("(j g) p -> j (g p)", g=2)).then_inc(a_in.s, 16)
                sp.wait_ge(zeroed.s, zeroed.at(1))
                for part, name in enumerate(("ev_ssm_c_re", "ev_ssm_c_im")):
                    for g in range(8):
                        src = t[name][0].rearrange("(c g) h p -> g h c p", g=8)[g]
                        sp.dma_start(c_pre[16 * g:16 * g + 16, part, :, 64 * (g % 2):64 * (g % 2) + 64], src).then_inc(c_in.s, 16)
                sp.dma_start(h[:, :, :], t["x"][0].rearrange("(t p) d -> p t d", p=P)).then_inc(loads_in.s, 16)
                W.load(sp, -SPLIT)
                sp.wait_ge(brow_ready.s, brow_ready.at(1))
                for a in range(2):
                    sp.dma_start(bias_rows[a, :, :, :], brow[:, a, :].unsqueeze(1).to_broadcast([AH, P, BX])).then_inc(rows_stored.s, 16)
                sp.wait_ge(rows_stored.s, rows_stored.at(32))
                sp.wait_ge(loads_in.s, loads_in.at(16))

            @b.gpsimd
            def _(pool):
                pool.memset(c_pre[:, :, :, :], 0.0).then_inc(zeroed.s, 1)

            @b.scalar
            def _(act):
                def load(dst, src, arrival=par_in):
                    act.dma_start(dst, src).then_inc(arrival.s, 16)
                    n_loads[arrival] = n_loads.get(arrival, 0) + 16
                load(rel[:, :], t["rel_bias"], rel_in)
                load(bucket[:, :], t["c_bucket"], rel_in)
                load(neg_rows[:, :, :], t["c_neg_rows"], rel_in)
                load(b_in[:, 0, :, :], t["ev_ssm_b_re"][0].rearrange("(j g) p h -> (g p) j h", g=2), b_in_ready)
                load(b_in[:, 1, :, :], t["ev_ssm_b_im"][0].rearrange("(j g) p h -> (g p) j h", g=2), b_in_ready)
                load(sink_b[:, :], t["ev_sinks"].to_broadcast([P, AH]), b_in_ready)
                load(ident[:, :], t["c_ident"])
                for name, c0 in (("norm_g", C_NORM_G), ("norm_mix_2", C_MIX), ("norm_mem_2", C_MEM), ("norm_ffn_2", C_FFN)):
                    load(rows[c0:c0 + 16, :], t[name].rearrange("l (k p) -> (l k) p", p=P))
                for l in range(2):
                    load(conv_rows[:, 2 * l, :], t["conv_w_2"][l, 0:2].rearrange("j (k p) -> (j k) p", p=P))
                    load(conv_rows[0:44, 2 * l + 1, :], t["conv_w_2"][l, 2].rearrange("(k p) -> k p", p=P))
                    load(conv_rows[44:88, 2 * l + 1, :], t["conv_b_2"][l].rearrange("(k p) -> k p", p=P))
                load(rows[C_GLU:C_GLU + 8, :], t["ev_glu_b"][0].rearrange("(k p) -> k p", p=P))
                load(rows[C_SKIP:C_SKIP + 4, :], t["ev_ssm_d"][0].rearrange("(k g) h -> k (g h)", k=4))
                for c0, name in ((C_EQ, "ev_q_norm_g"), (C_EK, "ev_k_norm_g")):
                    for i in range(2):
                        load(rows[c0:c0 + 1, 64 * i:64 * i + 64], t[name])
                load(rows[C_OQ:C_OQ + 1, :], t["od_q_norm_g"])
                load(rows[C_OK:C_OK + 1, :], t["od_k_norm_g"])
                load(causal[:, :], t["c_causal"])
                load(head_sum[:, :, :], t["c_head_sum"])
                act.wait_ge(dt_in.s, dt_in.at(1))
                act.activation(R[:, 12, :], R[:, 11, :], ACT.Sin, scale=6.283185).then_inc(dt_in.s, 1)
                act.activation(R[:, 13, :], R[:, 11, :], ACT.Sin, scale=3.1415925).then_inc(dt_in.s, 1)
                act.wait_ge(turned_in.s, turned_in.at(1))
                act.activation(col[:, 0:C_ROWS], ps[:, 0, 0:C_ROWS], ACT.Copy).then_inc(par_done.s, 1)
                act.activation(col[:, C_CONV:C_CONV + 352], ps[:, 1, 0:352], ACT.Copy).then_inc(par_done.s, 1)
                act.wait_ge(turned_in.s, turned_in.at(3))
                for i, (part, sign) in enumerate(((0, 1.0), (0, -1.0), (1, -1.0))):
                    act.activation(ssm_ct[:, i, :, :], ps[:, 4 + part, :].rearrange("p (c n) -> p c n", c=4),
                                   ACT.Copy, scale=sign).then_inc(par_done.s, 1)
                act.wait_ge(turned_in.s, turned_in.at(4))
                for part in range(2):
                    act.activation(ssm_bt[:, part, :, :], ps[:, 6 + part, :].rearrange("p (c n) -> p c n", c=4),
                                   ACT.Copy).then_inc(par_done.s, 1)

            @b.tensor
            def _(pe):
                pe.wait_ge(rel_in.s, rel_in.at(n_loads[rel_in]))
                pe.matmul(ps[0:AH, 2, :], rel[:, :], bucket[:, 0:512], start=True, stop=True)
                pe.matmul(ps[0:AH, 3, 0:BX - 512], rel[:, :], bucket[:, 512:BX], start=True, stop=True).then_inc(bias_made.s, 1)
                pe.wait_ge(par_in.s, par_in.at(n_loads[par_in]))
                pe.transpose(ps[:, 0, 0:C_ROWS], rows[:, :], ident[0:C_ROWS, 0:C_ROWS])
                for i in range(4):
                    mm = pe.transpose(ps[:, 1, 88 * i:88 * i + 88], conv_rows[:, i, :], ident[0:88, 0:88])
                mm.then_inc(turned_in.s, 1)
                pe.wait_ge(par_done.s, par_done.at(2))
                pe.wait_ge(brow_ready.s, brow_ready.at(2))
                for i in range(4):
                    mm = pe.transpose(ps[:, 1, 16 * i:16 * i + 16], par[:, i, :], ident[0:16, 0:16])
                mm.then_inc(turned_in.s, 1)
                pe.wait_ge(c_in.s, c_in.at(16 * 16))
                for part in range(2):
                    for k in range(4):
                        mm = pe.transpose(ps[:, 4 + part, k * P:(k + 1) * P], c_pre[:, part, k, :], ident[:, :])
                mm.then_inc(turned_in.s, 1)
                pe.wait_ge(bb_ready.s, bb_ready.at(1))
                for part in range(2):
                    for k in range(4):
                        mm = pe.transpose(ps[:, 6 + part, k * P:(k + 1) * P], b_pre[:, part, k, :], ident[:, :])
                mm.then_inc(turned_in.s, 1)

            @b.vector
            def _(dve):
                link = linker(dve, dve_link)
                dve.memset(eps_col[:, :], EPS)
                dve.memset(pih_col[:, :], math.pi / 2)
                link(dve.memset(b_pre[:, :, :, :], 0.0))
                dve.wait_ge(bias_made.s, bias_made.at(1))
                for a, root in enumerate((CD ** 0.5, AD ** 0.5)):
                    dve.scalar_tensor_tensor(brow[:, a, 0:512], ps[0:AH, 2, :], root, neg_rows[:, a, 0:512], ALU.mult, ALU.add)
                    ins = dve.scalar_tensor_tensor(brow[:, a, 512:BX], ps[0:AH, 3, 0:BX - 512], root, neg_rows[:, a, 512:BX],
                                                   ALU.mult, ALU.add)
                ins.then_inc(brow_ready.s, 1)
                dve.wait_ge(brow_ready.s, brow_ready.at(1))
                dve.wait_ge(a_in.s, a_in.at(48))

                tt = lambda o, a, x, op: link(dve.tensor_tensor(o, a, x, op))
                ts = lambda o, a, s1, s2, op0, op1: link(dve.tensor_scalar(o, a, s1, s2, op0, op1))
                r = lambda i: R[:, i, :]

                def exp_parts(z, power, frac, tmp):
                    ts(tmp, z, -87.0, 88.0, ALU.max, ALU.min)
                    ts(power, tmp, 1.0 / math.log(2), MAGIC, ALU.mult, ALU.add)
                    ts(power, power, -MAGIC, None, ALU.add, ALU.bypass)
                    link(dve.scalar_tensor_tensor(tmp, power, -0.693359375, tmp, ALU.mult, ALU.add))
                    link(dve.scalar_tensor_tensor(tmp, power, 2.12194440e-4, tmp, ALU.mult, ALU.add))
                    ts(frac, tmp, 1.0 / 9, 1.0, ALU.mult, ALU.add)
                    for k in range(8, 1, -1):
                        tt(frac, frac, tmp, ALU.mult)
                        ts(frac, frac, 1.0 / k, 1.0, ALU.mult, ALU.add)
                    tt(frac, frac, tmp, ALU.mult)
                    ts(RI[:, :], power, 127.0, None, ALU.add, ALU.bypass)
                    ts(RI[:, :], RI[:, :], 23, None, ALU.logical_shift_left, ALU.bypass)
                    link(dve.tensor_copy(power, RI[:, :].bitcast(F32)))

                a_re, a_im = a_rows[:, 0, :], a_rows[:, 1, :]
                link(dve.tensor_copy(r(0).rearrange("j (g p) -> j g p", g=2), dtl[:, :].unsqueeze(2).to_broadcast([16, 2, 64])))
                exp_parts(r(0), r(1), r(2), r(3))
                tt(r(4), r(1), r(2), ALU.mult)
                tt(r(4), r(4), r(1), ALU.add)
                tt(r(5), a_re, r(4), ALU.mult)
                exp_parts(r(5), r(6), r(7), r(3))
                tt(r(8), r(6), r(7), ALU.mult)
                tt(par[:, 0, :], r(8), r(6), ALU.add)
                ts(r(9), r(6), -1.0, None, ALU.add, ALU.bypass)
                tt(r(9), r(9), r(8), ALU.add)
                tt(r(10), a_im, r(4), ALU.mult)
                ts(r(10), r(10), 1.0 / (2 * math.pi), None, ALU.mult, ALU.bypass)
                ts(r(11), r(10), MAGIC, -MAGIC, ALU.add, ALU.add)
                tt(par[:, 1, :], r(10), r(11), ALU.subtract)
                dve.tensor_copy(r(11), par[:, 1, :]).then_inc(dt_in.s, 1)
                dve.wait_ge(dt_in.s, dt_in.at(3))
                tt(r(14), r(13), r(13), ALU.mult)
                ts(r(14), r(14), -2.0, None, ALU.mult, ALU.bypass)
                tt(r(15), r(9), r(14), ALU.mult)
                tt(r(15), r(15), r(9), ALU.add)
                tt(r(15), r(15), r(14), ALU.add)
                tt(r(16), par[:, 0, :], r(12), ALU.mult)
                tt(r(17), a_re, a_re, ALU.mult)
                tt(r(18), a_im, a_im, ALU.mult)
                tt(r(17), r(17), r(18), ALU.add)
                link(dve.reciprocal(r(17), r(17)))
                tt(r(19), r(15), a_re, ALU.mult)
                tt(r(20), r(16), a_im, ALU.mult)
                tt(r(19), r(19), r(20), ALU.add)
                tt(par[:, 2, :], r(19), r(17), ALU.mult)
                tt(r(21), r(16), a_re, ALU.mult)
                tt(r(22), r(15), a_im, ALU.mult)
                tt(r(21), r(21), r(22), ALU.subtract)
                dve.tensor_tensor(par[:, 3, :], r(21), r(17), ALU.mult).then_inc(brow_ready.s, 1)
                dve.wait_ge(par_in.s, par_in.at(n_loads[par_in]))
                dve.tensor_copy(ident_b[:, :], ident[:, :])
                dve.wait_ge(b_in_ready.s, b_in_ready.at(n_loads[b_in_ready]))
                link(dve.tensor_scalar(neg_sink[:, :], sink_b[:, :], -1.0, None, ALU.mult))
                dve.wait_ge(turned_in.s, turned_in.at(2))
                link(dve.tensor_copy(col[:, C_MAG:C_COLS], ps[:, 1, 0:4 * ST]))
                fre = col[:, C_FRE:C_FRE + ST].unsqueeze(2).to_broadcast([P, ST, GH])
                fim = col[:, C_FIM:C_FIM + ST].unsqueeze(2).to_broadcast([P, ST, GH])
                b_re, b_im = b_in[:, 0, :, :], b_in[:, 1, :, :]
                tt(bb[:, 0, :, :], fre, b_re, ALU.mult)
                tt(b_tmp[:, :, :], fim, b_im, ALU.mult)
                tt(bb[:, 0, :, :], bb[:, 0, :, :], b_tmp[:, :, :], ALU.subtract)
                tt(bb[:, 1, :, :], fre, b_im, ALU.mult)
                tt(b_tmp[:, :, :], fim, b_re, ALU.mult)
                tt(bb[:, 1, :, :], bb[:, 1, :, :], b_tmp[:, :, :], ALU.add)
                for part in range(2):
                    for g in range(2):
                        for j in range(4):
                            ins = dve.tensor_copy(b_pre[64 * g:64 * g + 64, part, :, 32 * j + 16 * g:32 * j + 16 * g + 16],
                                                  bb[64 * g:64 * g + 64, part, j::4, :])
                            if (part, g, j) != (1, 1, 3):
                                link(ins)
                ins.then_inc(bb_ready.s, 1)

        for s_, n in ((zeroed, 1), *n_loads.items(), (a_in, 48), (c_in, 256), (bias_made, 1), (brow_ready, 2), (rows_stored, 32), (turned_in, 4),
                      (par_done, 7), (dt_in, 3), (bb_ready, 1), (loads_in, 16)):
            s_.passed(n)

        class Norm:

            def __init__(self, src, n_tiles, gain, hi, lo, normed, stat, dram=None):
                self.dram = dram
                self.src, self.n_tiles, self.gain, self.hi, self.lo = src, n_tiles, gain, hi, lo
                self.normed, self.stat, self.n = normed, stat, n_tiles * P
                self.root_ready, self.normed_ready, self.hi_ready = sg["n_root"], sg["n_normed"], sg["n_hi"]
                self.turned, self.x_ready = sg["n_turned"], sg["n_x"]
                self.arrived = (sg["n_in0"], sg["n_in1"])

            def sync(self, sp):
                if self.dram is not None:
                    for i in range(self.n_tiles):
                        sp.dma_start(self.src[:, i, :], self.dram[i * P:(i + 1) * P, :]).then_inc(self.arrived[i].s, 16)

            def scalar(self, act):
                link, n = linker(act, act_link), self.n
                for i in range(self.n_tiles):
                    if self.dram is not None:
                        act.wait_ge(self.arrived[i].s, self.arrived[i].at(16))
                    link(act.activation(ps[:, 6:8, :].rearrange("p a b -> p (a b)"), self.src[:, i, :], ACT.Square,
                                        accum_out=self.stat[:, i:i + 1]))
                    act.activation(self.stat[:, T + i:T + i + 1], self.stat[:, i:i + 1], ACT.Sqrt, scale=1.0 / D,
                                   bias=eps_col[:, 0:1]).then_inc(self.root_ready.s, 1)
                for k in range(KD):
                    act.wait_ge(self.turned.s, self.turned.at(k + 1))
                    act.activation(self.hi[:, k, 0:n], ps[:, k, 0:n], ACT.Copy,
                                   scale=col[:, self.gain + k:self.gain + k + 1]).then_inc(self.hi_ready.s, 1)

            def vector(self, dve):
                link, n, stat = linker(dve, dve_link), self.n, self.stat
                for i in range(self.n_tiles):
                    dve.wait_ge(self.root_ready.s, self.root_ready.at(i + 1))
                    link(dve.reciprocal(stat[:, 2 * T + i:2 * T + i + 1], stat[:, T + i:T + i + 1]))
                    dve.tensor_scalar(self.normed[:, i, :], self.src[:, i, :], stat[:, 2 * T + i:2 * T + i + 1], None,
                                      ALU.mult).then_inc(self.normed_ready.s, 1)
                for k in range(KD):
                    dve.wait_ge(self.hi_ready.s, self.hi_ready.at(k + 1))
                    dve.scalar_tensor_tensor(self.lo[:, k, 0:n], ps[:, k, 0:n], col[:, self.gain + k:self.gain + k + 1],
                                             self.hi[:, k, 0:n].bitcast(F32), ALU.mult, ALU.subtract).then_inc(self.x_ready.s, 1)

            def tensor(self, pe):
                for i in range(self.n_tiles):
                    pe.wait_ge(self.normed_ready.s, self.normed_ready.at(i + 1))
                    for k in range(KD):
                        if k == 6 and i < self.n_tiles - 1:
                            pe.wait_ge(self.root_ready.s, self.root_ready.at(self.n_tiles))
                        mm = pe.transpose(ps[:, k, i * P:(i + 1) * P], self.normed[:, i, k * P:(k + 1) * P], ident[:, :])
                        if i == self.n_tiles - 1:
                            mm.then_inc(self.turned.s, 1)

            def wait_x(self, pe, k):
                pe.wait_ge(self.x_ready.s, self.x_ready.at(k + 1))

            def passed(self):
                if self.dram is not None:
                    for s_ in self.arrived:
                        s_.passed(16)
                for s_, k in ((self.root_ready, self.n_tiles), (self.normed_ready, self.n_tiles), (self.hi_ready, KD),
                              (self.turned, KD), (self.x_ready, KD)):
                    s_.passed(k)

        W.at_use = 0

        def project(jobs, norm, n, side=None):
            xs = (norm.hi, norm.lo)
            NBANK = side.banks if side else 8
            plan = []
            for first, width, kind, evacuate in jobs:
                for i, c0 in enumerate(range(0, width, 256)):
                    cols = min(256, width - c0)
                    if kind == "turned":
                        for j in range(cols // P):
                            plan.append((first + i, j, kind, None, evacuate, 2 * i + j, cols))
                    else:
                        for tt_ in range(n // P):
                            plan.append((first + i, 0, kind, tt_, evacuate, i, cols))
            last = max(p[0] for p in plan)
            ends = [m == len(plan) - 1 or plan[m + 1][0] != plan[m][0] for m in range(len(plan))]
            told = [m + 1 - sum(ends[:m + 1]) for m in range(len(plan))]
            with ExitStack() as c:
                b = c.enter_context(stage())

                @b.sync
                def _(sp):
                    norm.sync(sp)
                    if side:
                        side.sync(sp)
                    W.load(sp, last)

                @b.gpsimd
                def _(pool):
                    W.split(pool, last + 1)

                @b.vector
                def _(dve):
                    norm.vector(dve)
                    if side:
                        side.vector(dve)

                @b.tensor
                def _(pe):
                    norm.tensor(pe)
                    for m, (slot, j, kind, tile, _, _, cols) in enumerate(plan):
                        if m == 0 or plan[m - 1][0] != slot:
                            pe.wait_ge(W.split_done, slot + 1)
                        if side:
                            side.tensor(pe, m)
                        if m >= NBANK:
                            pe.wait_ge(bank_free.s, bank_free.at(m - NBANK + 1))
                        hi, lo = W.parts(slot)
                        for k in range(KD):
                            if m == 0:
                                norm.wait_x(pe, k)
                            if kind == "turned":
                                w = [v[:, k, j * P:(j + 1) * P] for v in (hi, lo)]
                                mm = product(pe, ps[:, m % NBANK, 0:n], w, [v[:, k, 0:n] for v in xs], k == 0, k == KD - 1, False)
                            else:
                                w = [v[:, k, 0:cols] for v in (hi, lo)]
                                x = [v[:, k, tile * P:(tile + 1) * P] for v in xs]
                                mm = product(pe, ps[:, m % NBANK, 0:cols], w, x, k == 0, k == KD - 1, True)
                        mm.then_inc(W.used if ends[m] else mm_done.s, 1)

                @b.scalar
                def _(act):
                    norm.scalar(act)
                    for m, (slot, j, kind, tile, evacuate, i, cols) in enumerate(plan):
                        if ends[m]:
                            act.wait_ge(W.used, slot + 1)
                        else:
                            act.wait_ge(mm_done.s, mm_done.at(told[m]))
                        if kind == "turned":
                            evacuate(act, i, ps[:, m % NBANK, 0:n]).then_inc(bank_free.s, 1)
                        else:
                            evacuate(act, tile, i, ps[:, m % NBANK, 0:cols]).then_inc(bank_free.s, 1)
                        if side:
                            side.scalar(act, m)

            norm.passed()
            if side:
                side.passed()
            mm_done.passed(told[-1])
            bank_free.passed(len(plan))
            W.at_use = last + 1

        class HeadNorm:
            banks = 6

            def __init__(self, parts, d_head, sq, inv, sel, load, n_loads, first, spread_at, per_step):
                self.first, self.spread_at, self.per_step = first, spread_at, per_step
                self.parts, self.d_head, self.sq, self.inv = parts, d_head, sq, inv
                self.sel, self.load, self.loaded = sel, load, 16 * n_loads
                self.n, self.per = len(parts), P // d_head
                self.rows = self.n * self.per
                self.squared, self.summed, self.root_ready = sg["h_squared"], sg["h_summed"], sg["h_root"]
                self.inv_ready, self.spread, self.used = sg["h_inv"], sg["h_spread"], sg["h_used"]

            def sync(self, sp):
                self.load(sp)

            def scalar(self, act, m):
                m -= self.first
                if 0 <= m < self.n:
                    if m >= 2:
                        act.wait_ge(self.summed.s, self.summed.at(m - 1))
                    act.wait_ge(bank_free.s, bank_free.at(self.first + m + 1))
                    act.activation(self.sq[:, m % 2, :], self.parts[m][0], ACT.Square).then_inc(self.squared.s, 1)
                if m == self.n + 3:
                    act.wait_ge(self.summed.s, self.summed.at(self.n))
                    act.activation(self.inv[0:self.rows, :], ps[0:self.rows, 6, :], ACT.Sqrt,
                                   bias=eps_col[0:self.rows, 0:1]).then_inc(self.root_ready.s, 1)

            def tensor(self, pe, m):
                i = m - self.first - 3
                if 0 <= i < self.n:
                    pe.wait_ge(self.squared.s, self.squared.at(i + 1))
                    c0 = 20 - self.per * i
                    pe.matmul(ps[0:self.rows, 6, :], head_sum[:, 0 if self.d_head == 64 else 1, c0:c0 + self.rows],
                              self.sq[:, i % 2, :], start=i == 0, stop=i == self.n - 1).then_inc(self.summed.s, 1)
                done = max(m - self.spread_at, -1) * self.per_step
                for i in range(max(done, 0), min(done + self.per_step, self.n)):
                    if i == 0:
                        pe.wait_ge(self.inv_ready.s, self.inv_ready.at(1))
                        pe.wait_ge(loads_in.s, loads_in.at(self.loaded))
                    if i >= 2:
                        pe.wait_ge(self.used.s, self.used.at(i - 1))
                    pe.matmul(ps[:, 6 + i % 2, :], self.sel[0:self.rows, i * P:(i + 1) * P], self.inv[0:self.rows, :],
                              start=True, stop=True).then_inc(self.spread.s, 1)

            def vector(self, dve):
                dve.wait_ge(self.root_ready.s, self.root_ready.at(1))
                dve.reciprocal(self.inv[0:self.rows, :], self.inv[0:self.rows, :]).then_inc(self.inv_ready.s, 1)
                for i, (x, gain) in enumerate(self.parts):
                    dve.wait_ge(self.spread.s, self.spread.at(i + 1))
                    dve.scalar_tensor_tensor(x, x, col[:, gain:gain + 1], ps[:, 6 + i % 2, :],
                                             ALU.mult, ALU.mult).then_inc(self.used.s, 1)

            def passed(self):
                loads_in.passed(self.loaded)
                for s_, n in ((self.squared, self.n), (self.summed, self.n), (self.root_ready, 1), (self.inv_ready, 1),
                              (self.spread, self.n), (self.used, self.n)):
                    s_.passed(n)

        class Index:
            banks = 4
            AT, PER_STEP = 7, 4

            def __init__(self, qi, ki, wi, seen, score, top, unseen, head_norm):
                self.qi, self.ki, self.wi, self.seen, self.score, self.top = qi, ki, wi, seen, score, top
                self.unseen, self.head_norm = unseen, head_norm
                self.units = [(qb, i) for qb in range(1, T) for i in range(IH)]
                self.wi_turned, self.dots_done = sg["c_ready"], sg["scores_done"]
                self.seen_ready, self.seen_used = sg["a_ready"], sg["b_ready"]

            def scores_of(self, qb):
                first = (qb - 1) * (qb + 2) // 2
                return self.score[:, first * P:(first + qb + 1) * P]

            def of_step(self, m):
                a = (m - self.AT) * self.PER_STEP
                return range(a, min(a + self.PER_STEP, len(self.units))) if a >= 0 else range(0)

            def sync(self, sp):
                self.head_norm.sync(sp)

            def scalar(self, act, m):
                self.head_norm.scalar(act, m)
                if m + 1 == self.AT:
                    act.wait_ge(self.wi_turned.s, self.wi_turned.at(1))
                    act.activation(self.wi[:, :, :], ps[:, 7, :].rearrange("p (t c) -> p t c", t=T)[:, :, P - IH:P], ACT.Copy,
                                   scale=(IH * ID) ** -0.5)
                for u in self.of_step(m + 1):
                    act.wait_ge(self.dots_done.s, self.dots_done.at(u + 1))
                    if u >= 4:
                        act.wait_ge(self.seen_used.s, self.seen_used.at(u - 3))
                    w = (self.units[u][0] + 1) * P
                    act.activation(self.seen[:, u % 4, 0:w], ps[:, 4 + u % 2, 0:w], ACT.Relu).then_inc(self.seen_ready.s, 1)

            def tensor(self, pe, m):
                self.head_norm.tensor(pe, m)
                if m == self.AT:
                    pe.wait_ge(bank_free.s, bank_free.at(6))
                    for i in range(T):
                        mm = pe.transpose(ps[:, 7, i * P:(i + 1) * P], self.ki[:, 1, i * P:(i + 1) * P], ident[:, :])
                    mm.then_inc(self.wi_turned.s, 1)
                for u in self.of_step(m):
                    qb, i = self.units[u]
                    if u >= 2:
                        pe.wait_ge(self.seen_ready.s, self.seen_ready.at(u - 1))
                    p0 = 64 * (i % 2)
                    pe.matmul(ps[:, 4 + u % 2, 0:(qb + 1) * P], self.qi[p0:p0 + 64, i // 2, qb * P:(qb + 1) * P],
                              self.ki[p0:p0 + 64, 0, 0:(qb + 1) * P], start=True, stop=True).then_inc(self.dots_done.s, 1)

            def vector(self, dve):
                link = linker(dve, dve_link)
                for u, (qb, i) in enumerate(self.units):
                    w = (qb + 1) * P
                    score = self.scores_of(qb)
                    dve.wait_ge(self.seen_ready.s, self.seen_ready.at(u + 1))
                    dve.scalar_tensor_tensor(score, self.seen[:, u % 4, 0:w], self.wi[:, qb, i:i + 1],
                                             by_x(causal, qb, w) if i == 0 else score, ALU.mult, ALU.add).then_inc(self.seen_used.s, 1)
                    dve.wait_ge(self.seen_used.s, self.seen_used.at(u + 1))
                for qb in range(1, T):
                    w = (qb + 1) * P
                    work, top = self.scores_of(qb), self.top
                    for _ in range(TOPK // 8):
                        link(dve.max(top[:, :], work))
                        link(dve.match_replace(out=work, in_to_replace=top[:, :], in_values=work, imm_value=-BIG))
                    link(dve.tensor_scalar(self.unseen[:, qb, 0:w], work, -1e35, NEG, ALU.is_gt, ALU.mult))
                self.head_norm.vector(dve)

            def passed(self):
                self.head_norm.passed()
                self.wi_turned.passed(1)
                for s_ in (self.dots_done, self.seen_ready, self.seen_used):
                    s_.passed(len(self.units))

        class ForgetGate:
            banks = 8

            def __init__(self, cum, sel, c32, sel32, fz, fa, b_f):
                self.cum, self.sel, self.c32, self.sel32 = cum, sel, c32, sel32
                self.fz, self.fa, self.b_f = fz, fa, b_f
                self.b_in, self.sel_in, self.soft_ready = sg["b_ready"], sg["a_ready"], sg["c_ready"]

            def evacuate(self, act, i, o):
                act.wait_ge(self.b_in.s, self.b_in.at(16))
                return act.activation(self.fz[:, :], o[0:FH, :], ACT.Identity, bias=self.b_f[:, 0:1])

            def sync(self, sp):
                sp.dma_start(self.b_f[:, :], t["b_forget_2"].rearrange("a h -> h a")).then_inc(self.b_in.s, 16)
                sp.dma_start(self.sel32[:, :], t["c_sel_twice"]).then_inc(self.sel_in.s, 16)

            def scalar(self, act, m):
                if m == 0:
                    link, fa = linker(act, act_link), self.fa
                    act.wait_ge(bank_free.s, bank_free.at(1))
                    link(act.activation(fa[:, :], self.fz[:, :], ACT.Abs))
                    link(act.activation(fa[:, :], fa[:, :], ACT.Exp, scale=-1.0))
                    act.activation(fa[:, :], fa[:, :], ACT.Ln, bias=1.0).then_inc(self.soft_ready.s, 1)

            def tensor(self, pe, m):
                pass

            def vector(self, dve):
                link, fz, fa, cum, c32 = linker(dve, dve_link), self.fz, self.fa, self.cum, self.c32
                dve.wait_ge(self.sel_in.s, self.sel_in.at(16))
                dve.tensor_copy(self.sel[:, :], self.sel32[:, :])
                link(dve.memset(c32[:, :], 0.0))
                link(dve.tensor_copy(cum[:, :], c32[:, :]))
                dve.wait_ge(self.soft_ready.s, self.soft_ready.at(1))
                link(dve.scalar_tensor_tensor(fz[:, :], fz[:, :], 0.0, fa[:, :], ALU.min, ALU.subtract))
                link(dve.memset(fa[:, :], 1.0))
                link(dve.tensor_tensor_scan(c32[0:FH, :], fa[:, :], fz[:, :], 0.0, ALU.mult, ALU.add))
                link(dve.tensor_scalar(c32[0:FH, :], c32[0:FH, :], -FD ** 0.5, None, ALU.mult))
                link(dve.tensor_copy(cum[0:FH, :], c32[0:FH, :]))
                dve.tensor_tensor(cum[LO:LO + FH, :], c32[0:FH, :], cum[0:FH, :].bitcast(F32), ALU.subtract)

            def passed(self):
                self.b_in.passed(16)
                self.sel_in.passed(16)
                self.soft_ready.passed(1)

        class Rope:
            banks = 6

            def __init__(self, tiles_, cos, sin, swap, tmp, mask):
                self.tiles, self.cos, self.sin, self.swap, self.tmp, self.mask = tiles_, cos, sin, swap, tmp, mask
                self.rope_in, self.swapped, self.used = sg["b_ready"], sg["h_spread"], sg["h_used"]

            def sync(self, sp):
                for dst, src in ((self.cos, "c_rope_cos"), (self.sin, "c_rope_sin"), (self.swap, "c_rope_swap"),
                                 (self.mask, "c_dilated")):
                    sp.dma_start(dst[:, :], t[src]).then_inc(self.rope_in.s, 16)

            def scalar(self, act, m):
                pass

            def tensor(self, pe, m):
                i = m - 3
                if 0 <= i < len(self.tiles):
                    if i == 0:
                        pe.wait_ge(self.rope_in.s, self.rope_in.at(64))
                    pe.wait_ge(bank_free.s, bank_free.at(i + 1))
                    if i >= 2:
                        pe.wait_ge(self.used.s, self.used.at(i - 1))
                    pe.matmul(ps[:, 6 + i % 2, :], self.swap[:, :], self.tiles[i], start=True, stop=True).then_inc(self.swapped.s, 1)

            def vector(self, dve):
                link = linker(dve, dve_link)
                dve.wait_ge(self.rope_in.s, self.rope_in.at(64))
                for i, x in enumerate(self.tiles):
                    dve.wait_ge(self.swapped.s, self.swapped.at(i + 1))
                    dve.tensor_tensor(self.tmp[:, i % 2, :], ps[:, 6 + i % 2, :], self.sin[:, :], ALU.mult).then_inc(self.used.s, 1)
                    link(dve.tensor_tensor(x, x, self.cos[:, :], ALU.mult))
                    link(dve.tensor_tensor(x, x, self.tmp[:, i % 2, :], ALU.add))

            def passed(self):
                self.rope_in.passed(64)
                self.swapped.passed(len(self.tiles))
                self.used.passed(len(self.tiles))

        def attention(heads, keys, scale, finish, sinks=None, bias_of=None, add=None, adds=lambda qb: True,
                      n_pair=2, bias_load=None):
            nh = len(heads)
            units = [(hd, qb) for hd in range(nh) for qb in range(T)]
            AHEAD, LEAD, NL = 3, 2, 4
            with ExitStack() as c:
                st = lambda name, shape, dt=F32: c.enter_context(nc.sbuf_tensor(nc.get_next_instruction_name() + name, shape, dt))
                L = st("L", [P, NL, S])
                PT = st("PT", [P, 2, T, S])
                stat = st("stat", [P, NL, 4])
                b = c.enter_context(stage())
                scores_done, logits_ready, probs_ready, probs_scaled = (sg[x] for x in ("scores_done", "logits_ready", "probs_ready", "probs_scaled"))
                turned, turned_copied, pv_done, out_free = (sg[x] for x in ("turned", "turned_copied", "pv_done", "out_free"))

                @b.sync
                def _(sp):
                    W.load(sp, W.at_use - 1)
                    if bias_load:
                        for hd in range(nh):
                            if hd >= 2:
                                sp.wait_ge(logits_ready.s, logits_ready.at(T * (hd - 1)))
                            bias_load(sp, hd)

                @b.gpsimd
                def _(pool):
                    W.split(pool, W.at_use)

                def width(qb):
                    k0, k1 = keys(qb)
                    return (k1 - k0) * P

                @b.tensor
                def _(pe):
                    def scores(u):
                        hd, qb = units[u]
                        q, k, _ = heads[hd]
                        k0, k1 = keys(qb)
                        if u >= AHEAD + 1:
                            pe.wait_ge(logits_ready.s, logits_ready.at(u - AHEAD))
                        o = ps[:, u % (AHEAD + 1), 0:width(qb)]
                        more = add is not None and adds(qb)
                        mm = pe.matmul(o, q[:, qb * P:(qb + 1) * P], k[:, k0 * P:k1 * P], start=True, stop=not more)
                        if more:
                            mm = add(pe, hd, qb, o)
                        mm.then_inc(scores_done.s, 1)

                    def turn(u):
                        hd, qb = units[u]
                        pe.wait_ge(probs_scaled.s, probs_scaled.at(u + 1))
                        if u >= 2:
                            pe.wait_ge(turned_copied.s, turned_copied.at(u - 1))
                        k0, k1 = keys(qb)
                        for i in range(k1 - k0):
                            mm = pe.transpose(ps[:, 4 + u % 2, i * P:(i + 1) * P], L[:, u % NL, i * P:(i + 1) * P], ident[:, :])
                        mm.then_inc(turned.s, 1)

                    def values(hd):
                        pe.wait_ge(turned_copied.s, turned_copied.at(T * (hd + 1)))
                        pair = hd // n_pair
                        if pair >= 2 and hd % n_pair == 0:
                            pe.wait_ge(out_free.s, out_free.at(pair - 1))
                        _, _, v = heads[hd]
                        d = v(0).shape[1]
                        p0 = d * (hd % n_pair)
                        kt = max(keys(qb)[1] for qb in range(T))
                        for kb in range(kt):
                            qs = [qb for qb in range(T) if keys(qb)[0] <= kb < keys(qb)[1]]
                            a, z = qs[0] * P, (qs[-1] + 1) * P
                            mm = pe.matmul(ps[p0:p0 + d, 6 + pair % 2, a:z], v(kb), PT[:, hd % 2, kb, a:z],
                                           start=kb == 0, stop=kb == kt - 1, skip_group_check=True)
                        mm.then_inc(pv_done.s, 1)

                    for u in range(AHEAD):
                        scores(u)
                    for u in range(len(units)):
                        if u + AHEAD < len(units):
                            scores(u + AHEAD)
                        turn(u)
                        if u % T == 0 and u > 0:
                            values(u // T - 1)
                    values(nh - 1)

                @b.vector
                def _(dve):
                    link = linker(dve, dve_link)

                    def logits(u):
                        hd, qb = units[u]
                        if u >= NL:
                            dve.wait_ge(turned.s, turned.at(u - NL + 1))
                        dve.wait_ge(scores_done.s, scores_done.at(u + 1))
                        if bias_load and qb == 0:
                            arrived = bias_in[hd % 2]
                            dve.wait_ge(arrived.s, arrived.at(16 * (hd // 2 + 1)))
                        w = width(qb)
                        init = BIG if sinks is None else sinks[:, hd:hd + 1]
                        dve.tensor_tensor_reduce(out=L[:, u % NL, 0:w], in0=ps[:, u % (AHEAD + 1), 0:w], in1=bias_of(hd, qb, w), scale=-scale,
                                                 scalar=init, op0=ALU.add, op1=ALU.min,
                                                 accum_out=stat[:, u % NL, 0:1]).then_inc(logits_ready.s, 1)

                    def scaled(u):
                        hd, qb = units[u]
                        dve.wait_ge(probs_ready.s, probs_ready.at(u + 1))
                        if sinks is not None:
                            link(dve.tensor_tensor(stat[:, u % NL, 1:2], stat[:, u % NL, 1:2], stat[:, u % NL, 3:4], ALU.add))
                        link(dve.reciprocal(stat[:, u % NL, 2:3], stat[:, u % NL, 1:2]))
                        w = width(qb)
                        dve.tensor_scalar(L[:, u % NL, 0:w], L[:, u % NL, 0:w], stat[:, u % NL, 2:3], None,
                                          ALU.mult).then_inc(probs_scaled.s, 1)

                    for u in range(LEAD):
                        logits(u)
                    for u in range(len(units)):
                        if u + LEAD < len(units):
                            logits(u + LEAD)
                        scaled(u)
                        if u % T == 2 and u > T and (u // T) % n_pair == 0:
                            finish(dve, u // T // n_pair - 1, link)
                    finish(dve, nh // n_pair - 1, link)

                @b.scalar
                def _(act):
                    def probs(u):
                        hd, qb = units[u]
                        act.wait_ge(logits_ready.s, logits_ready.at(u + 1))
                        w = width(qb)
                        if sinks is not None:
                            act.activation(stat[:, u % NL, 3:4], sinks[:, hd:hd + 1], ACT.Exp, scale=-1.0,
                                           bias=stat[:, u % NL, 0:1])
                        act.activation(L[:, u % NL, 0:w], L[:, u % NL, 0:w], ACT.Exp, scale=-1.0, bias=stat[:, u % NL, 0:1],
                                       accum_out=stat[:, u % NL, 1:2]).then_inc(probs_ready.s, 1)

                    def copy(u):
                        hd, qb = units[u]
                        if hd >= 2 and qb == 0:
                            act.wait_ge(pv_done.s, pv_done.at(hd - 1))
                        act.wait_ge(turned.s, turned.at(u + 1))
                        k0, k1 = keys(qb)
                        act.activation(PT[:, hd % 2, k0:k1, qb * P:(qb + 1) * P],
                                       ps[:, 4 + u % 2, 0:(k1 - k0) * P].rearrange("p (k q) -> p k q", q=P),
                                       ACT.Copy).then_inc(turned_copied.s, 1)

                    for u in range(LEAD):
                        probs(u)
                    for u in range(len(units)):
                        if u + LEAD < len(units):
                            probs(u + LEAD)
                        copy(u)

            n = len(units)
            for s_, k in ((scores_done, n), (logits_ready, n), (probs_ready, n), (probs_scaled, n), (turned, n),
                          (turned_copied, n), (pv_done, nh), (out_free, nh // n_pair)):
                s_.passed(k)
            if bias_load:
                for s_ in bias_in:
                    s_.passed(16 * (nh // 2))

        def out_view(pair):
            return ps[:, 6 + pair % 2, :]

        def split_out(pair0, gate=None, n_pair=2):
            def finish(dve, pair, link):
                pv_done, out_free = sg["pv_done"], sg["out_free"]
                dve.wait_ge(pv_done.s, pv_done.at(n_pair * (pair + 1)))
                hi, lo, o = x_hi[:, pair0 + pair, :], x_lo[:, pair0 + pair, :], out_view(pair)
                if gate is None:
                    link(dve.tensor_copy(hi, o))
                    dve.tensor_tensor(lo, o, hi.bitcast(F32), ALU.subtract).then_inc(out_free.s, 1)
                else:
                    g = gate[:, pair, :]
                    link(dve.tensor_tensor(g, o, g, ALU.mult))
                    link(dve.tensor_copy(hi, g))
                    dve.tensor_tensor(lo, g, hi.bitcast(F32), ALU.subtract).then_inc(out_free.s, 1)
            return finish

        def add_to_h(first, xs, k_tiles):
            groups = [(k, min(4, k_tiles - k)) for k in range(0, k_tiles, 4)]
            with ExitStack() as c:
                b = c.enter_context(stage())
                last = first + 2 * len(groups) - 1

                @b.sync
                def _(sp):
                    W.load(sp, last)

                @b.gpsimd
                def _(pool):
                    W.split(pool, last + 1)

                @b.tensor
                def _(pe):
                    for half in range(2):
                        for i, (k0, kk) in enumerate(groups):
                            slot = first + half * len(groups) + i
                            pe.wait_ge(W.split_done, slot + 1)
                            hi, lo = W.parts(slot)
                            for tile in range(T):
                                for k in range(kk):
                                    x = [v[:, k0 + k, tile * P:(tile + 1) * P] for v in xs]
                                    mm = product(pe, ps[:, 4 * half + tile, :], [v[:, k, :] for v in (hi, lo)], x,
                                                 k0 + k == 0, k0 + k == k_tiles - 1, True)
                                if tile == T - 1:
                                    mm.then_inc(W.used, 1)
                                if k0 + kk == k_tiles and tile < T - 1:
                                    mm.then_inc(mm_done.s, 1)

                @b.vector
                def _(dve):
                    for half in range(2):
                        for tile in range(T):
                            if tile < T - 1:
                                dve.wait_ge(mm_done.s, mm_done.at(3 * half + tile + 1))
                            else:
                                dve.wait_ge(W.used, first + (half + 1) * len(groups))
                            hv = h[:, tile, half * 512:half * 512 + 512]
                            dve.tensor_tensor(hv, hv, ps[:, 4 * half + tile, :], ALU.add)

            mm_done.passed(6)
            W.at_use = last + 1

        def copy_to(dst):
            return lambda act, i, o: act.activation(dst(i), o, ACT.Copy)

        def silu_to(dst):
            return lambda act, i, o: act.activation(dst(i), o, ACT.Silu)

        tokens_to = lambda dst: (lambda act, tile, i, o: act.activation(dst[:, tile, 256 * i:256 * i + o.shape[1]], o, ACT.Copy))
        xs = (x_hi, x_lo)
        as_rows = lambda tiles_: tiles_[:, 0:8, :].rearrange("p (t a) s -> p t (a s)", a=2)
        causal_keys = lambda qb: (0, qb + 1)
        by_x = lambda m, qb, w: m[:, (3 - qb) * P:(3 - qb) * P + w]

        W.at_use = 0
        with ExitStack() as c:
            st = lambda name, shape, dt=F32: c.enter_context(nc.sbuf_tensor(name, shape, dt))
            u = st("ssm_u", [P, 4, S])
            gate_b = st("gate_b", [P, 4, S])
            attention_memory = ExitStack()
            sa = lambda name, shape: attention_memory.enter_context(nc.sbuf_tensor(name, shape, F32))
            qkg = sa("ev_qkg", [P, 10, S])
            qk, gate_a = qkg[:, 0:6, :], qkg[:, 6:10, :]
            v = sa("ev_v", [P, T, 2 * AD])
            window = sa("window_bias", [P, AH, 2 * P])
            with ExitStack() as c2:
                s2 = lambda name, shape: c2.enter_context(nc.sbuf_tensor(name, shape, F32))
                sel64 = s2("ev_sel64", [12, 6 * P])

                def load(sp):
                    sp.dma_start(sel64[:, :], t["c_sel64"]).then_inc(loads_in.s, 16)
                    sp.dma_start(window[:, :, :], bass.AP(bias_rows, AH * P * BX + 127 + 256, [[BX - 1, P], [P * BX, AH], [1, 2 * P]])).then_inc(loads_in.s, 16)

                side = HeadNorm([(qk[:, i, :], C_EQ if i < 4 else C_EK) for i in range(6)], AD,
                                s2("ev_squares", [P, 2, S]), s2("ev_inverse", [12, S]), sel64, load, 2, 0, 12, 1)
                project([(w_ev_q, AW, "turned", copy_to(lambda i: qk[:, i, :])),
                         (w_ev_k, 256, "turned", copy_to(lambda i: qk[:, 4 + i, :])),
                         (w_ev_v, 128, "tokens", tokens_to(v)),
                         (w_ev_rest, 512, "turned", silu_to(lambda i: gate_a[:, i, :])),
                         (w_ev_rest + 2, 512, "turned", copy_to(lambda i: u[:, i, :])),
                         (w_ev_rest + 4, 512, "turned", silu_to(lambda i: gate_b[:, i, :]))],
                        Norm(h, T, C_NORM_G, x_hi, x_lo, as_rows(qkg), norm_stat), S, side)

            with ExitStack() as c2:
                heads = []
                for i in range(AH):
                    p0 = 64 * (i % 2)
                    kv = i // (AH // AKV)
                    heads.append((qk[p0:p0 + 64, i // 2, :], qk[p0:p0 + 64, 4 + kv, :],
                                  (lambda kv: lambda kb: v[:, kb, kv * AD:(kv + 1) * AD])(kv)))
                attention(heads, lambda qb: (max(qb - 1, 0), qb + 1), AD ** -0.5, split_out(0, gate_a), sinks=neg_sink,
                          bias_of=lambda hd, qb, w: window[:, hd, 2 * P - w:2 * P])

            attention_memory.close()

            with ExitStack() as c2:
                s2 = lambda name, shape, dt=F32: c2.enter_context(nc.sbuf_tensor(name, shape, dt))
                time = s2("time", [P, S])
                wrk = s2("phase", [P, 2, S])
                cs = s2("cos_sin", [P, 2, 2, S])
                vb = s2("v_parts", [P, 4, S])
                z = s2("z", [P, 2, 2, S])
                pr = s2("products", [P, 2, 4, S])
                b = c2.enter_context(stage())
                time_in, turns_ready, table_ready, z_ready, pr_ready = (sg[x] for x in ("b_ready", "a_ready", "c_ready", "d_ready", "e_ready"))
                bu_done, bu_free, y_ready, gelu_done = sg["scores_done"], sg["logits_ready"], sg["pv_done"], sg["out_free"]
                pr_used = sg["turned"]

                @b.sync
                def _(sp):
                    sp.dma_start(time[:, :], t["c_time"]).then_inc(time_in.s, 16)
                    W.load(sp, W.at_use - 1)

                @b.gpsimd
                def _(pool):
                    W.split(pool, W.at_use)
                    for j in range(ST):
                        pool.wait_ge(z_ready.s, z_ready.at(2 * (j + 1)))
                        if j >= 2:
                            pool.wait_ge(pr_used.s, pr_used.at(j - 1))
                        for i, (a, x) in enumerate(((0, 0), (1, 1), (1, 0), (0, 1))):
                            pool.tensor_tensor(pr[:, j % 2, i, :], cs[:, j % 2, a, :], z[:, j % 2, x, :], ALU.mult).then_inc(pr_ready.s, 1)

                @b.scalar
                def _(act):
                    link = linker(act, act_link)
                    for j in range(ST):
                        act.wait_ge(turns_ready.s, turns_ready.at(j + 1))
                        if j >= 2:
                            act.wait_ge(pr_ready.s, pr_ready.at(4 * (j - 1)))
                        act.activation(cs[:, j % 2, 1, :], wrk[:, j % 2, :], ACT.Sin, scale=6.283185)
                        link(act.activation(wrk[:, j % 2, :], wrk[:, j % 2, :], ACT.Abs))
                        act.activation(cs[:, j % 2, 0, :], wrk[:, j % 2, :], ACT.Sin, scale=-6.283185,
                                       bias=pih_col[:, 0:1]).then_inc(table_ready.s, 1)
                    for k in range(4):
                        act.wait_ge(y_ready.s, y_ready.at(k + 1))
                        act.activation(u[:, k, :], u[:, k, :], ACT.Gelu_apprx_tanh).then_inc(gelu_done.s, 1)

                @b.tensor
                def _(pe):
                    def input_products(j):
                        if j >= 2:
                            pe.wait_ge(bu_free.s, bu_free.at(j - 1))
                        p0 = 32 * (j % 4)
                        for part in range(2):
                            mm = pe.matmul(ps[:, 2 * (j % 2) + part, :], ssm_bt[p0:p0 + 32, part, j // 4, :],
                                           u[p0:p0 + 32, j // 4, :], start=True, stop=True)
                        mm.then_inc(bu_done.s, 1)

                    def output_products(j):
                        pe.wait_ge(pr_ready.s, pr_ready.at(4 * (j + 1)))
                        p0 = 32 * (j % 4)
                        for i, part in enumerate((0, 1, 2, 2)):
                            mm = pe.matmul(ps[p0:p0 + 32, 4 + j // 4, :], ssm_ct[:, part, j // 4, p0:p0 + 32],
                                           pr[:, j % 2, i, :], start=i == 0, stop=i == 3)
                        mm.then_inc(pr_used.s, 1)

                    input_products(0)
                    input_products(1)
                    for j in range(ST):
                        output_products(j)
                        if j + 2 < ST:
                            input_products(j + 2)

                @b.vector
                def _(dve):
                    link = linker(dve, dve_link)

                    def turns(j):
                        r = col[:, C_TURN + j:C_TURN + j + 1]
                        if j >= 2:
                            dve.wait_ge(table_ready.s, table_ready.at(j - 1))
                        w = wrk[:, j % 2, :]
                        link(dve.tensor_scalar(w, time[:, :], r, MAGIC, ALU.mult, ALU.add))
                        link(dve.tensor_scalar(w, w, -MAGIC, None, ALU.add, ALU.bypass))
                        dve.scalar_tensor_tensor(w, time[:, :], r, w, ALU.mult, ALU.subtract).then_inc(turns_ready.s, 1)

                    dve.wait_ge(time_in.s, time_in.at(16))
                    turns(0)
                    turns(1)
                    for j in range(ST):
                        dve.wait_ge(table_ready.s, table_ready.at(j + 1))
                        dve.wait_ge(bu_done.s, bu_done.at(j + 1))
                        re, im = ps[:, 2 * (j % 2), :], ps[:, 2 * (j % 2) + 1, :]
                        cos, sin = cs[:, j % 2, 0, :], cs[:, j % 2, 1, :]
                        dve.tensor_tensor(vb[:, 0, :], re, cos, ALU.mult)
                        dve.tensor_tensor(vb[:, 1, :], im, sin, ALU.mult)
                        dve.tensor_tensor(vb[:, 2, :], im, cos, ALU.mult)
                        dve.tensor_tensor(vb[:, 3, :], re, sin, ALU.mult).then_inc(bu_free.s, 1)
                        dve.wait_ge(bu_free.s, bu_free.at(j + 1))
                        dve.tensor_tensor(vb[:, 0, :], vb[:, 0, :], vb[:, 1, :], ALU.add)
                        link(dve.tensor_tensor(vb[:, 2, :], vb[:, 2, :], vb[:, 3, :], ALU.subtract))
                        if j >= 2:
                            dve.wait_ge(pr_ready.s, pr_ready.at(4 * (j - 1)))
                        mag = col[:, C_MAG + j:C_MAG + j + 1].to_broadcast([P, S])
                        dve.tensor_tensor_scan(z[:, j % 2, 0, :], mag, vb[:, 0, :], 0.0, ALU.mult, ALU.add).then_inc(z_ready.s, 1)
                        dve.tensor_tensor_scan(z[:, j % 2, 1, :], mag, vb[:, 2, :], 0.0, ALU.mult, ALU.add).then_inc(z_ready.s, 1)
                        dve.wait_ge(z_ready.s, z_ready.at(2 * (j + 1)))
                        if j + 2 < ST:
                            turns(j + 2)
                    dve.wait_ge(pr_used.s, pr_used.at(ST))
                    for k in range(4):
                        ins = dve.scalar_tensor_tensor(u[:, k, :], u[:, k, :], col[:, C_SKIP + k:C_SKIP + k + 1],
                                                       ps[:, 4 + k, :], ALU.mult, ALU.add)
                        ins.then_inc(y_ready.s, 1)
                    for k in range(4):
                        dve.wait_ge(gelu_done.s, gelu_done.at(k + 1))
                        link(dve.tensor_copy(x_hi[:, 4 + k, :], u[:, k, :]))
                        dve.tensor_tensor(x_lo[:, 4 + k, :], u[:, k, :], x_hi[:, 4 + k, :].bitcast(F32), ALU.subtract)
            for s_, n in ((time_in, 16), (turns_ready, ST), (table_ready, ST), (z_ready, 2 * ST), (pr_ready, 4 * ST),
                          (bu_done, ST), (bu_free, ST), (y_ready, 4), (gelu_done, 4), (pr_used, ST)):
                s_.passed(n)

            with ExitStack() as c2:
                val = c2.enter_context(nc.sbuf_tensor("glu_val", [P, 4, S], F32))
                gat = c2.enter_context(nc.sbuf_tensor("glu_gate", [P, 4, S], F32))
                b = c2.enter_context(stage())
                glu_ready = sg["a_ready"]

                @b.sync
                def _(sp):
                    W.load(sp, w_glu + 1)

                @b.gpsimd
                def _(pool):
                    W.split(pool, w_glu + 2)

                @b.tensor
                def _(pe):
                    for half in range(2):
                        pe.wait_ge(W.split_done, w_glu + half + 1)
                        hi, lo = W.parts(w_glu + half)
                        for i in range(4):
                            for k in range(4):
                                mm = product(pe, ps[:, 4 * half + i, :], [w[:, k, i * P:(i + 1) * P] for w in (hi, lo)],
                                             [x[:, 4 + k, :] for x in xs], k == 0, k == 3, False)
                            mm.then_inc(W.used if i == 3 else mm_done.s, 1)

                @b.scalar
                def _(act):
                    for half, (dst, func) in enumerate(((val, ACT.Identity), (gat, ACT.Sigmoid))):
                        for i in range(4):
                            if i < 3:
                                act.wait_ge(mm_done.s, mm_done.at(3 * half + i + 1))
                            else:
                                act.wait_ge(W.used, w_glu + half + 1)
                            bias = col[:, C_GLU + 4 * half + i:C_GLU + 4 * half + i + 1]
                            act.activation(dst[:, i, :], ps[:, 4 * half + i, :], func, bias=bias).then_inc(glu_ready.s, 1)

                @b.vector
                def _(dve):
                    link = linker(dve, dve_link)
                    dve.wait_ge(W.used, w_glu + 2)
                    for i in range(4):
                        dve.wait_ge(glu_ready.s, glu_ready.at(4 + i + 1))
                        link(dve.tensor_tensor(val[:, i, :], val[:, i, :], gat[:, i, :], ALU.mult))
                        link(dve.tensor_tensor(val[:, i, :], val[:, i, :], gate_b[:, i, :], ALU.mult))
                        link(dve.tensor_copy(x_hi[:, 4 + i, :], val[:, i, :]))
                        dve.tensor_tensor(x_lo[:, 4 + i, :], val[:, i, :], x_hi[:, 4 + i, :].bitcast(F32), ALU.subtract)
            mm_done.passed(6)
            glu_ready.passed(8)
            W.at_use = w_glu + 2
        add_to_h(w_ev_out, xs, KD)

        with ExitStack() as c:
            st = lambda name, shape, dt=F32: c.enter_context(nc.sbuf_tensor(name, shape, dt))
            qk = st("od_qk", [P, 10, S])
            v = st("od_v", [P, T, 2 * CD])
            gate = st("od_gate", [P, 8, S])
            unseen = st("unseen", [P, T, S], BF16)
            with ExitStack() as c2:
                s2 = lambda name, shape, dt=F32: c2.enter_context(nc.sbuf_tensor(name, shape, dt))
                qi = s2("qi", [P, 4, S])
                ki = s2("ki", [P, 2, S])
                wi = s2("wi", [P, T, IH])
                sel128 = s2("sel128", [10, 10 * P])
                load_sel = lambda sp: sp.dma_start(sel128[:, :], t["c_sel128"][0:10, 0:10 * P]).then_inc(loads_in.s, 16)
                head_norm = HeadNorm([(qk[:, i, :], C_OQ if i < 8 else C_OK) for i in range(10)], CD,
                                     s2("od_squares", [P, 2, S]), s2("od_inverse", [12, S]), sel128, load_sel, 1, 6, 26, 5)
                index = Index(qi, ki, wi, s2("seen", [P, 4, S]), s2("score", [P, 9 * P]), s2("top", [P, 8]), unseen, head_norm)
                project([(w_od_qi, IH * ID, "turned", copy_to(lambda i: qi[:, i, :])),
                         (w_od_ki, 256, "turned", copy_to(lambda i: ki[:, i, :])),
                         (w_od_q, CW, "turned", copy_to(lambda i: qk[:, i, :])),
                         (w_od_k, 256, "turned", copy_to(lambda i: qk[:, 8 + i, :])),
                         (w_od_v, 256, "tokens", tokens_to(v)),
                         (w_od_gate, CW, "turned", silu_to(lambda i: gate[:, i, :]))],
                        Norm(h, T, C_NORM_G + 8, x_hi, x_lo, as_rows(qk), norm_stat), S, index)

            with ExitStack() as c2:
                far = c2.enter_context(nc.sbuf_tensor("head_bias", [P, 2, S], F32))
                heads = [(qk[:, i, :], qk[:, 8 + i // 4, :], (lambda kv: lambda kb: v[:, kb, kv * CD:(kv + 1) * CD])(i // 4))
                         for i in range(CH)]

                def load_bias(sp, hd):
                    sp.dma_start(far[:, hd % 2, :], bass.AP(bias_rows, hd * P * BX + 127, [[BX - 1, P], [1, S]])).then_inc(bias_in[hd % 2].s, 16)

                def add_unseen(pe, hd, qb, o):
                    return pe.matmul(o, ident_b[:, :], unseen[:, qb, 0:(qb + 1) * P], start=False, stop=True)

                attention(heads, causal_keys, CD ** -0.5, split_out(0, gate, 1),
                          bias_of=lambda hd, qb, w: by_x(far[:, hd % 2, :], qb, w), add=add_unseen, adds=lambda qb: qb > 0,
                          n_pair=1, bias_load=load_bias)
        add_to_h(w_od_out, xs, KD)

        for layer in range(2):
            with ExitStack() as c:
                st = lambda name, shape, dt=F32: c.enter_context(nc.sbuf_tensor(f"{name}{layer}", shape, dt))
                km = st("km", [P, 2, MT])
                vm = st("vm", [P, 2, MH * FD])
                with ExitStack() as c2:
                    mem = c2.enter_context(nc.sbuf_tensor(f"mem{layer}", [P, 2, D], F32))
                    m_hi = c2.enter_context(nc.sbuf_tensor(f"m_hi{layer}", [P, KD, MT], F32R))
                    m_lo = c2.enter_context(nc.sbuf_tensor(f"m_lo{layer}", [P, KD, MT], F32R))
                    project([(w_mem_k[layer], 256, "turned", copy_to(lambda i: km[:, i, :])),
                             (w_mem_v[layer], 256, "tokens", tokens_to(vm))],
                            Norm(mem, 2, C_MEM + 8 * layer, m_hi, m_lo, mem, norm_stat, t["mem_2"][0]), MT)
                qk = st("qk", [P, 12, S])
                q, k = qk[:, 0:6, :], qk[:, 6:12, :]
                v = st("v", [P, T, FH * FD])
                qm = st("qm", [P, 2, S])
                if layer == 0:
                    cum, sel_head = st("cum", [LO + FH, S], F32R), st("sel_head", [LO + FH, FH * P], F32R)
                else:
                    mask = st("dilated_mask", [P, S])
                jobs = [(w_q[layer], FW, "turned", copy_to(lambda i: q[:, i, :])),
                        (w_k[layer], FW, "turned", copy_to(lambda i: k[:, i, :])),
                        (w_v[layer], FW, "tokens", tokens_to(v)),
                        (w_qm[layer], 256, "turned", copy_to(lambda i: qm[:, i, :]))]
                with ExitStack() as c2:
                    s2 = lambda name, shape: c2.enter_context(nc.sbuf_tensor(f"{name}{layer}", shape, F32))
                    if layer == 0:
                        side = ForgetGate(cum, sel_head, s2("cum32", [LO + FH, S]), s2("sel_head32", [LO + FH, FH * P]),
                                          s2("forget_logit", [FH, S]), s2("forget_soft", [FH, S]), s2("b_f", [FH, 1]))
                        jobs.insert(0, (w_forget, P, "turned", side.evacuate))
                    else:
                        side = Rope([qk[:, i, :] for i in range(12)], s2("rope_cos", [P, S]), s2("rope_sin", [P, S]),
                                    s2("rope_swap", [P, P]), s2("rope_tmp", [P, 2, S]), mask)
                    project(jobs, Norm(h, T, C_MIX + 8 * layer, x_hi, x_lo, as_rows(qk), norm_stat), S, side)

                def head_list(q_, k_, v_, n, d=FD):
                    return [(q_[64 * (i % 2):64 * (i % 2) + 64, i // 2, :], k_[64 * (i % 2):64 * (i % 2) + 64, i // 2, :],
                             (lambda i: lambda kb: v_[:, kb, i * d:(i + 1) * d])(i)) for i in range(n)]

                if layer == 0:
                    def add_decay(pe, hd, qb, o):
                        return pe.matmul(o, sel_head[:, hd * P:(hd + 1) * P], cum[:, 0:(qb + 1) * P], start=False, stop=True)
                    attention(head_list(q, k, v, FH), causal_keys, FD ** -0.5, split_out(0),
                              bias_of=lambda hd, qb, w: by_x(causal, qb, w), add=add_decay)
                else:
                    attention(head_list(q, k, v, FH), causal_keys, FD ** -0.5, split_out(0),
                              bias_of=lambda hd, qb, w: by_x(mask, qb, w))
                attention(head_list(qm, km, vm, MH), lambda qb: (0, 2), FD ** -0.5, split_out(6),
                          bias_of=lambda hd, qb, w: causal[:, 0:w])
            add_to_h(w_out[layer], xs, KD)

            with ExitStack() as c:
                st = lambda name, shape, dt=F32: c.enter_context(nc.sbuf_tensor(f"{name}{layer}", shape, dt))
                a_hi, a_lo = st("a_hi", [P, HALF, S], F32R), st("a_lo", [P, HALF, S], F32R)
                cv = st("cv", [P, 4, 2, S])
                norm = Norm(h, T, C_FFN + 8 * layer, x_hi, x_lo, cv[:, :, :, :].rearrange("p b v s -> p b (v s)"), norm_stat)
                base_ready, conv_done, silu_done, joined = sg["a_ready"], sg["b_ready"], sg["c_ready"], sg["d_ready"]
                banks_read, added = sg["bank_free"], sg["added"]
                units = [(part, i) for part in range(2) for i in range(HALF)]
                groups = [(k, min(4, HALF - k)) for k in range(0, HALF, 4)]
                tap = lambda j, half, u: col[:, C_CONV + 176 * layer + 44 * j + FC * half + u:][:, 0:1]
                up_slot = lambda u: w_up[layer, u // HALF] + u % HALF
                down_bank = lambda half, tile: (6 + 4 * half + tile) % 8
                up_bank = lambda i, half: (2 * i + half) % 8
                b = c.enter_context(stage())

                @b.sync
                def _(sp):
                    W.load(sp, w_down[layer, 1] + 2 * len(groups) - 1)

                @b.gpsimd
                def _(pool):
                    W.split(pool, w_down[layer, 1] + 2 * len(groups))

                @b.tensor
                def _(pe):
                    norm.tensor(pe)
                    for part in range(2):
                        for i in range(HALF):
                            u = part * HALF + i
                            pe.wait_ge(W.split_done, up_slot(u) + 1)
                            hi, lo = W.parts(up_slot(u))
                            if i >= 4:
                                pe.wait_ge(banks_read.s, banks_read.at(u - 3))
                            elif part == 1:
                                pe.wait_ge(added.s, added.at(min(8, 4 + 2 * i)))
                            for half in range(2):
                                for kt in range(KD):
                                    if u == 0 and half == 0:
                                        norm.wait_x(pe, kt)
                                    mm = product(pe, ps[:, up_bank(i, half), :], [w[:, kt, half * P:half * P + P] for w in (hi, lo)],
                                                 [x[:, kt, :] for x in xs], kt == 0, kt == KD - 1, False)
                            mm.then_inc(W.used, 1)
                        for half in range(2):
                            pe.wait_ge(banks_read.s, banks_read.at(HALF * part + (9 if half == 0 else HALF)))
                            for g, (k0, kk) in enumerate(groups):
                                slot = w_down[layer, part] + half * len(groups) + g
                                pe.wait_ge(W.split_done, slot + 1)
                                pe.wait_ge(joined.s, joined.at(HALF * part + k0 + kk))
                                hi, lo = W.parts(slot)
                                for tile in range(T):
                                    for kt in range(kk):
                                        x = [v[:, k0 + kt, tile * P:(tile + 1) * P] for v in (a_hi, a_lo)]
                                        mm = product(pe, ps[:, down_bank(half, tile), :], [v[:, kt, :] for v in (hi, lo)], x,
                                                     k0 + kt == 0, k0 + kt == HALF - 1, True)
                                    if tile == T - 1:
                                        mm.then_inc(W.used, 1)
                                    elif g == len(groups) - 1:
                                        mm.then_inc(mm_done.s, 1)

                @b.scalar
                def _(act):
                    norm.scalar(act)

                    def base(u):
                        act.wait_ge(W.used, up_slot(u) + 1)
                        if u >= 4:
                            act.wait_ge(joined.s, joined.at(u - 3))
                        for half in range(2):
                            act.activation(cv[:, u % 4, half, :], ps[:, up_bank(u % HALF, half), :], ACT.Identity,
                                           scale=tap(2, half, u), bias=tap(3, half, u)).then_inc(base_ready.s, 1)

                    def gate_silu(u):
                        act.wait_ge(conv_done.s, conv_done.at(u + 1))
                        act.activation(cv[:, u % 4, 1, :], cv[:, u % 4, 1, :], ACT.Silu).then_inc(silu_done.s, 1)

                    for part in range(2):
                        base(part * HALF)
                        for u in range(part * HALF, (part + 1) * HALF):
                            if u + 1 < (part + 1) * HALF:
                                base(u + 1)
                            gate_silu(u)

                @b.vector
                def _(dve):
                    norm.vector(dve)
                    link = linker(dve, dve_link)

                    def conv(u):
                        dve.wait_ge(base_ready.s, base_ready.at(2 * u + 2))
                        for back, j in ((1, 1), (2, 0)):
                            for half in range(2):
                                o = cv[:, u % 4, half, back:S]
                                ins = dve.scalar_tensor_tensor(o, ps[:, up_bank(u % HALF, half), 0:S - back], tap(j, half, u), o,
                                                               ALU.mult, ALU.add)
                                if (back, half) != (2, 1):
                                    link(ins)
                        ins.then_inc(banks_read.s, 1)
                        dve.wait_ge(banks_read.s, banks_read.at(u + 1))
                        dve.sem_inc(conv_done.s, 1)

                    def join(u):
                        part, i = units[u]
                        dve.wait_ge(silu_done.s, silu_done.at(u + 1))
                        if u == HALF:
                            dve.wait_ge(W.used, w_down[layer, 0] + 2 * len(groups))
                        a = cv[:, u % 4, 0, :]
                        link(dve.tensor_tensor(a, a, cv[:, u % 4, 1, :], ALU.mult))
                        link(dve.tensor_copy(a_hi[:, i, :], a))
                        dve.tensor_tensor(a_lo[:, i, :], a, a_hi[:, i, :].bitcast(F32), ALU.subtract).then_inc(joined.s, 1)

                    for part in range(2):
                        conv(part * HALF)
                        for u in range(part * HALF, (part + 1) * HALF):
                            if u + 1 < (part + 1) * HALF:
                                conv(u + 1)
                            join(u)
                        for half in range(2):
                            for tile in range(T):
                                if tile < T - 1:
                                    dve.wait_ge(mm_done.s, mm_done.at(6 * part + 3 * half + tile + 1))
                                else:
                                    dve.wait_ge(W.used, w_down[layer, part] + (half + 1) * len(groups))
                                hv = h[:, tile, half * 512:half * 512 + 512]
                                dve.tensor_tensor(hv, hv, ps[:, down_bank(half, tile), :], ALU.add).then_inc(added.s, 1)

                norm.passed()
                n = len(units)
                for s_, k_ in ((banks_read, n), (base_ready, 2 * n), (conv_done, n), (silu_done, n), (joined, n),
                               (added, 16), (mm_done, 12)):
                    s_.passed(k_)
                W.at_use = w_down[layer, 1] + 2 * len(groups)

        with ExitStack() as c:
            st = lambda name, shape, dt=F32: c.enter_context(nc.sbuf_tensor(name, shape, dt))
            gain = st("final_gain", [P, D])
            res = st("res", [P, T, D])
            stat = st("final_stat", [P, 3 * T])
            b = c.enter_context(stage())
            gain_in, root_ready, res_ready, stored = sg["b_ready"], sg["a_ready"], sg["c_ready"], sg["stored"]

            @b.sync
            def _(sp):
                sp.dma_start(gain[:, :], t["norm_final_2"].rearrange("(a d) -> a d", a=1).to_broadcast([P, D])).then_inc(gain_in.s, 16)
                for i in range(T):
                    sp.wait_ge(res_ready.s, res_ready.at(i + 1))
                    sp.dma_start(out[0, i * P:(i + 1) * P, :], res[:, i, :]).then_inc(stored.s, 16)
                sp.wait_ge(stored.s, stored.at(16 * T))

            @b.scalar
            def _(act):
                link = linker(act, act_link)
                for i in range(T):
                    link(act.activation(res[:, i, :], h[:, i, :], ACT.Square, accum_out=stat[:, i:i + 1]))
                act.activation(stat[:, T:2 * T], stat[:, 0:T], ACT.Sqrt, scale=1.0 / D, bias=eps_col[:, 0:1]).then_inc(root_ready.s, 1)

            @b.vector
            def _(dve):
                link = linker(dve, dve_link)
                dve.wait_ge(gain_in.s, gain_in.at(16))
                dve.wait_ge(root_ready.s, root_ready.at(1))
                link(dve.reciprocal(stat[:, 2 * T:3 * T], stat[:, T:2 * T]))
                for i in range(T):
                    dve.scalar_tensor_tensor(res[:, i, :], h[:, i, :], stat[:, 2 * T + i:2 * T + i + 1], gain[:, :],
                                             ALU.mult, ALU.mult).then_inc(res_ready.s, 1)


def constants():
    f = np.float32
    p, x = np.arange(P)[:, None], np.arange(S)[None, :]
    dist = p - x + 384
    causal = np.where(dist >= 0, f(0), f(NEG)).astype(f)
    n = np.maximum(511 - np.arange(BX), 0)
    nf = np.maximum(n, 1).astype(f)
    large = NB // 2 + (np.log(nf / f(NB // 2)) / f(math.log(1024 / (NB // 2))) * f(NB - NB // 2)).astype(np.int32)
    bucket_of = np.where(n < NB // 2, n, np.minimum(large, NB - 1))
    bucket = (bucket_of[None, :] == np.arange(NB)[:, None]).astype(f)
    d = 511 - np.arange(BX)
    neg = np.zeros((AH, 2, BX), f)
    neg[:, 0, :] = np.where(d < 0, f(NEG), f(0))
    neg[:, 1, :] = np.where((d < 0) | (d >= P), f(NEG), f(0))
    count = (dist >= 0) * ((dist <= 128).astype(int) + (dist % 4 == 0) + (dist % 16 == 0))
    dilated = np.where(count > 0, np.log(np.maximum(count, 1)) * math.sqrt(FD), NEG).astype(f)
    head_sum = np.zeros((P, 2, 40), f)
    head_sum[:64, 0, 20] = head_sum[64:, 0, 21] = 1 / 64
    head_sum[:, 1, 20] = 1 / 128
    sel64 = np.zeros((12, 6 * P), f)
    sel128 = np.zeros((12, 12 * P), f)
    for r in range(12):
        sel64[r, 64 * r:64 * r + 64] = 1
        sel128[r, P * r:P * r + P] = 1
    sel_twice = np.zeros((LO + FH, FH * P), f)
    sel_twice[0:FH] = sel_twice[LO:LO + FH] = sel128[0:FH, 0:FH * P]
    inv = f(1) / (f(10000.0) ** (np.arange(0, 64, 2, dtype=f) / f(64)))
    ang = np.arange(S, dtype=f)[:, None] * inv[None, :]
    cos, sin = (np.tile(g(ang).astype(f).T, (4, 1)) for g in (np.cos, np.sin))
    swap = np.zeros((P, P), f)
    for m in range(P):
        swap[m + 32 if m % 64 < 32 else m - 32, m] = -1 if m % 64 < 32 else 1
    time = np.tile(np.arange(S, dtype=f)[None, :], (P, 1))
    return {"c_causal": causal, "c_bucket": bucket, "c_neg_rows": neg, "c_dilated": dilated, "c_head_sum": head_sum,
            "c_sel64": sel64, "c_sel128": sel128, "c_sel_twice": sel_twice,
            "c_rope_cos": np.ascontiguousarray(cos), "c_rope_sin": np.ascontiguousarray(sin),
            "c_rope_swap": swap, "c_time": time, "c_ident": np.eye(P, dtype=f)}


def kernel(**inputs):
    import concourse.bacc as bacc
    from concourse.bass_utils import run_bass_kernel_spmd

    nc = bacc.Bacc("TRN2", target_bir_lowering=False, num_devices=1)
    arrays = {name: np.ascontiguousarray(a) for name, a in inputs.items()}
    arrays.update(constants())
    views = {name: nc.dram_tensor(name, a.shape, mybir.dt.from_np(a.dtype), kind="ExternalInput").ap()
             for name, a in arrays.items()}
    out = nc.dram_tensor("y", (1, S, D), F32, kind="ExternalOutput").ap()
    block_kernel(nc, views, out)
    result = run_bass_kernel_spmd(nc, [arrays], core_ids=[0])
    return result.results[0]["y"]
```
